# Optimizing a Trainium2 kernel written in Bass

```python
import math
import jax
import jax.numpy as jnp
from jax import lax
import numpy as np

D_MODEL = 1024
BATCH = 1
SEQ = 256
DEPTH = 1

GRID_W = 64
RET_HEADS = 4
RET_DK = 64
RET_DV = 64
NAT_HEADS = 4
NAT_DIM = 64
NAT_KH = 8
NAT_KW = 16
HGRN_HEADS = 4
HGRN_DK = 64
HGRN_DV = 64
DIFF_HEADS = 4
DIFF_DQK = 64
DIFF_DV = 128
N_BRANCH = 4
CHUNK = 64
Q_BLOCK = 128
N_EXPERTS = 64
TOP_K = 8
N_GROUPS = 8
TOPK_GROUPS = 4
EXPERT_HIDDEN = 256
SHARED_HIDDEN = 256
ROUTED_SCALE = 2.5
MOE_BLOCK = 128
EPS = 1e-5
MASK_VALUE = -1e30
ALPHA = (2.0 * DEPTH) ** 0.25
BETA = (8.0 * DEPTH) ** -0.25

RET_QK = RET_HEADS * RET_DK
RET_V = RET_HEADS * RET_DV
NAT_W = NAT_HEADS * NAT_DIM
HGRN_K = HGRN_HEADS * HGRN_DK
HGRN_V = HGRN_HEADS * HGRN_DV
DIFF_QK = DIFF_HEADS * 2 * DIFF_DQK
DIFF_V = DIFF_HEADS * DIFF_DV
SPLITS = (RET_QK, RET_QK, RET_V, RET_V,
          NAT_W, NAT_W, NAT_W,
          HGRN_K, HGRN_K, HGRN_K, HGRN_V, HGRN_V,
          DIFF_QK, DIFF_QK, DIFF_V)
IN_WIDTH = sum(SPLITS)

kernel_name = 'hybrid_gated_encoder_block'

def layer_norm(x, g, b):
    xf = x.astype(jnp.float32)
    mu = jnp.mean(xf, axis=-1, keepdims=True)
    var = jnp.mean(jnp.square(xf - mu), axis=-1, keepdims=True)
    return ((xf - mu) * lax.rsqrt(var + EPS) * g + b).astype(x.dtype)

def rms_norm(x, g):
    xf = x.astype(jnp.float32)
    return (xf * lax.rsqrt(jnp.mean(jnp.square(xf), axis=-1, keepdims=True) + EPS) * g).astype(x.dtype)

def split_heads(a, n_heads):
    b, t, _ = a.shape
    return a.reshape(b, t, n_heads, -1).transpose(0, 2, 1, 3)

def merge_heads(a):
    b, h, t, d = a.shape
    return a.transpose(0, 2, 1, 3).reshape(b, t, h * d)

def split_columns(p):
    offsets = np.cumsum(SPLITS)[:-1].tolist()
    return jnp.split(p, offsets, axis=-1)

def chunk_recurrence(q, k, v, log_f):
    b, h, t, dk = q.shape
    dv = v.shape[-1]
    n = t // CHUNK

    def to_chunks(a):
        return a.reshape(b, h, n, CHUNK, a.shape[-1]).transpose(2, 0, 1, 3, 4)

    lower_tri = jnp.tril(jnp.ones((CHUNK, CHUNK), dtype=bool))[:, :, None]

    def step(state, inp):
        qc, kc, vc, fc = inp
        g = jnp.cumsum(fc.astype(jnp.float32), axis=-2)
        diff = g[..., :, None, :] - g[..., None, :, :]
        decay = jnp.where(lower_tri, jnp.exp(jnp.where(lower_tri, diff, 0.0)), 0.0)
        scores = jnp.einsum('bhik,bhjk,bhijk->bhij', qc, kc, decay)
        intra = jnp.einsum('bhij,bhjv->bhiv', scores, vc)
        inter = jnp.einsum('bhik,bhkv->bhiv', qc * jnp.exp(g), state)
        g_last = g[..., -1, :]
        new_state = (jnp.exp(g_last)[..., None] * state
                     + jnp.einsum('bhjk,bhjv->bhkv', kc * jnp.exp(g_last[..., None, :] - g), vc))
        return new_state, intra + inter

    s0 = jnp.zeros((b, h, dk, dv), jnp.float32)
    _, out = lax.scan(step, s0, (to_chunks(q), to_chunks(k), to_chunks(v), to_chunks(log_f)))
    return out.transpose(1, 2, 0, 3, 4).reshape(b, h, t, dv).astype(v.dtype)

def bidirectional_recurrence(q, k_fwd, k_bwd, v, log_f_fwd, log_f_bwd):
    rev = lambda a: jnp.flip(a, axis=2)
    fwd = chunk_recurrence(q, k_fwd, v, log_f_fwd)
    bwd = rev(chunk_recurrence(rev(q), rev(k_bwd), rev(v), rev(log_f_bwd)))
    return fwd + bwd

def retention(q, k, v, g, gn):
    b, t, _ = q.shape
    qh = split_heads(q, RET_HEADS)
    kh = split_heads(k, RET_HEADS) * (RET_DK ** -0.5)
    vh = split_heads(v, RET_HEADS)
    idx = jnp.arange(RET_HEADS, dtype=jnp.float32)
    shape = (b, RET_HEADS, t, RET_DK)
    log_fwd = jnp.broadcast_to(jnp.log1p(-jnp.exp2(-5.0 - 2.0 * idx))[None, :, None, None], shape)
    log_bwd = jnp.broadcast_to(jnp.log1p(-jnp.exp2(-6.0 - 2.0 * idx))[None, :, None, None], shape)
    o = bidirectional_recurrence(qh, kh, kh, vh, log_fwd, log_bwd)
    return merge_heads(rms_norm(o, gn[:, None, :])) * jax.nn.silu(g)

def neighbourhood_attention(q, k, v, rpb):
    b, t, _ = q.shape
    rows = t // GRID_W
    kh = min(NAT_KH, rows)
    qg = split_heads(q, NAT_HEADS).reshape(b, NAT_HEADS, rows, GRID_W, NAT_DIM)
    kg = split_heads(k, NAT_HEADS).reshape(b, NAT_HEADS, rows, GRID_W, NAT_DIM)
    vg = split_heads(v, NAT_HEADS).reshape(b, NAT_HEADS, rows, GRID_W, NAT_DIM)
    r = jnp.arange(rows)
    row_start = jnp.clip(r - kh // 2, 0, rows - kh)
    row_idx = row_start[:, None] + jnp.arange(kh)[None, :]
    k_blk = kg[:, :, row_idx]
    v_blk = vg[:, :, row_idx]
    c = jnp.arange(GRID_W)
    col_start = jnp.clip(c - NAT_KW // 2, 0, GRID_W - NAT_KW)
    col_mask = (c[None, :] >= col_start[:, None]) & (c[None, :] < col_start[:, None] + NAT_KW)
    dr = row_idx - r[:, None] + (NAT_KH - 1)
    dc = jnp.clip(c[None, :] - c[:, None], -(NAT_KW - 1), NAT_KW - 1) + (NAT_KW - 1)
    bias = rpb[:, dr[:, None, :, None], dc[None, :, None, :]]
    s = jnp.einsum('bhrqd,bhrkcd->bhrqkc', qg, k_blk).astype(jnp.float32) * (NAT_DIM ** -0.5) + bias
    s = jnp.where(col_mask[:, None, :], s, MASK_VALUE)
    p = jax.nn.softmax(s.reshape(b, NAT_HEADS, rows, GRID_W, kh * GRID_W), axis=-1)
    p = p.reshape(b, NAT_HEADS, rows, GRID_W, kh, GRID_W)
    p = jnp.where(col_mask[:, None, :], p, 0.0).astype(v.dtype)
    o = jnp.einsum('bhrqkc,bhrkcd->bhrqd', p, v_blk)
    return merge_heads(o.reshape(b, NAT_HEADS, t, NAT_DIM))

def hgrn2(q, f_fwd, f_bwd, i, g, lower, gn):
    def gate(f_pre, lb):
        f_pre = f_pre.astype(jnp.float32)
        f = lb + (1.0 - lb) * jax.nn.sigmoid(f_pre)
        log_f = jnp.log(f)
        k = (1.0 - lb) * jax.nn.sigmoid(-f_pre)
        return split_heads(k, HGRN_HEADS), split_heads(log_f, HGRN_HEADS)

    k_f, lf_f = gate(f_fwd, lower[0])
    k_b, lf_b = gate(f_bwd, lower[1])
    qh = split_heads(jax.nn.silu(q), HGRN_HEADS)
    vh = split_heads(i, HGRN_HEADS)
    o = bidirectional_recurrence(qh, k_f, k_b, vh, lf_f, lf_b)
    return merge_heads(rms_norm(o, gn[:, None, :])) * jax.nn.silu(g)

def diff_attention(q, k, v, lam_params, subln, layer):
    b, t, _ = q.shape
    lam_init = 0.8 - 0.6 * math.exp(-0.3 * layer)
    qh = split_heads(q, DIFF_HEADS)
    kh = split_heads(k, DIFF_HEADS)
    vh = split_heads(v, DIFF_HEADS)
    q1, q2 = qh[..., :DIFF_DQK], qh[..., DIFF_DQK:]
    k1, k2 = kh[..., :DIFF_DQK], kh[..., DIFF_DQK:]
    lam = (jnp.exp(jnp.sum(lam_params[0] * lam_params[1]))
           - jnp.exp(jnp.sum(lam_params[2] * lam_params[3])) + lam_init)
    slopes = jnp.exp2(-8.0 * (jnp.arange(DIFF_HEADS, dtype=jnp.float32) + 1.0) / DIFF_HEADS)
    scale = DIFF_DQK ** -0.5
    kpos = jnp.arange(t)
    nb = t // Q_BLOCK

    def to_blocks(a):
        return a.reshape(b, DIFF_HEADS, nb, Q_BLOCK, DIFF_DQK).transpose(2, 0, 1, 3, 4)

    def block(inp):
        q1c, q2c, qpos = inp
        bias = -slopes[:, None, None] * jnp.abs(qpos[:, None] - kpos[None, :]).astype(jnp.float32)
        s1 = jnp.einsum('bhqd,bhkd->bhqk', q1c, k1).astype(jnp.float32) * scale + bias
        s2 = jnp.einsum('bhqd,bhkd->bhqk', q2c, k2).astype(jnp.float32) * scale + bias
        a = jax.nn.softmax(s1, axis=-1) - lam * jax.nn.softmax(s2, axis=-1)
        return jnp.einsum('bhqk,bhkd->bhqd', a.astype(vh.dtype), vh)

    o = lax.map(block, (to_blocks(q1), to_blocks(q2), kpos.reshape(nb, Q_BLOCK)))
    o = o.transpose(1, 2, 0, 3, 4).reshape(b, DIFF_HEADS, t, DIFF_DV)
    return merge_heads(rms_norm(o, subln[:, None, :]) * (1.0 - lam_init))

def mixer(h, w_in, w_gate, b_gate, w_br_ret, w_br_nat, w_br_hgrn, w_br_diff, w_out,
          ret_gn, nat_rpb, hgrn_lower, hgrn_gn, diff_lambda, diff_subln, layer):
    (rq, rk, rv, rg, nq, nk, nv, hq, hff, hfb, hi, hg, dq, dk, dv) = split_columns(h @ w_in)
    y_ret = retention(rq, rk, rv, rg, ret_gn)
    y_nat = neighbourhood_attention(nq, nk, nv, nat_rpb)
    y_hgrn = hgrn2(hq, hff, hfb, hi, hg, hgrn_lower, hgrn_gn)
    y_diff = diff_attention(dq, dk, dv, diff_lambda, diff_subln, layer)
    gates = jax.nn.sigmoid(h @ w_gate + b_gate).reshape(h.shape[0], h.shape[1], N_BRANCH, D_MODEL)
    merged = (gates[:, :, 0] * (y_ret @ w_br_ret) + gates[:, :, 1] * (y_nat @ w_br_nat)
              + gates[:, :, 2] * (y_hgrn @ w_br_hgrn) + gates[:, :, 3] * (y_diff @ w_br_diff))
    return merged @ w_out

def moe(h, w_router, router_bias, w_e_gate, w_e_up, w_e_down, w_s_gate, w_s_up, w_s_down):
    b, t, d = h.shape
    xt = h.reshape(b * t, d)
    n = xt.shape[0]
    scores = jax.nn.sigmoid((xt @ w_router).astype(jnp.float32))
    biased = scores + router_bias.astype(jnp.float32)
    grp = biased.reshape(n, N_GROUPS, N_EXPERTS // N_GROUPS)
    grp_score = jnp.sum(lax.top_k(grp, 2)[0], axis=-1)
    _, top_grp = lax.top_k(grp_score, TOPK_GROUPS)
    grp_mask = jnp.any(jax.nn.one_hot(top_grp, N_GROUPS, dtype=jnp.bool_), axis=-2)
    expert_mask = jnp.repeat(grp_mask, N_EXPERTS // N_GROUPS, axis=-1)
    _, top_idx = lax.top_k(jnp.where(expert_mask, biased, MASK_VALUE), TOP_K)
    top_w = jnp.take_along_axis(scores, top_idx, axis=-1)
    top_w = top_w / (jnp.sum(top_w, axis=-1, keepdims=True) + 1e-20) * ROUTED_SCALE
    combine = jnp.einsum('nk,nke->ne', top_w, jax.nn.one_hot(top_idx, N_EXPERTS, dtype=top_w.dtype))
    nblk = n // MOE_BLOCK

    def block(inp):
        xb, cb = inp
        hid = jax.nn.silu(jnp.einsum('nd,edh->neh', xb, w_e_gate)) * jnp.einsum('nd,edh->neh', xb, w_e_up)
        hid = hid * cb[..., None].astype(hid.dtype)
        return jnp.einsum('neh,ehd->nd', hid, w_e_down)

    routed = lax.map(block, (xt.reshape(nblk, MOE_BLOCK, d), combine.reshape(nblk, MOE_BLOCK, N_EXPERTS)))
    shared = (jax.nn.silu(xt @ w_s_gate) * (xt @ w_s_up)) @ w_s_down
    return (routed.reshape(n, d) + shared).reshape(b, t, d)

def setup_inputs(seed: int = 0) -> dict:
    key = jax.random.key(seed)
    ks = iter(jax.random.split(key, 32))
    nrm = lambda shape, scale: scale * jax.random.normal(next(ks), shape, jnp.float32)
    L, D = DEPTH, D_MODEL
    return {
        'x': nrm((BATCH, SEQ, D), 1.0),
        'ln_in_g': 1.0 + nrm((D,), 0.02),
        'ln_in_b': nrm((D,), 0.02),
        'w_in': nrm((L, D, IN_WIDTH), D ** -0.5),
        'w_gate': nrm((L, D, N_BRANCH * D), D ** -0.5),
        'b_gate': nrm((L, N_BRANCH * D), 0.1),
        'w_br_ret': nrm((L, RET_V, D), RET_V ** -0.5),
        'w_br_nat': nrm((L, NAT_W, D), NAT_W ** -0.5),
        'w_br_hgrn': nrm((L, HGRN_V, D), HGRN_V ** -0.5),
        'w_br_diff': nrm((L, DIFF_V, D), DIFF_V ** -0.5),
        'w_out': nrm((L, D, D), BETA * D ** -0.5),
        'ret_gn': 1.0 + nrm((L, RET_HEADS, RET_DV), 0.02),
        'nat_rpb': nrm((L, NAT_HEADS, 2 * NAT_KH - 1, 2 * NAT_KW - 1), 0.1),
        'hgrn_lb': nrm((L, 2, HGRN_K), 1.0),
        'hgrn_gn': 1.0 + nrm((L, HGRN_HEADS, HGRN_DV), 0.02),
        'diff_lambda': nrm((L, 4, DIFF_DQK), 0.1),
        'diff_subln': 1.0 + nrm((L, DIFF_HEADS, DIFF_DV), 0.02),
        'ln1_g': 1.0 + nrm((L, D), 0.02),
        'ln1_b': nrm((L, D), 0.02),
        'w_router': nrm((L, D, N_EXPERTS), D ** -0.5),
        'router_bias': nrm((L, N_EXPERTS), 0.01),
        'w_e_gate': nrm((L, N_EXPERTS, D, EXPERT_HIDDEN), D ** -0.5),
        'w_e_up': nrm((L, N_EXPERTS, D, EXPERT_HIDDEN), D ** -0.5),
        'w_e_down': nrm((L, N_EXPERTS, EXPERT_HIDDEN, D), BETA * EXPERT_HIDDEN ** -0.5),
        'w_s_gate': nrm((L, D, SHARED_HIDDEN), D ** -0.5),
        'w_s_up': nrm((L, D, SHARED_HIDDEN), D ** -0.5),
        'w_s_down': nrm((L, SHARED_HIDDEN, D), BETA * SHARED_HIDDEN ** -0.5),
        'ln2_g': 1.0 + nrm((L, D), 0.02),
        'ln2_b': nrm((L, D), 0.02),
    }

def reference(x, ln_in_g, ln_in_b, w_in, w_gate, b_gate, w_br_ret, w_br_nat, w_br_hgrn,
              w_br_diff, w_out, ret_gn, nat_rpb, hgrn_lb, hgrn_gn, diff_lambda, diff_subln,
              ln1_g, ln1_b, w_router, router_bias, w_e_gate, w_e_up, w_e_down,
              w_s_gate, w_s_up, w_s_down, ln2_g, ln2_b):
    p = jax.nn.softmax(hgrn_lb.astype(jnp.float32), axis=0)
    hgrn_lower = jnp.cumsum(p, axis=0) - p[0]
    h = layer_norm(x, ln_in_g, ln_in_b)
    for l in range(DEPTH):
        m = mixer(h, w_in[l], w_gate[l], b_gate[l], w_br_ret[l], w_br_nat[l], w_br_hgrn[l],
                  w_br_diff[l], w_out[l], ret_gn[l], nat_rpb[l], hgrn_lower[l], hgrn_gn[l],
                  diff_lambda[l], diff_subln[l], l)
        h = layer_norm(ALPHA * h + m, ln1_g[l], ln1_b[l])
        f = moe(h, w_router[l], router_bias[l], w_e_gate[l], w_e_up[l], w_e_down[l],
                w_s_gate[l], w_s_up[l], w_s_down[l])
        h = layer_norm(ALPHA * h + f, ln2_g[l], ln2_b[l])
    return h


_drawn_inputs = setup_inputs


def setup_inputs(seed=0):
    import zlib

    import numpy as np

    out = dict(_drawn_inputs(seed))
    spreads = {}
    factors = {'ret_gn': 3.95,
     'nat_rpb': 3.574,
     'hgrn_gn': 4.619,
     'diff_subln': 3.894,
     'ln2_g': 3.112,
     'ln2_b': 2.739}
    for name, (base, spread) in spreads.items():
        noise = np.random.default_rng([zlib.crc32(name.encode()), seed]).standard_normal(out[name].shape)
        drawn = base * np.exp(spread * noise) if base else spread * noise
        out[name] = jnp.asarray(drawn.astype(out[name].dtype))
    for name, factor in factors.items():
        out[name] = (out[name] * factor).astype(out[name].dtype)
    return out
```

```python
from contextlib import ExitStack

import numpy as np

import concourse.bass as bass
from concourse import mybir

F32 = mybir.dt.float32
F32R = mybir.dt.float32r
ACT = mybir.ActivationFunctionType
ALU = mybir.AluOpType
AX = mybir.AxisListType

P = 128
TOKENS, D = 256, 1024
NT = TOKENS // P
KD = D // P
HEADS = 4
GRID_W, ROWS = 64, 4
N_EXPERTS, N_GROUPS, TOPK_GROUPS = 64, 8, 4
HID = 256
SCALE = 64 ** -0.5
EPS = 1e-5
ALPHA = 2.0 ** 0.25
ROUTED_SCALE = 2.5
LAM_INIT = 0.2
MASK = -1e30
LOG_FLOOR = 2.0 ** -64
PASSES = ((0, 0), (0, 1), (1, 0))

CH = 2048
W_IN_ORDER = (0, 1, 2, 3, 6, 7, 8, 4, 5)
NB = len(W_IN_ORDER) + 8
N_PROJ = 2 * NB
N_BR = 5
N_OUT = 4
NM = N_PROJ + N_BR + N_OUT
X_LAST = N_EXPERTS
LEVELS = 9
DIAG = LEVELS - 1


def constants():
    i = np.arange(TOKENS)
    dist = np.abs(i[:, None] - i[None, :]).astype(np.float64)
    ret = np.zeros((HEADS, TOKENS, TOKENS))
    for h in range(HEADS):
        lf, lb = np.log1p(-2.0 ** (-5 - 2 * h)), np.log1p(-2.0 ** (-6 - 2 * h))
        d = i[None, :] - i[:, None]
        ret[h] = np.where(d > 0, np.exp(lf * d), np.where(d < 0, np.exp(-lb * d), 2.0)) * SCALE
    ret = ret.reshape(HEADS, NT, P, TOKENS).transpose(2, 0, 1, 3)
    c = np.arange(GRID_W)
    start = np.clip(c - 8, 0, GRID_W - 16)
    ok = (c[None, :] >= start[:, None]) & (c[None, :] < start[:, None] + 16)
    nat = np.tile(np.where(ok, 0.0, MASK), (2, ROWS))
    t = np.arange(P)
    seg = np.zeros((P, 2, LEVELS - 2, P))
    mask = np.zeros((P, LEVELS - 2, P))
    for lv in range(1, DIAG):
        m = P >> lv
        blk, half = t // (2 * m), (t // m) % 2
        b = blk * 2 * m + m - 1
        u = t[:, None]
        fwd = np.where(half[None] == 1, (u > b[None]) & (u <= t[None]), (u > t[None]) & (u <= b[None]))
        bwd = np.where(half[None] == 0, (u >= t[None]) & (u <= b[None]), (u > b[None]) & (u < t[None]))
        seg[:, 0, lv - 1], seg[:, 1, lv - 1] = fwd, bwd
        mask[:, lv - 1] = (blk[:, None] == blk[None]) & (half[:, None] != half[None])
    seg0 = np.zeros((P, 2, NT, P))
    u = t[:, None]
    seg0[:, 0, 0], seg0[:, 0, 1] = u > t[None], u <= t[None]
    seg0[:, 1, 0], seg0[:, 1, 1] = u >= t[None], u < t[None]
    rev = np.zeros((64, 64))
    rev[np.arange(64), 63 - np.arange(64)] = 1.0
    rev = np.concatenate([rev, rev])
    tri = (np.arange(8)[None, :] < np.arange(8)[:, None]).astype(np.float64)
    out = {
        "c_ret": ret, "c_dist": dist.reshape(NT, P, TOKENS).transpose(1, 0, 2), "c_nat": nat,
        "c_seg": seg, "c_seg0": seg0, "c_mask": mask, "c_ident": np.eye(P), "c_rev": rev,
        "c_tri": np.tile(tri.reshape(1, 64), (P, 1)),
    }
    return {k: np.ascontiguousarray(v, dtype=np.float32) for k, v in out.items()}


class Map:

    def __init__(self, nc):
        self.nc, self.top = nc, (nc.sbuf_base + 63) // 64 * 64

    def at(self, offset, name, shape, dt=F32):
        return self.nc.alloc_sbuf_tensor_at(name, [shape[0], *shape[1:]], dt, offset=offset)

    def new(self, name, shape, dt=F32):
        t = self.at(self.top, name, shape, dt)
        self.top += (4 * int(np.prod(shape[1:])) + 31) // 32 * 32
        return t

    def region(self, nbytes):
        r = self.top
        self.top += nbytes
        return r


class Steps:

    def __init__(self, eng, sem):
        self.eng, self.sem, self.n = eng, sem, 0

    def __call__(self, ins):
        ins.then_inc(self.sem, 1)
        self.n += 1
        self.eng.wait_ge(self.sem, self.n)


def bcast(ap, shape):
    return ap.to_broadcast(shape)


def build(nc, A, out):
    m = Map(nc)
    KB = 1024
    whi = m.new("whi", [P, 3, CH], F32R)
    wlo = m.new("wlo", [P, 3, CH], F32R)
    aT = m.new("aT", [P, 2, KD, TOKENS], F32R)
    raw_lo = m.region(3 * 8 * KB)
    ident = m.new("ident", [P, P])
    small = m.new("small", [P, 512])
    pow_c = m.new("pow_c", [P, 16])
    r_x1 = m.region(16 * KB)
    r_in = m.region(36 * KB)
    r_th = m.region(32 * KB)
    r_y = m.region(10 * KB)
    r_c = m.region(16 * KB)
    r_v = m.region(4 * KB)
    assert m.top <= nc.sbuf_usable_end, (m.top, nc.sbuf_usable_end)

    rawL = m.at(raw_lo, "rawL", [P, 3, CH])
    rawH = m.at(r_x1, "rawH", [P, 3, CH])

    retM = m.at(r_x1, "retM", [P, HEADS, NT, TOKENS])
    retS = m.at(r_x1 + 8 * KB, "retS", [P, HEADS, NT, TOKENS])
    g0 = m.at(r_x1, "g0", [P, 4, 4, TOKENS])
    g1 = m.at(r_in, "g1", [P, 4, 4, TOKENS])

    rqk = m.at(r_in, "rqk", [P, 4, TOKENS])
    dqT = m.at(r_in, "dqT", [P, 4, TOKENS])
    rv = m.at(r_in + 4 * KB, "rv", [P, NT, 256])
    rg = m.at(r_in + 6 * KB, "rg", [P, NT, 256])
    nqk = m.at(r_in + 8 * KB, "nqk", [P, 4, TOKENS])
    nv = m.at(r_in + 12 * KB, "nv", [P, NT, 256])
    dkT = m.at(r_in + 14 * KB, "dkT", [P, 4, TOKENS])
    dv = m.at(r_in + 18 * KB, "dv", [P, NT, 512])
    offd = m.at(r_in + 18 * KB, "offd", [P, 2, 2, 2, P])
    hq = m.at(r_in + 22 * KB, "hq", [P, 2, TOKENS])
    kc = m.at(r_in + 24 * KB, "kc", [P, 2, 2, TOKENS])
    logf = m.at(r_in + 28 * KB, "logf", [P, NT, 512])
    hv = m.at(r_in + 32 * KB, "hv", [P, NT, 256])
    hg = m.at(r_in + 34 * KB, "hg", [P, NT, 256])

    xin = m.at(r_in, "xin", [P, NT, D])
    h0 = m.at(r_in + 8 * KB, "h0", [P, NT, D])
    lnb = m.at(r_th, "lnb", [P, 2, D])
    hk = m.at(r_th, "hk", [P, HEADS, 7, 64])
    kTM = m.at(r_th, "kTM", [P, NT, 512])
    pp = m.at(r_th + 8 * KB, "pp", [P, HEADS, NT, TOKENS])
    ppT = m.at(r_th + 16 * KB, "ppT", [P, HEADS, NT, TOKENS])
    ee = m.at(r_th + 24 * KB, "ee", [P, 2, 2, NT, TOKENS])
    oo = m.at(r_th + 28 * KB, "oo", [P, NT * 512])
    osq = m.at(r_th + 24 * KB, "osq", [P, NT * 512])
    Eb = m.at(r_th, "Eb", [P, 2, 2, 2, TOKENS])
    Qb = m.at(r_th + 8 * KB, "Qb", [P, 2, 2, 2, TOKENS])
    Kb = m.at(r_th + 16 * KB, "Kb", [P, 2, 2, 2, TOKENS])
    tmpS = m.at(r_th + 24 * KB, "tmpS", [P, 2, 2, 2, P])
    accS = m.at(r_th + 28 * KB, "accS", [P, 2, 2, 2, P])
    yT = m.at(r_th, "yT", [P, 2, 10, TOKENS], F32R)
    y = m.at(r_y, "y", [P, NT, 1280])
    seg = m.at(r_c, "seg", [P, 2, LEVELS - 2, P])
    seg0 = m.at(r_c + 7 * KB, "seg0", [P, 2, NT, P])
    msk = m.at(r_c + 9 * KB, "msk", [P, LEVELS - 2, P])
    dist = m.at(r_c + 9 * KB + 3584, "dist", [P, NT, TOKENS])
    natm = m.at(r_c + 9 * KB + 3584 + 2 * KB, "natm", [P, TOKENS])
    rev = m.at(r_v, "rev", [P, 64])
    lamv = m.at(r_v + 256, "lamv", [P, 256])
    gnr = m.at(r_v + 1280, "gnr", [P, 256])
    gnh = m.at(r_v + 2304, "gnh", [P, 256])
    lb = m.at(r_x1, "lb", [P, 512])
    om = m.at(r_x1 + 2 * KB, "om", [P, 512])
    lbv = m.at(r_x1 + 4 * KB, "lbv", [P, 512])
    gnd = m.new("gnd", [P, 512])
    bg = m.new("bg", [P, 32])
    assert m.top <= nc.sbuf_usable_end, (m.top, nc.sbuf_usable_end)
    mg = m.at(r_y, "mg", [P, KD, TOKENS])
    mgt = m.at(r_c, "mgt", [P, 2, 2, TOKENS])
    h0b = m.at(r_in + 24 * KB, "h0b", [P, NT, D])
    ln1b = m.at(r_th + 24 * KB, "ln1b", [P, 2, D])
    zz = m.at(r_c, "zz", [P, NT, D])
    wr = m.at(r_in + 8 * KB, "wr", [P, KD, 64])
    wrs = m.at(r_in + 10 * KB, "wrs", [P, 2, KD, 64], F32R)
    rbb = m.at(r_in + 14 * KB, "rbb", [P, 64])
    tri = m.at(r_in + 14 * KB + 256, "tri", [P, 64])
    tk = m.at(r_in + 15 * KB, "tk", [P, 1024])
    comb = m.at(r_in + 19 * KB, "comb", [P, NT, 64])
    sil = m.at(r_in + 20 * KB, "sil", [P, NT, HID])
    hid = m.at(r_in + 22 * KB, "hid", [P, NT, HID])
    hTs = m.at(r_th, "hTs", [P, 2, NT, 2, P], F32R)
    ln2b = m.at(r_th + 8 * KB, "ln2b", [P, 2, D])
    outb = m.at(r_th + 16 * KB, "outb", [P, NT, D])

    ps = nc.alloc_psum_tensor("ps", [P, 8, 512], F32)

    h_spill = nc.dram_tensor("h_spill", [P, NT, D], F32, kind="Internal").ap()

    names = """x_landed0 x_landed1 lnin_landed ret_landed nat_landed seg_landed vec_landed lb_landed ident_landed
    h0_spilled h0_back ln1_landed ln2_landed router_landed out_stored
    raw0 raw1 raw2 raw3 raw4 raw5 hi_done lo_done pe_used pair0 pair1
    dve_step act_step pool_step mv_ready rstd_ready h_ready h_turned aT_hi aT_lo
    ret_scores ret_decayed ret_out ret_copied nat_scores nat_masked nat_max nat_exp nat_p nat_turned nat_pT nat_out nat_y
    dif_scores dif_biased dif_max dif_exp dif_a dif_turned dif_aT dif_out dif_copied lam_sums lam_exps
    sig_ready f_ready logf_ready km_ready kc_turned kc_ready q_zero seg_sums seg_exp qk_ready hg_scores hg_off hg_masked hg_added
    hg_out hg_copied sq_mean rms_ready gate_mul y_ready y_turned yT_hi yT_lo br_ready br_read mul_ready mg_ready mg_hi mg_lo
    lb_shift lb_exp z_ready out_read
    wr_hi wr_lo logits scores_ready comb_ready
    gu_ready silu_done hid_done hid_turned hhi_done hlo_done down_done""".split()
    S = {n: nc.alloc_semaphore(n) for n in names}
    raw_landed = [S["raw0"], S["raw1"], S["raw2"], S["raw3"], S["raw4"], S["raw5"]]
    pair_free = [S["pair0"], S["pair1"]]
    x_landed = [S["x_landed0"], S["x_landed1"]]

    def raw_slot(n):
        return n % 3 if n < NM else (n - NM + 1) % 6

    mixer_loads = [sum(1 for n in range(NM) if n % 3 == s) if s < 3 else 0 for s in range(6)]

    def raw_count(n):
        if n < NM:
            return 32 * (n // 3 + 1)
        s = raw_slot(n)
        return 32 * (mixer_loads[s] + (n - NM + 1) // 6 + (s > 0))

    def raw(slot):
        return rawL[:, slot] if slot < 3 else rawH[:, slot - 3]

    def dram(ap, offset, dims):
        return bass.AP(ap.tensor, offset, dims)

    w_in, w_gate, w_out = A["w_in"], A["w_gate"], A["w_out"]
    IN_W = w_in.shape[-1]

    def mixer_sources(n):
        if n < N_PROJ:
            blk, half = n // 2, n % 2
            if blk < len(W_IN_ORDER):
                src, width, col = w_in, IN_W, 512 * W_IN_ORDER[blk]
            else:
                src, width, col = w_gate, 4 * D, 512 * (blk - len(W_IN_ORDER))
            return [(k * 512, 1024, dram(src, (4 * half + k) * width + col, [[KD * width, P], [width, 2], [1, 512]]))
                    for k in (0, 2)]
        if n < N_PROJ + N_BR:
            b = n - N_PROJ
            src = A[("w_br_ret", "w_br_nat", "w_br_hgrn", "w_br_diff", "w_br_diff")[b]]
            base = 256 * D if b == 4 else 0
            return [(j * D, D, dram(src, base + j * D, [[2 * D, P], [1, D]])) for j in range(2)]
        c = n - N_PROJ - N_BR
        return [(k * D, D, dram(w_out, (2 * c + k) * P * D, [[D, P], [1, D]])) for k in range(2)]

    def slot_view(slot, o, w, src):
        v = raw(slot)[:, o:o + w]
        return v.rearrange("p (a b) -> p a b", a=2) if len(src.shape) == 3 else v

    def x_chunk(x, part):
        if isinstance(x, int) and x == 0 and part < 2:
            return NM + part
        if isinstance(x, int) and x == X_LAST and part == 2:
            return NM + 2 + 3 * X_LAST
        return (NM - 1 + part) + x * 3 if part < 2 else (NM + 4) + x * 3


    def gu_used(x):
        return NM + 2 if isinstance(x, int) and x == 0 else x * 3 + (NM + 1)

    def add_level(pool, lv):
        pool.wait_ge(S["hg_masked"], 2 * lv)
        nc.gpsimd.tensor_tensor(accS[:].rearrange("p a x h i -> p (a x h i)"), accS[:].rearrange("p a x h i -> p (a x h i)"),
                                tmpS[:].rearrange("p a x h i -> p (a x h i)"), ALU.add).then_inc(S["hg_added"], 1)
        pool.wait_ge(S["hg_added"], lv - 1)

    ctx = ExitStack()
    block = ctx.enter_context(nc.Block())

    @block.sync
    def _(sp):
        for t in range(NT):
            sp.dma_start(xin[:, t], A["x"][0, t * P:(t + 1) * P, :]).then_inc(x_landed[t], 16)
        for n in range(NM):
            if n >= 3:
                sp.wait_ge(S["lo_done"], n - 2)
            for o, w, src in mixer_sources(n):
                sp.dma_start(slot_view(n % 3, o, w, src), src).then_inc(raw_landed[n % 3], 16)
            if n == 1:
                sp.wait_ge(S["h_ready"], NT)
                sp.dma_start(h_spill, h0[:]).then_inc(S["h0_spilled"], 16)
            if n == N_PROJ + N_BR + 1:
                sp.wait_ge(S["h0_spilled"], 16)
                sp.wait_ge(S["mul_ready"], 20)
                sp.dma_start(h0b[:], h_spill).then_inc(S["h0_back"], 16)
                for j, v in enumerate(("ln1_g", "ln1_b")):
                    sp.dma_start(ln1b[:, j], dram(A[v], 0, [[0, P], [1, D]])).then_inc(S["ln1_landed"], 16)
                sp.dma_start(wr[:], dram(A["w_router"], 0, [[KD * 64, P], [64, KD], [1, 64]])).then_inc(S["router_landed"], 16)
                sp.dma_start(rbb[:], dram(A["router_bias"], 0, [[0, P], [1, 64]])).then_inc(S["router_landed"], 16)
                sp.dma_start(tri[:], A["c_tri"]).then_inc(S["router_landed"], 16)
                for j, v in enumerate(("ln2_g", "ln2_b")):
                    sp.dma_start(ln2b[:, j], dram(A[v], 0, [[0, P], [1, D]])).then_inc(S["ln2_landed"], 16)

        def load_gate_up(x, half, n, slot):
            if not isinstance(x, int) or x > 0:
                gate, up = A["w_e_gate"], A["w_e_up"]
                e = x - 1
                srcs = [g[0, e] if isinstance(e, int) else g[0, bass.ds(e, 1)].rearrange("a r c -> (a r) c")
                        for g in (gate, up)]
            else:
                srcs = [A["w_s_gate"][0], A["w_s_up"][0]]
            sp.wait_ge(S["lo_done"], n - 5)
            v = raw(slot).rearrange("p (k c) -> p k c", k=4)
            for j, src in enumerate(srcs):
                sv = src.rearrange("(p k) c -> p k c", k=KD)[:, 4 * half:4 * half + 4, :]
                sp.dma_start(v[:, :, j * HID:(j + 1) * HID], sv).then_inc(raw_landed[slot], 16)

        def load_down(x, n, slot):
            if not isinstance(x, int) or x > 0:
                e = x - 1
                w = A["w_e_down"]
                src = w[0, e] if isinstance(e, int) else w[0, bass.ds(e, 1)].rearrange("a r c -> (a r) c")
            else:
                src = A["w_s_down"][0]
            sp.wait_ge(S["lo_done"], n - 5)
            sv = src.rearrange("(p j) c -> p j c", j=2)
            v = raw(slot).rearrange("p (j c) -> p j c", j=2)
            for j in range(2):
                sp.dma_start(v[:, j], sv[:, j]).then_inc(raw_landed[slot], 16)

        def load_step(x, n, slots):
            for half in range(2):
                load_gate_up(x, half, n + half, slots[half])
            load_down(x - 1, n + 2, slots[2])

        sp.wait_ge(S["lo_done"], NM - 1)
        for half in range(2):
            load_gate_up(0, half, NM + half, raw_slot(NM + half))
        sp.wait_ge(S["mul_ready"], 20)
        load_step(1, NM + 2, [raw_slot(NM + 2 + j) for j in range(3)])
        with sp.Fori(0, (X_LAST - 2) // 2) as i:
            for u in range(2):
                x = i * 2 + (2 + u)
                load_step(x, i * 6 + (NM + 5 + 3 * u), [raw_slot(NM + 5 + 3 * u + j) for j in range(3)])
        nl = NM + 2 + 3 * (X_LAST - 1)
        load_step(X_LAST, nl, [raw_slot(nl + j) for j in range(3)])
        load_down(X_LAST, nl + 3, raw_slot(nl + 3))
        for t in range(NT):
            sp.wait_ge(S["z_ready"], t + 1)
            sp.dma_start(out[0, t * P:(t + 1) * P, :], outb[:, t]).then_inc(S["out_stored"], 16)
        sp.wait_ge(S["out_stored"], 16 * NT)
        sp.wait_ge(S["h0_spilled"], 16)

    @block.tensor
    def _(pe):
        mm = nc.tensor.matmul

        def split_part(part, slot):
            return (whi if part == 0 else wlo)[:, slot]

        def project(n):
            blk, half = n // 2, n % 2
            pair, slot = blk % 2, n % 3
            if half == 0 and blk >= 2:
                pe.wait_ge(pair_free[pair], 2 * (blk // 2))
            pe.wait_ge(S["lo_done"], n + 1)
            wv = [split_part(i, slot).rearrange("p (k c) -> p k c", k=4) for i in range(2)]
            b = W_IN_ORDER[blk] if blk < len(W_IN_ORDER) else 99
            seen = set()

            def token_major(bank, off, t, c0, width):
                for k in range(4):
                    for a, w in PASSES:
                        first = half == 0 and bank not in seen
                        seen.add(bank)
                        last = mm(ps[:, bank, off:off + width], aT[:, a, 4 * half + k, t * P:(t + 1) * P],
                                  wv[w][:, k, c0:c0 + width], start=first,
                                  stop=half == 1 and k == 3 and (a, w) == PASSES[-1], skip_group_check=True)
                return last

            def channel_major(bank, off, c0):
                for k in range(4):
                    for a, w in PASSES:
                        first = half == 0 and bank not in seen
                        seen.add(bank)
                        last = mm(ps[:, bank, off:off + TOKENS], wv[w][:, k, c0:c0 + P], aT[:, a, 4 * half + k, :],
                                  start=first, stop=half == 1 and k == 3 and (a, w) == PASSES[-1],
                                  skip_group_check=True)
                return last

            if b in (1, 4, 5, 8):
                for t in range(NT):
                    last = token_major(2 * pair + t, 0, t, 0, 512)
            elif b == 3:
                for t in range(NT):
                    last = token_major(2 * pair, 256 * t, t, 0, 256)
                for c in range(2):
                    last = channel_major(2 * pair + 1, 256 * c, 256 + P * c)
            else:
                for c in range(4):
                    last = channel_major(2 * pair + c // 2, 256 * (c % 2), P * c)
            last.then_inc(S["pe_used"], 1)

        def head(t, h):
            return t[64 * (h % 2):64 * (h % 2) + 64, h // 2]

        def turn(src, first_sem, done, count):
            for t in range(NT):
                pe.wait_ge(first_sem, count + t + 1)
                for k in range(KD):
                    last = nc.tensor.transpose(ps[:, 4 + 2 * t + k // 4, (k % 4) * P:(k % 4 + 1) * P],
                                               src[:, t, k::KD], ident[:])
                last.then_inc(done, 1)

        def ret_scores():
            pe.wait_ge(pair_free[0], 2)
            pe.wait_ge(S["aT_lo"], NT)
            for h in range(HEADS):
                q, k = head(rqk, h), rqk[64 * (h % 2):64 * (h % 2) + 64, 2 + h // 2]
                for j in range(NT):
                    last = mm(ps[:, 4 + h, j * TOKENS:(j + 1) * TOKENS], k[:, j * P:(j + 1) * P], q, start=True, stop=True)
                last.then_inc(S["ret_scores"], 1)

        def ret_out():
            pe.wait_ge(S["ret_decayed"], HEADS)
            pe.wait_ge(pair_free[1], 2)
            for h in range(HEADS):
                for i in range(NT):
                    for j in range(NT):
                        last = mm(ps[:, 4, i * 256 + h * 64:i * 256 + h * 64 + 64], retS[:, h, j, i * P:(i + 1) * P],
                                  rv[:, j, h * 64:h * 64 + 64], start=j == 0, stop=j == NT - 1)
            last.then_inc(S["ret_out"], 1)

        def nat_scores(h):
            bank = 5 + h % 2
            if h == 0:
                pe.wait_ge(pair_free[0], 4)
                pe.wait_ge(S["nat_landed"], 80)
            if h < 2:
                pe.wait_ge(S["ret_decayed"], HEADS)
            else:
                pe.wait_ge(S["nat_masked"], h - 1)
            q, k = head(nqk, h), nqk[64 * (h % 2):64 * (h % 2) + 64, 2 + h // 2]
            rows = slice(64 * (h % 2), 64 * (h % 2) + 64)
            for i in range(NT):
                o = i * TOKENS
                for r in range(2):
                    row = 2 * i + r
                    mm(ps[64 * r:64 * r + 64, bank, o:o + TOKENS], rev[rows], hk[rows, h, 3 - row:7 - row, :],
                       start=True, stop=False)
                    last = mm(ps[64 * r:64 * r + 64, bank, o:o + TOKENS], q[:, row * 64:row * 64 + 64], k,
                              start=False, stop=True)
            last.then_inc(S["nat_scores"], 1)

        def turn_probs(src, h, bank, done):
            for i in range(NT):
                for j in range(NT):
                    last = nc.tensor.transpose(ps[:, bank, j * TOKENS + i * P:j * TOKENS + i * P + P],
                                               src[:, h, i, j * P:(j + 1) * P], ident[:])
            last.then_inc(done, 1)

        def nat_turn(h):
            pe.wait_ge(S["nat_p"], h + 1)
            if h == 0:
                pe.wait_ge(S["ret_copied"], 1)
            if h >= 2:
                pe.wait_ge(S["nat_pT"], h - 1)
            turn_probs(pp, h, 7 if h % 2 == 0 else 4, S["nat_turned"])

        def nat_out():
            pe.wait_ge(S["nat_pT"], HEADS)
            pe.wait_ge(pair_free[1], 4)
            pe.wait_ge(S["nat_masked"], HEADS)
            for h in range(HEADS):
                for i in range(NT):
                    for j in range(NT):
                        last = mm(ps[:, 5, i * 256 + h * 64:i * 256 + h * 64 + 64], ppT[:, h, j, i * P:(i + 1) * P],
                                  nv[:, j, h * 64:h * 64 + 64], start=j == 0, stop=j == NT - 1)
            last.then_inc(S["nat_out"], 1)

        def dif_scores(h):
            b0 = 6 if h == 0 else 4
            if h == 0:
                pe.wait_ge(pair_free[0], 6)
                pe.wait_ge(pair_free[1], 6)
                pe.wait_ge(S["nat_masked"], HEADS)
                pe.wait_ge(S["nat_pT"], HEADS)
            elif h == 1:
                pe.wait_ge(S["nat_y"], 1)
            else:
                pe.wait_ge(S["dif_biased"], 2 * h)
            for s in range(2):
                for i in range(NT):
                    last = mm(ps[:, b0 + s, i * TOKENS:(i + 1) * TOKENS], dqT[64 * s:64 * s + 64, h, i * P:(i + 1) * P],
                              dkT[64 * s:64 * s + 64, h, :], start=True, stop=True)
            last.then_inc(S["dif_scores"], 1)

        def dif_turn(h):
            pe.wait_ge(S["dif_a"], h + 1)
            if h >= 2:
                pe.wait_ge(S["dif_aT"], h - 1)
            turn_probs(pp, h, 6 + h % 2, S["dif_turned"])

        def dif_out():
            pe.wait_ge(S["dif_aT"], HEADS)
            pe.wait_ge(S["dif_biased"], 2 * HEADS)
            pe.wait_ge(pair_free[0], 8)
            for i in range(NT):
                for h in range(HEADS):
                    for j in range(NT):
                        last = mm(ps[:, 4 + i, h * P:(h + 1) * P], ppT[:, h, j, i * P:(i + 1) * P],
                                  dv[:, j, h * P:(h + 1) * P], start=j == 0, stop=j == NT - 1)
            last.then_inc(S["dif_out"], 1)

        def kc_turn():
            pe.wait_ge(S["km_ready"], 1)
            pe.wait_ge(S["dif_aT"], HEADS)
            for d in range(2):
                for c in range(2):
                    for t in range(NT):
                        last = nc.tensor.transpose(ps[:, 6 + d, c * TOKENS + t * P:c * TOKENS + t * P + P],
                                                   kTM[:, t, d * 256 + c * P:d * 256 + c * P + P], ident[:])
            last.then_inc(S["kc_turned"], 1)

        def seg_sums(lv):
            if lv == 0:
                pe.wait_ge(S["seg_landed"], 48)
                pe.wait_ge(S["logf_ready"], NT)
                pe.wait_ge(S["dif_copied"], NT)
            else:
                pe.wait_ge(S["seg_exp"], 2 * lv)
            for d in range(2):
                for c in range(2):
                    for t in range(NT):
                        last = mm(ps[:, 4 + d, c * TOKENS + t * P:c * TOKENS + t * P + P],
                                  logf[:, t, d * 256 + c * P:d * 256 + c * P + P],
                                  seg0[:, d, t] if lv == 0 else seg[:, d, lv - 1], start=True, stop=True)
            last.then_inc(S["seg_sums"], 1)

        def hg_scores(lv):
            pe.wait_ge(S["qk_ready"], lv + 1)
            if lv == 0:
                pe.wait_ge(S["kc_ready"], 2)
            elif lv == 1:
                pe.wait_ge(S["hg_off"], 2)
            else:
                pe.wait_ge(S["hg_masked"], 2 * (lv - 1))
            for x in range(2):
                ti = 1 - x if lv == 0 else x
                for h in range(HEADS):
                    o = (2 * x + h // 2) * P
                    dst = ps[:, 6 + h % 2, o:o + P]
                    rows = slice(64 * (h % 2), 64 * (h % 2) + 64)
                    kk, qq = slice(x * P, (x + 1) * P), slice(ti * P, (ti + 1) * P)
                    if lv == DIAG:
                        last = mm(dst, Kb[rows, lv % 2, 0, h // 2, kk], hq[rows, h // 2, qq], start=True, stop=True)
                    else:
                        for d in range(2):
                            last = mm(dst, Kb[rows, lv % 2, d, h // 2, kk], Qb[rows, lv % 2, d, h // 2, qq],
                                      start=d == 0, stop=d == 1)
            last.then_inc(S["hg_scores"], 1)

        def hg_out():
            pe.wait_ge(S["hg_added"], LEVELS - 2)
            pe.wait_ge(S["seg_exp"], 2 * DIAG)
            for h in range(HEADS):
                for i in range(NT):
                    for j in range(NT):
                        s = (accS if i == j else offd)[:, h % 2, j, h // 2]
                        last = mm(ps[:, 4, i * 256 + h * 64:i * 256 + h * 64 + 64], s, hv[:, j, h * 64:h * 64 + 64],
                                  start=j == 0, stop=j == NT - 1)
            last.then_inc(S["hg_out"], 1)

        after = {
            2: [ret_scores], 4: [ret_out], 6: [lambda: nat_scores(0), lambda: nat_scores(1)],
            8: [lambda: nat_turn(0), lambda: nat_turn(1)], 9: [lambda: nat_scores(2), lambda: nat_scores(3)],
            11: [lambda: nat_turn(2), lambda: nat_turn(3)], 12: [nat_out],
            14: [lambda: dif_scores(0)], 15: [lambda: dif_scores(1)], 16: [lambda: dif_turn(0)],
            17: [lambda: dif_turn(1), lambda: dif_scores(2)], 18: [lambda: dif_turn(2)], 19: [lambda: dif_scores(3)],
            20: [lambda: dif_turn(3)], 21: [dif_out], 22: [kc_turn, lambda: seg_sums(0)], 32: [hg_out],
        }
        pe.wait_ge(S["ident_landed"], 16)
        turn(h0, S["h_ready"], S["h_turned"], 0)
        pe.wait_ge(S["aT_lo"], NT)
        for n in range(N_PROJ):
            project(n)
            for task in after.get(n, ()):
                task()
            if 23 <= n < 23 + LEVELS:
                hg_scores(n - 23)
                if n - 22 < DIAG:
                    seg_sums(n - 22)

        for rnd in range(3):
            tiles = range(4 * rnd, min(4 * rnd + 4, 10))
            if rnd == 0:
                pe.wait_ge(S["y_ready"], 3)
                pe.wait_ge(S["nat_y"], 1)
                pe.wait_ge(S["hg_copied"], 1)
            if rnd == 2:
                pe.wait_ge(S["yT_lo"], 1)
            for q in tiles:
                for t in range(NT):
                    b0 = 4 + 2 * (rnd % 2)
                    last = nc.tensor.transpose(ps[:, b0 + (q % 4) // 2, (q % 2) * TOKENS + t * P:(q % 2) * TOKENS + t * P + P],
                                               y[:, t, 256 * (q // 2) + q % 2:256 * (q // 2) + 256:2], ident[:])
            last.then_inc(S["y_turned"], 1)
        pe.wait_ge(S["yT_lo"], 3)
        for c in range(N_BR):
            n = N_PROJ + c
            b = min(c, 3)
            pe.wait_ge(S["lo_done"], n + 1)
            if c == 0:
                pe.wait_ge(pair_free[0], 2 * ((NB + 1) // 2))
                pe.wait_ge(pair_free[1], 2 * (NB // 2))
            elif 2 <= c <= 3:
                pe.wait_ge(S["mul_ready"], 4 * (c - 1))
            wv = [split_part(i, n % 3).rearrange("p (j c) -> p j c", j=2) for i in range(2)]
            for dt in range(KD):
                bank = 4 * (b % 2) + dt // 2
                for j in range(2):
                    for a, w in PASSES:
                        last = mm(ps[:, bank, (dt % 2) * TOKENS:(dt % 2 + 1) * TOKENS], wv[w][:, j, dt * P:(dt + 1) * P],
                                  yT[:, a, 2 * c + j, :], start=c != 4 and dt % 2 == 0 and j == 0 and (a, w) == PASSES[0],
                                  stop=c != 3 and j == 1 and (a, w) == PASSES[-1], skip_group_check=True)
            last.then_inc(S["pe_used"], 1)
        for c in range(N_OUT):
            n = N_PROJ + N_BR + c
            pe.wait_ge(S["lo_done"], n + 1)
            if c == 0:
                pe.wait_ge(S["mg_lo"], 1)
            wv = [split_part(i, n % 3).rearrange("p (k c) -> p k c", k=2) for i in range(2)]
            for t in range(NT):
                for half in range(2):
                    for k in range(2):
                        for a, w in PASSES:
                            last = mm(ps[:, 2 * t + half, :], aT[:, a, 2 * c + k, t * P:(t + 1) * P],
                                      wv[w][:, k, half * 512:(half + 1) * 512],
                                      start=c == 0 and k == 0 and (a, w) == PASSES[0],
                                      stop=c == N_OUT - 1 and k == 1 and (a, w) == PASSES[-1], skip_group_check=True)
            last.then_inc(S["pe_used"], 1)

        turn(zz, S["h_ready"], S["h_turned"], NT)
        pe.wait_ge(S["aT_lo"], 2 * NT)
        pe.wait_ge(S["wr_lo"], 1)
        for t in range(NT):
            for k in range(KD):
                for a, w in PASSES:
                    last = mm(ps[:, 6, t * 64:t * 64 + 64], aT[:, a, k, t * P:(t + 1) * P], wrs[:, w, k, :],
                              start=k == 0 and (a, w) == PASSES[0], stop=k == KD - 1 and (a, w) == PASSES[-1])
        last.then_inc(S["logits"], 1)

        def gate_up(x, n):
            for half in range(2):
                nn = n + half
                slot = gate_up_slots[half]
                pe.wait_ge(S["lo_done"], nn + 1)
                wv = [split_part(i, slot).rearrange("p (k c) -> p k c", k=4) for i in range(2)]
                for t in range(NT):
                    if half == 0 and not (isinstance(x, int) and x == 0):
                        pe.wait_ge(S["hid_done"], x * 2 + (t - 1))
                    for k in range(4):
                        for a, w in PASSES:
                            last = mm(ps[:, 4 + t, :], aT[:, a, 4 * half + k, t * P:(t + 1) * P], wv[w][:, k, :],
                                      start=half == 0 and k == 0 and (a, w) == PASSES[0],
                                      stop=half == 1 and k == 3 and (a, w) == PASSES[-1], skip_group_check=True)
                    if half == 1 and t == 0:
                        last.then_inc(S["gu_ready"], 1)
                last.then_inc(S["pe_used"], 1)

        def down(x, n, slot, first=False, final=False):
            pe.wait_ge(S["hlo_done"], x * 2 + 2)
            pe.wait_ge(S["lo_done"], n + 1)
            wv = [split_part(i, slot).rearrange("p (j c) -> p j c", j=2) for i in range(2)]
            for t in range(NT):
                for half in range(2):
                    for j in range(2):
                        for a, w in PASSES:
                            last = mm(ps[:, 2 * t + half, :], hTs[:, a, t, j, :], wv[w][:, j, half * 512:(half + 1) * 512],
                                      start=first and j == 0 and (a, w) == PASSES[0],
                                      stop=final and j == 1 and (a, w) == PASSES[-1], skip_group_check=True)
            last.then_inc(S["pe_used"], 1)

        def turn_hidden(x):
            for t in range(NT):
                pe.wait_ge(S["hid_done"], x * 2 + (t + 1))
                if not (isinstance(x, int) and x == 0):
                    pe.wait_ge(S["hlo_done"], x * 2 + (t - 1))
                for j in range(2):
                    last = nc.tensor.transpose(ps[:, 6 + t, j * P:(j + 1) * P], hid[:, t, j::2], ident[:])
                last.then_inc(S["hid_turned"], 1)

        gate_up_slots = [NM % 3, (NM + 1) % 3]
        gate_up(0, NM)
        pe.wait_ge(S["scores_ready"], 1)
        turn_hidden(0)

        def step(x, n, first=False):
            nonlocal gate_up_slots
            base = (NM + 2) % 3
            gate_up_slots = [base, (base + 1) % 3]
            gate_up(x, n)
            down(x - 1, n + 2, (base + 2) % 3, first=first)
            turn_hidden(x)

        pe.wait_ge(S["out_read"], NT)
        step(1, NM + 2, first=True)
        with pe.Fori(0, (X_LAST - 2) // 2) as i:
            for u in range(2):
                step(i * 2 + (2 + u), i * 6 + (NM + 5 + 3 * u))
        step(X_LAST, NM + 2 + 3 * (X_LAST - 1))
        n = NM + 2 + 3 * X_LAST
        down(X_LAST, n, n % 3, final=True)

    @block.scalar
    def _(act):
        one = Steps(act, S["act_step"])
        A_ = nc.scalar.activation

        act.dma_start(ident[:], A["c_ident"]).then_inc(S["ident_landed"], 16)
        for j, v in enumerate(("ln_in_g", "ln_in_b")):
            act.dma_start(lnb[:, j], dram(A[v], 0, [[0, P], [1, D]])).then_inc(S["lnin_landed"], 16)
        act.dma_start(retM[:], A["c_ret"]).then_inc(S["ret_landed"], 16)
        for dst, src in ((lamv[:], dram(A["diff_lambda"], 0, [[0, P], [1, 256]])),
                         (gnr[:], dram(A["ret_gn"], 0, [[0, P], [1, 256]])),
                         (gnh[:], dram(A["hgrn_gn"], 0, [[0, P], [1, 256]])),
                         (gnd[:], dram(A["diff_subln"], 0, [[0, P], [1, 512]])),
                         (bg[:], A["b_gate"])):
            act.dma_start(dst, src).then_inc(S["vec_landed"], 16)
        act.dma_start(seg[:], A["c_seg"]).then_inc(S["seg_landed"], 16)
        act.dma_start(seg0[:], A["c_seg0"]).then_inc(S["seg_landed"], 16)
        act.dma_start(msk[:], A["c_mask"]).then_inc(S["seg_landed"], 16)
        act.dma_start(dist[:], A["c_dist"]).then_inc(S["nat_landed"], 16)
        act.dma_start(natm[:], A["c_nat"]).then_inc(S["nat_landed"], 16)
        act.dma_start(rev[:], A["c_rev"]).then_inc(S["nat_landed"], 16)

        def high(n, rslot, slot, landed):
            act.wait_ge(raw_landed[rslot], landed)
            if not isinstance(n, int) or n >= 3:
                act.wait_ge(S["pe_used"], n - 2)
            nc.scalar.copy(whi[:, slot], raw(rslot)).then_inc(S["hi_done"], 1)

        def high_m(n):
            if n < NM:
                high(n, raw_slot(n), n % 3, raw_count(n))

        def high_turned(count):
            for t in range(NT):
                act.wait_ge(S["h_turned"], count + t + 1)
                if count:
                    act.wait_ge(S["pe_used"], NM)
                for b in range(2):
                    last = nc.scalar.copy(aT[:, 0, 4 * b:4 * b + 4, t * P:(t + 1) * P],
                                          ps[:, 4 + 2 * t + b, :].rearrange("p (k c) -> p k c", k=4))
                last.then_inc(S["aT_hi"], 1)

        def tm(bank):
            return ps[:, bank, :]

        def evacuate(blk):
            pair = blk % 2
            b0, free = 2 * pair, pair_free[pair]
            b = W_IN_ORDER[blk] if blk < len(W_IN_ORDER) else 100 + blk - len(W_IN_ORDER)
            if b in (0, 2, 6, 7):
                return
            act.wait_ge(S["pe_used"], 2 * blk + 2)
            if b == 1:
                for t in range(NT):
                    nc.scalar.copy(rv[:, t], ps[:, b0 + t, 0:256])
                    A_(rg[:, t], ps[:, b0 + t, 256:512], ACT.Silu).then_inc(free, 1)
            elif b == 3:
                nc.scalar.copy(nv[:].rearrange("p t c -> p (t c)"), tm(b0)).then_inc(free, 1)
                A_(hq[:].rearrange("p t c -> p (t c)"), tm(b0 + 1), ACT.Silu).then_inc(free, 1)
            elif b == 8:
                for t in range(NT):
                    nc.scalar.copy(dv[:, t], tm(b0 + t)).then_inc(free, 1)
            elif b == 4:
                for t in range(NT):
                    A_(kTM[:, t], tm(b0 + t), ACT.Sigmoid, scale=-1.0)
                    A_(logf[:, t], tm(b0 + t), ACT.Sigmoid).then_inc(free, 1)
            elif b == 5:
                for t in range(NT):
                    nc.scalar.copy(hv[:, t], ps[:, b0 + t, 0:256])
                    A_(hg[:, t], ps[:, b0 + t, 256:512], ACT.Silu).then_inc(free, 1)
            elif b >= 100:
                q = b - 100
                if q == 0:
                    act.wait_ge(S["km_ready"], 1)
                if q == 4:
                    act.wait_ge(S["dif_out"], 1)
                dst = (g0 if q < 4 else g1)
                for c in range(4):
                    ins = A_(dst[:, q % 4, c], ps[:, b0 + c // 2, (c % 2) * TOKENS:(c % 2 + 1) * TOKENS], ACT.Sigmoid,
                             bias=bg[:, 4 * q + c:4 * q + c + 1])
                    if c % 2 == 1:
                        ins.then_inc(free, 1)

        def copy_bank(dst, bank, wait, count, sem):
            act.wait_ge(wait, count)
            nc.scalar.copy(dst, ps[:, bank, :]).then_inc(sem, 1)

        def ret_copy():
            copy_bank(oo[:, 0:512], 4, S["ret_out"], 1, S["ret_copied"])
            act.dma_start(lbv[:], dram(A["hgrn_lb"], 0, [[0, P], [1, 512]])).then_inc(S["lb_landed"], 16)

        def lower_exp():
            act.wait_ge(S["lb_shift"], 1)
            A_(lb[:], lb[:], ACT.Exp).then_inc(S["lb_exp"], 1)

        def nat_exp(h):
            act.wait_ge(S["nat_max"], h + 1)
            for i in range(NT):
                last = A_(pp[:, h, i], pp[:, h, i], ACT.Exp, bias=small[:, 2 * h + i:2 * h + i + 1],
                          accum_out=small[:, 8 + 2 * h + i:9 + 2 * h + i])
            last.then_inc(S["nat_exp"], 1)

        def nat_copy(h):
            copy_bank(ppT[:, h].rearrange("p j i -> p (j i)"), 7 if h % 2 == 0 else 4, S["nat_turned"], h + 1, S["nat_pT"])

        def nat_y():
            act.wait_ge(S["nat_out"], 1)
            nc.scalar.copy(y[:, :, 256:512], ps[:, 5, :].rearrange("p (t c) -> p t c", t=2)).then_inc(S["nat_y"], 1)

        def dif_exp(h):
            act.wait_ge(S["dif_max"], h + 1)
            for s in range(2):
                for i in range(NT):
                    c = 32 + 8 * h + 2 * s + i
                    last = A_(ee[:, h % 2, s, i], ee[:, h % 2, s, i], ACT.Exp, bias=small[:, c:c + 1],
                              accum_out=small[:, c + 4:c + 5])
            last.then_inc(S["dif_exp"], 1)

        def dif_copy(h):
            copy_bank(ppT[:, h].rearrange("p j i -> p (j i)"), 6 + h % 2, S["dif_turned"], h + 1, S["dif_aT"])

        def dif_o():
            act.wait_ge(S["dif_out"], 1)
            act.wait_ge(S["y_ready"], 1)
            for i in range(NT):
                nc.scalar.copy(oo[:, 512 * i:512 * i + 512], ps[:, 4 + i, :]).then_inc(S["dif_copied"], 1)

        def lam_exp():
            act.wait_ge(S["lam_sums"], 2)
            A_(small[:, 66:68], small[:, 64:66], ACT.Exp).then_inc(S["lam_exps"], 1)

        def log_f():
            for t in range(NT):
                act.wait_ge(S["f_ready"], t + 1)
                A_(logf[:, t], logf[:, t], ACT.Ln).then_inc(S["logf_ready"], 1)

        def kc_copy():
            act.wait_ge(S["kc_turned"], 1)
            for d in range(2):
                nc.scalar.copy(kc[:, d].rearrange("p c t -> p (c t)"), ps[:, 6 + d, :]).then_inc(S["kc_ready"], 1)

        def seg_exp(lv):
            if lv == 0:
                act.wait_ge(S["kc_ready"], 2)
                act.wait_ge(S["y_ready"], 2)
                act.wait_ge(S["kc_turned"], 1)
            if lv >= 2:
                act.wait_ge(S["qk_ready"], lv - 1)
            act.wait_ge(S["seg_sums"], lv + 1)
            for d in range(2):
                A_(Eb[:, lv % 2, d].rearrange("p c t -> p (c t)"), ps[:, 4 + d, :], ACT.Exp).then_inc(S["seg_exp"], 1)

        def hg_off():
            act.wait_ge(S["hg_scores"], 1)
            act.wait_ge(S["dif_out"], 1)
            for x in range(2):
                nc.scalar.copy(offd[:, x].rearrange("p x h i -> p (x h i)"), ps[:, 6 + x, :]).then_inc(S["hg_off"], 1)

        def hg_copy():
            act.wait_ge(S["qk_ready"], LEVELS)
            act.wait_ge(S["hg_out"], 1)
            nc.scalar.copy(oo[:, 0:512], ps[:, 4, :]).then_inc(S["hg_copied"], 1)

        after = {
            4: [ret_copy], 6: [lambda: nat_exp(0), lambda: nat_exp(1)], 8: [lambda: nat_copy(0), lambda: nat_copy(1)],
            9: [lambda: nat_exp(2), lambda: nat_exp(3)], 11: [lambda: nat_copy(2), lambda: nat_copy(3)],
            12: [nat_y, lam_exp, lower_exp], 14: [lambda: dif_exp(0)],
            15: [lambda: dif_exp(1)], 16: [lambda: dif_copy(0)], 17: [lambda: dif_copy(1), lambda: dif_exp(2)],
            18: [lambda: dif_copy(2), log_f], 19: [lambda: dif_exp(3)], 20: [lambda: dif_copy(3)], 21: [dif_o],
            22: [kc_copy, lambda: seg_exp(0)], 23: [hg_off], 32: [hg_copy],
        }
        for n in range(2):
            high_m(n)
        high_turned(0)
        act.wait_ge(S["h_ready"], NT)
        for r in (0, 64):
            act.dma_start(hk[r:r + 64], dram(A["rpb"], 0, [[1, 64], [127, HEADS * 7], [1, 64]])).then_inc(S["nat_landed"], 16)
        for n in range(N_PROJ):
            high_m(n + 2)
            if n % 2 == 1:
                evacuate(n // 2)
            for task in after.get(n, ()):
                task()
            if 23 <= n < 23 + DIAG - 1:
                seg_exp(n - 22)

        def high_y(rnd):
            act.wait_ge(S["y_turned"], rnd + 1)
            nq = min(4, 10 - 4 * rnd)
            b0 = 4 + 2 * (rnd % 2)
            for b in range((nq + 1) // 2):
                last = nc.scalar.copy(yT[:, 0, 4 * rnd + 2 * b:4 * rnd + 2 * b + 2, :],
                                      ps[:, b0 + b, :].rearrange("p (q t) -> p q t", q=2))
            last.then_inc(S["yT_hi"], 1)

        for rnd in range(3):
            high_y(rnd)
        for n in range(N_PROJ + 2, NM):
            high_m(n)
            if n == N_PROJ + N_BR + 1:
                act.wait_ge(S["mg_ready"], 1)
                act.wait_ge(S["pe_used"], N_PROJ)
                nc.scalar.copy(aT[:, 0].rearrange("p k t -> p (k t)"), mg[:].rearrange("p k t -> p (k t)")).then_inc(S["mg_hi"], 1)
        act.wait_ge(S["router_landed"], 48)
        nc.scalar.copy(wrs[:, 0], wr[:]).then_inc(S["wr_hi"], 1)
        for n in range(NM, NM + 2):
            high(n, raw_slot(n), n % 3, raw_count(n))
        high_turned(NT)
        act.wait_ge(S["logits"], 1)
        A_(tk[:, 0:128], ps[:, 6, 0:128], ACT.Sigmoid).then_inc(S["scores_ready"], 1)

        def silu(x, t):
            act.wait_ge(S["gu_ready"] if t == 0 else S["pe_used"], (x + 1) if t == 0 else gu_used(x))
            if not (isinstance(x, int) and x == 0):
                act.wait_ge(S["hid_done"], x * 2 + (t - 1))
            A_(sil[:, t], ps[:, 4 + t, 0:HID], ACT.Silu).then_inc(S["silu_done"], 1)

        def high_hidden(x, n):
            for t in range(NT):
                act.wait_ge(S["hid_turned"], x * 2 + (t + 1))
                if t == 0 and not (isinstance(x, int) and x == 0):
                    act.wait_ge(S["pe_used"], n)
                nc.scalar.copy(hTs[:, 0, t], ps[:, 6 + t, 0:256].rearrange("p (j c) -> p j c", j=2)).then_inc(S["hhi_done"], 1)

        def step(x, n, rslots, landed):
            base = (NM + 2) % 3
            high(n, rslots[0], base, landed[0])
            silu(x - 1, 0)
            silu(x - 1, 1)
            high(n + 1, rslots[1], (base + 1) % 3, landed[1])
            high_hidden(x - 1, n)
            high(n + 2, rslots[2], (base + 2) % 3, landed[2])

        def static_step(x):
            n = NM + 2 + 3 * (x - 1)
            step(x, n, [raw_slot(n + j) for j in range(3)], [raw_count(n + j) for j in range(3)])

        static_step(1)
        with act.Fori(0, (X_LAST - 2) // 2) as i:
            for u in range(2):
                n0 = NM + 5 + 3 * u
                step(i * 2 + (2 + u), i * 6 + n0, [raw_slot(n0 + j) for j in range(3)],
                     [i * 32 + raw_count(n0 + j) for j in range(3)])
        static_step(X_LAST)
        n = NM + 2 + 3 * X_LAST
        silu(X_LAST, 0)
        silu(X_LAST, 1)
        high_hidden(X_LAST, n)
        high(n, raw_slot(n), n % 3, raw_count(n))

    @block.gpsimd
    def _(pool):
        nc.gpsimd.memset(pow_c[:], -0.5).then_inc(S["pool_step"], 1)
        pool.wait_ge(S["pool_step"], 1)
        norms = [0]

        def power(dst, src, w):
            norms[0] += 1
            pool.wait_ge(S["mv_ready"], norms[0])
            nc.gpsimd.tensor_tensor(dst, src, pow_c[:, 0:w], ALU.pow).then_inc(S["rstd_ready"], 1)

        power(small[:, 76:78], small[:, 74:76], 2)
        pool.wait_ge(S["vec_landed"], 80)
        pool.wait_ge(pair_free[1], 2)
        for t in range(NT):
            last = nc.gpsimd.tensor_tensor(rg[:, t], rg[:, t], gnr[:], ALU.mult)
        last.then_inc(S["gate_mul"], 1)
        power(small[:, 88:96], small[:, 80:88], 8)
        power(small[:, 88:96], small[:, 80:88], 8)
        pool.wait_ge(pair_free[0], 2 * 5)
        for t in range(NT):
            last = nc.gpsimd.tensor_tensor(hg[:, t], hg[:, t], gnh[:], ALU.mult)
        last.then_inc(S["gate_mul"], 1)
        for lv in range(DIAG):
            if lv == 0:
                pool.wait_ge(S["y_ready"], 2)
            if lv >= 2:
                pool.wait_ge(S["hg_scores"], lv - 1)
            nc.gpsimd.memset(Qb[:, lv % 2], 0.0).then_inc(S["q_zero"], 1)
            if lv >= 3:
                add_level(pool, lv - 1)
        for lv in (DIAG - 1, DIAG):
            add_level(pool, lv)
        power(small[:, 88:96], small[:, 80:88], 8)
        for b in range(1, 4):
            for g in range(4):
                pool.wait_ge(S["mul_ready"], 4 * b + g + 1)
                src = mgt[:, g % 2].rearrange("p a t -> p (a t)")
                dst = mg[:, 2 * g:2 * g + 2].rearrange("p a t -> p (a t)")
                nc.gpsimd.tensor_tensor(dst, dst, src, ALU.add).then_inc(S["br_read"], 1)
        power(small[:, 76:78], small[:, 74:76], 2)
        power(small[:, 76:78], small[:, 74:76], 2)

    @block.vector
    def _(dve):
        one = Steps(dve, S["dve_step"])
        V = nc.vector
        norms = [0]

        def low(n, rslot, slot):
            dve.wait_ge(S["hi_done"], n + 1)
            V.tensor_tensor(wlo[:, slot], raw(rslot), whi[:, slot].bitcast(F32), ALU.subtract).then_inc(S["lo_done"], 1)

        def low_m(n):
            if n < NM:
                low(n, raw_slot(n), n % 3)

        def layer_norm(src, dst, gb, landed, landed_count, ready, waits=None):
            st = small[:, 128:128 + 24].rearrange("p (t s) -> p t s", t=NT)
            mv = small[:, 68:72].rearrange("p (t s) -> p t s", t=NT)
            for t in range(NT):
                if waits:
                    waits(t)
                for q in range(2):
                    one(V.bn_stats(st[:, t, 6 * q:6 * q + 6], src[:, t, 512 * q:512 * q + 512]))
                one(V.bn_aggr(mv[:, t], st[:, t]))
            norms[0] += 1
            V.tensor_scalar(small[:, 74:76], mv[:, :, 1], EPS, None, ALU.add).then_inc(S["mv_ready"], 1)
            dve.wait_ge(S["rstd_ready"], norms[0])
            dve.wait_ge(landed, landed_count)
            for t in range(NT):
                one(V.tensor_scalar(dst[:, t], src[:, t], mv[:, t, 0:1], small[:, 76 + t:77 + t], ALU.subtract, ALU.mult))
                one(V.tensor_tensor(dst[:, t], dst[:, t], gb[:, 0], ALU.mult))
                V.tensor_tensor(dst[:, t], dst[:, t], gb[:, 1], ALU.add).then_inc(ready, 1)

        def low_turned(count):
            for t in range(NT):
                dve.wait_ge(S["aT_hi"], count + t + 1)
                for b in range(2):
                    last = V.tensor_tensor(aT[:, 1, 4 * b:4 * b + 4, t * P:(t + 1) * P],
                                           ps[:, 4 + 2 * t + b, :].rearrange("p (k c) -> p k c", k=4),
                                           aT[:, 0, 4 * b:4 * b + 4, t * P:(t + 1) * P].bitcast(F32), ALU.subtract)
                last.then_inc(S["aT_lo"], 1)

        def evacuate(blk):
            pair = blk % 2
            b0, free = 2 * pair, pair_free[pair]
            if blk >= len(W_IN_ORDER):
                return
            b = W_IN_ORDER[blk]
            dst = {0: rqk, 2: nqk, 6: dqT, 7: dkT}.get(b)
            if dst is None:
                return
            dve.wait_ge(S["pe_used"], 2 * blk + 2)
            if b == 6:
                dve.wait_ge(S["ret_scores"], HEADS)
            for c in range(2):
                d = dst[:, 2 * c:2 * c + 2].rearrange("p c t -> p (c t)")
                f = SCALE if (b == 2 and c == 0) or b == 6 else 1.0
                V.tensor_scalar(d, ps[:, b0 + c, :], f, None, ALU.mult).then_inc(free, 1)

        def ret_decay():
            dve.wait_ge(S["ret_landed"], 16)
            for h in range(HEADS):
                dve.wait_ge(S["ret_scores"], h + 1)
                V.tensor_tensor(retS[:, h].rearrange("p j i -> p (j i)"), ps[:, 4 + h, :],
                                retM[:, h].rearrange("p j i -> p (j i)"), ALU.mult).then_inc(S["ret_decayed"], 1)

        def rms(width, gain, col, gains_ready):
            n = NT * HEADS * width
            o, sq = oo[:, 0:n], osq[:, 0:n]
            one(V.tensor_tensor(sq, o, o, ALU.mult))
            one(V.tensor_reduce(small[:, 96:104], sq.rearrange("p (g c) -> p g c", c=width), AX.X, ALU.add))
            norms[0] += 1
            V.tensor_scalar(small[:, 80:88], small[:, 96:104], 1.0 / width, EPS, ALU.mult, ALU.add).then_inc(S["mv_ready"], 1)
            dve.wait_ge(S["rstd_ready"], norms[0])
            r = small[:, 88:96].unsqueeze(2).to_broadcast([P, NT * HEADS, width])
            one(V.tensor_tensor(sq.rearrange("p (g c) -> p g c", c=width), o.rearrange("p (g c) -> p g c", c=width), r, ALU.mult))
            if gains_ready is not None:
                dve.wait_ge(S["gate_mul"], gains_ready)
            w = HEADS * width
            V.tensor_tensor(y[:, :, col:col + w], sq.rearrange("p (t c) -> p t c", t=NT), gain, ALU.mult).then_inc(S["y_ready"], 1)

        def ret_norm():
            dve.wait_ge(S["ret_copied"], 1)
            rms(64, rg[:], 0, 1)

        def nat_mask(h):
            dve.wait_ge(S["nat_scores"], h + 1)
            V.tensor_tensor(pp[:, h], ps[:, 5 + h % 2, :].rearrange("p (i k) -> p i k", i=NT),
                            natm[:].unsqueeze(1).to_broadcast([P, NT, TOKENS]), ALU.add).then_inc(S["nat_masked"], 1)
            dve.wait_ge(S["nat_masked"], h + 1)
            V.tensor_reduce(small[:, 2 * h:2 * h + 2], pp[:, h], AX.X, ALU.max, negate=True).then_inc(S["nat_max"], 1)

        def nat_norm(h):
            dve.wait_ge(S["nat_exp"], h + 1)
            one(V.reciprocal(small[:, 16 + 2 * h:18 + 2 * h], small[:, 8 + 2 * h:10 + 2 * h]))
            for i in range(NT):
                last = V.tensor_scalar(pp[:, h, i], pp[:, h, i], small[:, 16 + 2 * h + i:17 + 2 * h + i], None, ALU.mult)
            last.then_inc(S["nat_p"], 1)

        def dif_bias(h):
            dve.wait_ge(S["dif_scores"], h + 1)
            b0 = 6 if h == 0 else 4
            slope = 2.0 ** (-8.0 * (h + 1) / HEADS)
            if h == 0:
                dve.wait_ge(S["nat_landed"], 80)
                dve.wait_ge(S["y_ready"], 1)
            if h >= 2:
                dve.wait_ge(S["dif_a"], h - 1)
            for s in range(2):
                V.scalar_tensor_tensor(out=ee[:, h % 2, s].rearrange("p i k -> p (i k)"), in0=dist[:].rearrange("p i k -> p (i k)"),
                                       scalar=-slope, in1=ps[:, b0 + s, :], op0=ALU.mult, op1=ALU.add).then_inc(S["dif_biased"], 1)
            dve.wait_ge(S["dif_biased"], 2 * h + 2)
            c = 32 + 8 * h
            V.tensor_reduce(small[:, c:c + 4], ee[:, h % 2].rearrange("p s i k -> p (s i) k"), AX.X, ALU.max,
                            negate=True).then_inc(S["dif_max"], 1)

        def dif_combine(h):
            dve.wait_ge(S["dif_exp"], h + 1)
            if h == 0:
                dve.wait_ge(S["nat_turned"], HEADS)
            c = 36 + 8 * h
            one(V.reciprocal(small[:, 104:108], small[:, c:c + 4]))
            one(V.tensor_scalar(small[:, 108:110], small[:, 106:108], small[:, 64:65], None, ALU.mult))
            for i in range(NT):
                last = V.tensor_scalar(ee[:, h % 2, 1, i], ee[:, h % 2, 1, i], small[:, 108 + i:109 + i], None, ALU.mult)
            one(last)
            for i in range(NT):
                last = V.scalar_tensor_tensor(out=pp[:, h, i], in0=ee[:, h % 2, 0, i], scalar=small[:, 104 + i:105 + i],
                                              in1=ee[:, h % 2, 1, i], op0=ALU.mult, op1=ALU.subtract)
            last.then_inc(S["dif_a"], 1)
            dve.wait_ge(S["dif_a"], h + 1)

        def lam_sums():
            dve.wait_ge(S["vec_landed"], 80)
            v = lamv[:].rearrange("p (a b c) -> p a b c", a=2, b=2)
            w = small[:, 256:384].rearrange("p (a c) -> p a c", a=2)
            one(V.tensor_tensor(w, v[:, :, 0], v[:, :, 1], ALU.mult))
            V.tensor_reduce(small[:, 64:66], w, AX.X, ALU.add).then_inc(S["lam_sums"], 2)
            one(V.tensor_scalar(gnd[:], gnd[:], 1.0 - LAM_INIT, None, ALU.mult))

        def lam():
            dve.wait_ge(S["lam_exps"], 1)
            one(V.tensor_tensor(small[:, 64:65], small[:, 66:67], small[:, 67:68], ALU.subtract))
            one(V.tensor_scalar(small[:, 64:65], small[:, 64:65], LAM_INIT, None, ALU.add))

        def dif_norm():
            dve.wait_ge(S["dif_copied"], NT)
            rms(P, gnd[:].unsqueeze(1).to_broadcast([P, NT, 512]), 768, None)

        def lower_shift():
            dve.wait_ge(S["lb_landed"], 16)
            V.tensor_tensor(lb[:], lbv[:], lbv[:], ALU.subtract).then_inc(S["lb_shift"], 1)

        def lower():
            dve.wait_ge(S["lb_exp"], 1)
            one(V.reciprocal(lbv[:], lb[:]))
            one(V.tensor_tensor(lbv[:], lb[:], lbv[:], ALU.mult))
            one(V.tensor_tensor(lb[:], lbv[:], lbv[:], ALU.subtract))
            one(V.tensor_scalar(om[:], lb[:], -1.0, 1.0, ALU.mult, ALU.add))

        def forget():
            dve.wait_ge(pair_free[1], 2 * 4)
            for t in range(NT):
                one(V.tensor_tensor(logf[:, t], logf[:, t], om[:], ALU.mult))
                one(V.tensor_tensor(logf[:, t], logf[:, t], lb[:], ALU.add))
                V.tensor_scalar(logf[:, t], logf[:, t], LOG_FLOOR, None, ALU.max).then_inc(S["f_ready"], 1)
            for t in range(NT):
                last = V.tensor_tensor(kTM[:, t], kTM[:, t], om[:], ALU.mult)
            last.then_inc(S["km_ready"], 1)

        def queries_keys(lv):
            if lv == 0:
                dve.wait_ge(S["kc_ready"], 2)
            if lv == DIAG:
                dve.wait_ge(S["hg_scores"], lv - 1)
                V.tensor_tensor(Kb[:, lv % 2, 0], kc[:, 0], kc[:, 1], ALU.add).then_inc(S["qk_ready"], 1)
                return
            dve.wait_ge(S["q_zero"], lv + 1)
            dve.wait_ge(S["seg_exp"], 2 * lv + 2)
            if lv >= 2:
                dve.wait_ge(S["hg_scores"], lv - 1)
            half = P >> lv
            E, Q, K = Eb[:, lv % 2], Qb[:, lv % 2], Kb[:, lv % 2]
            V.tensor_tensor(K.rearrange("p d c t -> p (d c t)"), kc[:].rearrange("p d c t -> p (d c t)"),
                            E.rearrange("p d c t -> p (d c t)"), ALU.mult)
            for d in range(2):
                s = 1 - d
                q, e, o = (v.rearrange("p c (b s m) -> p (c b) s m", s=2, m=half)[:, :, s] for v in (hq[:], E[:, d], Q[:, d]))
                last = V.tensor_tensor(o, q, e, ALU.mult)
            last.then_inc(S["qk_ready"], 1)

        def mask_level(lv):
            dve.wait_ge(S["hg_scores"], lv + 1)
            if lv == 1:
                dve.wait_ge(S["y_ready"], 2)
            if lv >= 3:
                dve.wait_ge(S["hg_added"], lv - 2)
            mk = (ident[:] if lv == DIAG else msk[:, lv - 1]).unsqueeze(1).to_broadcast([P, HEADS, P])
            dst = accS if lv == 1 else tmpS
            for x in range(2):
                V.tensor_tensor(dst[:, x].rearrange("p x h i -> p (x h) i"), ps[:, 6 + x, :].rearrange("p (h i) -> p h i", h=HEADS), mk, ALU.mult).then_inc(S["hg_masked"], 1)

        def hg_norm():
            dve.wait_ge(S["hg_copied"], 1)
            rms(64, hg[:], 512, 2)

        after = {
            2: [ret_decay, lam_sums], 4: [ret_norm],
            6: [lambda: nat_mask(0), lambda: nat_mask(1), lambda: nat_norm(0), lambda: nat_norm(1)],
            9: [lambda: nat_mask(2), lambda: nat_mask(3), lambda: nat_norm(2), lambda: nat_norm(3)],
            8: [lower_shift], 13: [lam, lower], 14: [lambda: dif_bias(0), lambda: dif_combine(0)], 15: [forget, lambda: dif_bias(1), lambda: dif_combine(1)],
            17: [lambda: dif_bias(2), lambda: dif_combine(2)], 19: [lambda: dif_bias(3), lambda: dif_combine(3)],
            21: [dif_norm], 32: [hg_norm],
        }
        layer_norm(xin, h0, lnb, S["lnin_landed"], 32, S["h_ready"], lambda t: dve.wait_ge(x_landed[t], 16))
        for n in range(2):
            low_m(n)
        low_turned(0)
        for n in range(N_PROJ):
            low_m(n + 2)
            if n % 2 == 1:
                evacuate(n // 2)
            for task in after.get(n, ()):
                task()
            if 22 <= n < 22 + LEVELS:
                queries_keys(n - 22)
            if 24 <= n < 24 + DIAG:
                mask_level(n - 23)

        for rnd in range(3):
            dve.wait_ge(S["yT_hi"], rnd + 1)
            nq = min(4, 10 - 4 * rnd)
            b0 = 4 + 2 * (rnd % 2)
            for b in range((nq + 1) // 2):
                q = slice(4 * rnd + 2 * b, 4 * rnd + 2 * b + 2)
                last = V.tensor_tensor(yT[:, 1, q, :], ps[:, b0 + b, :].rearrange("p (q t) -> p q t", q=2),
                                       yT[:, 0, q, :].bitcast(F32), ALU.subtract)
            last.then_inc(S["yT_lo"], 1)

        def merge(b):
            dve.wait_ge(S["pe_used"], N_PROJ + (b + 1 if b < 3 else N_BR))
            for g in range(4):
                gates = (g0 if b < 2 else g1)[:, (2 * b + g // 2) % 4, 2 * (g % 2):2 * (g % 2) + 2]
                if b == 0:
                    dst = mg[:, 2 * g:2 * g + 2]
                    if g == 0:
                        dve.wait_ge(S["y_turned"], 3)
                else:
                    if 4 * (b - 1) + g >= 2:
                        dve.wait_ge(S["br_read"], 4 * (b - 1) + g - 1)
                    dst = mgt[:, g % 2]
                V.tensor_tensor(dst.rearrange("p a t -> p (a t)"), ps[:, 4 * (b % 2) + g, :],
                                gates.rearrange("p a t -> p (a t)"), ALU.mult).then_inc(S["mul_ready"], 1)

        for n in range(N_PROJ + 2, NM):
            low_m(n)
            if n < N_PROJ + N_BR:
                merge(n - N_PROJ - 2)
            if n == N_PROJ + N_BR:
                merge(3)
                dve.wait_ge(S["br_read"], 12)
                V.memset(small[:, 500:501], 0.0).then_inc(S["mul_ready"], 4)
                V.memset(small[:, 501:502], 0.0).then_inc(S["mg_ready"], 1)
            if n == N_PROJ + N_BR + 1:
                dve.wait_ge(S["mg_hi"], 1)
                V.tensor_tensor(aT[:, 1].rearrange("p k t -> p (k t)"), mg[:].rearrange("p k t -> p (k t)"),
                                aT[:, 0].rearrange("p k t -> p (k t)").bitcast(F32), ALU.subtract).then_inc(S["mg_lo"], 1)
        dve.wait_ge(S["h0_back"], 16)
        dve.wait_ge(S["pe_used"], NM)

        def add_residual(src, t, sem=None):
            for half in range(2):
                last = V.scalar_tensor_tensor(out=src[1][:, t, half * 512:(half + 1) * 512],
                                              in0=src[0][:, t, half * 512:(half + 1) * 512], scalar=ALPHA,
                                              in1=ps[:, 2 * t + half, :], op0=ALU.mult, op1=ALU.add)
            last.then_inc(S["out_read"], 1)

        for t in range(NT):
            add_residual((h0b, zz), t)
        dve.wait_ge(S["out_read"], NT)
        dve.wait_ge(S["wr_hi"], 1)
        V.tensor_tensor(wrs[:, 1], wr[:], wrs[:, 0].bitcast(F32), ALU.subtract).then_inc(S["wr_lo"], 1)
        layer_norm(zz, zz, ln1b, S["ln1_landed"], 32, S["h_ready"])
        for n in range(NM, NM + 2):
            low(n, raw_slot(n), n % 3)
        low_turned(NT)

        dve.wait_ge(S["scores_ready"], 1)
        sc = tk[:, 0:128].rearrange("p (t e) -> p t e", t=NT)
        biased = tk[:, 128:256].rearrange("p (t e) -> p t e", t=NT)
        one(V.tensor_tensor(biased, sc, rbb[:].unsqueeze(1).to_broadcast([P, NT, 64]), ALU.add))
        for t in range(NT):
            top = tk[:, 256:320]
            for g in range(N_GROUPS):
                last = V.max(top[:, 8 * g:8 * g + 8], biased[:, t, 8 * g:8 * g + 8])
            one(last)
            gs = tk[:, 320:328]
            tv = top.rearrange("p (g k) -> p g k", g=N_GROUPS)
            one(V.tensor_tensor(gs, tv[:, :, 0], tv[:, :, 1], ALU.add))
            other = gs.unsqueeze(1).to_broadcast([P, 8, 8])
            own = gs.unsqueeze(2).to_broadcast([P, 8, 8])
            gt = tk[:, 384:448].rearrange("p (a b) -> p a b", a=8)
            eq = tk[:, 448:512].rearrange("p (a b) -> p a b", a=8)
            V.tensor_tensor(gt, other, own, ALU.is_gt)
            one(V.tensor_tensor(eq, other, own, ALU.is_equal))
            one(V.tensor_tensor(eq, eq, tri[:].rearrange("p (a b) -> p a b", a=8), ALU.mult))
            one(V.tensor_tensor(gt, gt, eq, ALU.add))
            rank = tk[:, 328:336]
            one(V.tensor_reduce(rank, gt, AX.X, ALU.add))
            keep = tk[:, 336:344]
            drop = tk[:, 344:352]
            one(V.tensor_scalar(keep, rank, TOPK_GROUPS - 0.5, None, ALU.is_lt))
            one(V.tensor_scalar(drop, keep, -MASK, MASK, ALU.mult, ALU.add))
            cand = tk[:, 512:576]
            cv = cand.rearrange("p (g k) -> p g k", g=8)
            one(V.tensor_tensor(cv, biased[:, t].rearrange("p (g k) -> p g k", g=8), keep.unsqueeze(2).to_broadcast([P, 8, 8]), ALU.mult))
            one(V.tensor_tensor(cv, cv, drop.unsqueeze(2).to_broadcast([P, 8, 8]), ALU.add))
            best = tk[:, 352:360]
            one(V.max(best, cand))
            left = tk[:, 576:640]
            one(V.match_replace(left, best, cand, 3.0 * MASK))
            sel = tk[:, 640:704]
            one(V.tensor_tensor(sel, cand, left, ALU.not_equal))
            one(V.tensor_tensor(sel, sel, sc[:, t], ALU.mult))
            one(V.tensor_reduce(tk[:, 360:361], sel, AX.X, ALU.add))
            one(V.tensor_scalar(tk[:, 361:362], tk[:, 360:361], 1e-20, None, ALU.add))
            one(V.reciprocal(tk[:, 362:363], tk[:, 361:362]))
            one(V.tensor_scalar(comb[:, t], sel, tk[:, 362:363], ROUTED_SCALE, ALU.mult, ALU.mult))

        def hidden(x, t):
            dve.wait_ge(S["silu_done"], x * 2 + (t + 1))
            first = isinstance(x, int) and x == 0
            if not first:
                dve.wait_ge(S["hid_turned"], x * 2 + (t - 1))
            up = ps[:, 4 + t, HID:2 * HID]
            if first:
                V.tensor_tensor(hid[:, t], up, sil[:, t], ALU.mult).then_inc(S["hid_done"], 1)
            else:
                e = x - 1
                w = comb[:, t, e:e + 1] if isinstance(e, int) else comb[:, t, bass.ds(e, 1)]
                V.scalar_tensor_tensor(out=hid[:, t], in0=up, scalar=w, in1=sil[:, t], op0=ALU.mult,
                                       op1=ALU.mult).then_inc(S["hid_done"], 1)

        def low_hidden(x):
            for t in range(NT):
                dve.wait_ge(S["hhi_done"], x * 2 + (t + 1))
                V.tensor_tensor(hTs[:, 1, t], ps[:, 6 + t, 0:256].rearrange("p (j c) -> p j c", j=2),
                                hTs[:, 0, t].bitcast(F32), ALU.subtract).then_inc(S["hlo_done"], 1)

        def step(x, n, rslots):
            base = (NM + 2) % 3
            low(n, rslots[0], base)
            hidden(x - 1, 0)
            hidden(x - 1, 1)
            low(n + 1, rslots[1], (base + 1) % 3)
            low_hidden(x - 1)
            low(n + 2, rslots[2], (base + 2) % 3)

        def static_step(x):
            n = NM + 2 + 3 * (x - 1)
            step(x, n, [raw_slot(n + j) for j in range(3)])

        static_step(1)
        with dve.Fori(0, (X_LAST - 2) // 2) as i:
            for u in range(2):
                n0 = NM + 5 + 3 * u
                step(i * 2 + (2 + u), i * 6 + n0, [raw_slot(n0 + j) for j in range(3)])
        static_step(X_LAST)
        n = NM + 2 + 3 * X_LAST
        hidden(X_LAST, 0)
        hidden(X_LAST, 1)
        low_hidden(X_LAST)
        low(n, raw_slot(n), n % 3)
        dve.wait_ge(S["pe_used"], n + 1)
        for t in range(NT):
            add_residual((zz, outb), t)
        dve.wait_ge(S["out_read"], 2 * NT)
        layer_norm(outb, outb, ln2b, S["ln2_landed"], 32, S["z_ready"])

    ctx.close()


_INPUTS = ["x", "ln_in_g", "ln_in_b", "w_in", "w_gate", "b_gate", "w_br_ret", "w_br_nat", "w_br_hgrn", "w_br_diff",
           "w_out", "ret_gn", "rpb", "hgrn_lb", "hgrn_gn", "diff_lambda", "diff_subln", "ln1_g", "ln1_b", "w_router",
           "router_bias", "w_e_gate", "w_e_up", "w_e_down", "w_s_gate", "w_s_up", "w_s_down", "ln2_g", "ln2_b"]


def kernel(**inputs):
    import concourse.bacc as bacc
    from concourse.bass_utils import run_bass_kernel_spmd

    a = {k: np.asarray(v) for k, v in inputs.items()}
    a["b_gate"] = np.ascontiguousarray(a["b_gate"].reshape(32, P).T)
    rpb = a.pop("nat_rpb")[0]
    pad = np.zeros((HEADS, 7, 127), rpb.dtype)
    pad[:, :, 48:79] = rpb[:, 4:11]
    a["rpb"] = pad
    arrays = {k: np.ascontiguousarray(a[k]) for k in _INPUTS}
    arrays.update(constants())
    nc = bacc.Bacc("TRN2", target_bir_lowering=False, num_devices=1)
    args = {k: nc.dram_tensor("in_" + k, v.shape, mybir.dt.from_np(v.dtype), kind="ExternalInput").ap() for k, v in arrays.items()}
    out = nc.dram_tensor("out_0", (1, TOKENS, D), F32, kind="ExternalOutput").ap()
    build(nc, args, out)
    r = run_bass_kernel_spmd(nc, [{"in_" + k: v for k, v in arrays.items()}], core_ids=[0])
    return r.results[0]["out_0"]
```

```python
from contextlib import ExitStack

import numpy as np

import concourse.bass as bass
from concourse import mybir

F32 = mybir.dt.float32
F32R = mybir.dt.float32r
ACT = mybir.ActivationFunctionType
ALU = mybir.AluOpType
AX = mybir.AxisListType

P = 128
TOKENS, D = 256, 1024
NT = TOKENS // P
KD = D // P
HEADS = 4
GRID_W, ROWS = 64, 4
N_EXPERTS, N_GROUPS, TOPK_GROUPS = 64, 8, 4
HID = 256
SCALE = 64 ** -0.5
EPS = 1e-5
ALPHA = 2.0 ** 0.25
ROUTED_SCALE = 2.5
LAM_INIT = 0.2
MASK = -1e30
LOG_FLOOR = 2.0 ** -64
PASSES = ((0, 0), (0, 1), (1, 0))

CH = 2048
W_IN_ORDER = (0, 1, 2, 3, 6, 7, 8, 4, 5)
NB = len(W_IN_ORDER) + 8
N_PROJ = 2 * NB
N_BR = 5
N_OUT = 4
NM = N_PROJ + N_BR + N_OUT
PAIRS = N_EXPERTS // 2
LEVELS = 9
DIAG = LEVELS - 1


def constants():
    i = np.arange(TOKENS)
    dist = np.abs(i[:, None] - i[None, :]).astype(np.float64)
    ret = np.zeros((HEADS, TOKENS, TOKENS))
    for h in range(HEADS):
        lf, lb = np.log1p(-2.0 ** (-5 - 2 * h)), np.log1p(-2.0 ** (-6 - 2 * h))
        d = i[None, :] - i[:, None]
        ret[h] = np.where(d > 0, np.exp(lf * d), np.where(d < 0, np.exp(-lb * d), 2.0)) * SCALE
    ret = ret.reshape(HEADS, NT, P, TOKENS).transpose(2, 0, 1, 3)
    c = np.arange(GRID_W)
    start = np.clip(c - 8, 0, GRID_W - 16)
    ok = (c[None, :] >= start[:, None]) & (c[None, :] < start[:, None] + 16)
    nat = np.tile(np.where(ok, 0.0, MASK), (2, ROWS))
    t = np.arange(P)
    seg = np.zeros((P, 2, LEVELS - 2, P))
    mask = np.zeros((P, LEVELS - 2, P))
    for lv in range(1, DIAG):
        m = P >> lv
        blk, half = t // (2 * m), (t // m) % 2
        b = blk * 2 * m + m - 1
        u = t[:, None]
        fwd = np.where(half[None] == 1, (u > b[None]) & (u <= t[None]), (u > t[None]) & (u <= b[None]))
        bwd = np.where(half[None] == 0, (u >= t[None]) & (u <= b[None]), (u > b[None]) & (u < t[None]))
        seg[:, 0, lv - 1], seg[:, 1, lv - 1] = fwd, bwd
        mask[:, lv - 1] = (blk[:, None] == blk[None]) & (half[:, None] != half[None])
    seg0 = np.zeros((P, 2, NT, P))
    u = t[:, None]
    seg0[:, 0, 0], seg0[:, 0, 1] = u > t[None], u <= t[None]
    seg0[:, 1, 0], seg0[:, 1, 1] = u >= t[None], u < t[None]
    rev = np.zeros((64, 64))
    rev[np.arange(64), 63 - np.arange(64)] = 1.0
    rev = np.concatenate([rev, rev])
    tri = (np.arange(8)[None, :] < np.arange(8)[:, None]).astype(np.float64)
    up = (np.arange(P)[:, None] < np.arange(P)[None, :]).astype(np.float64)
    out = {
        "c_up": np.stack([up, np.ones((P, P))], 1), "c_slot": np.concatenate([np.tile(np.arange(P, dtype=np.float64), (P, 1)), np.arange(P)[:, None]], 1),
        "c_ret": ret, "c_dist": dist.reshape(NT, P, TOKENS).transpose(1, 0, 2), "c_nat": nat,
        "c_seg": seg, "c_seg0": seg0, "c_mask": mask, "c_ident": np.eye(P), "c_rev": rev,
        "c_tri": np.tile(tri.reshape(1, 64), (P, 1)),
    }
    return {k: np.ascontiguousarray(v, dtype=np.float32) for k, v in out.items()}


class Map:

    def __init__(self, nc):
        self.nc, self.top = nc, (nc.sbuf_base + 63) // 64 * 64

    def at(self, offset, name, shape, dt=F32):
        return self.nc.alloc_sbuf_tensor_at(name, [shape[0], *shape[1:]], dt, offset=offset)

    def new(self, name, shape, dt=F32):
        t = self.at(self.top, name, shape, dt)
        self.top += (4 * int(np.prod(shape[1:])) + 31) // 32 * 32
        return t

    def region(self, nbytes):
        r = self.top
        self.top += nbytes
        return r


class Steps:

    def __init__(self, eng, sem):
        self.eng, self.sem, self.n = eng, sem, 0

    def __call__(self, ins):
        ins.then_inc(self.sem, 1)
        self.n += 1
        self.eng.wait_ge(self.sem, self.n)


def bcast(ap, shape):
    return ap.to_broadcast(shape)


def build(nc, A, out):
    m = Map(nc)
    KB = 1024
    whi = m.new("whi", [P, 3, CH], F32R)
    wlo = m.new("wlo", [P, 3, CH], F32R)
    aT = m.new("aT", [P, 2, KD, TOKENS], F32R)
    raw_lo = m.region(3 * 8 * KB)
    ident = m.new("ident", [P, P])
    small = m.new("small", [P, 512])
    pow_c = m.new("pow_c", [P, 16])
    r_x1 = m.region(16 * KB)
    r_in = m.region(36 * KB)
    r_th = m.region(32 * KB)
    r_y = m.region(10 * KB)
    r_c = m.region(16 * KB)
    r_v = m.region(4 * KB)
    assert m.top <= nc.sbuf_usable_end, (m.top, nc.sbuf_usable_end)

    rawL = m.at(raw_lo, "rawL", [P, 3, CH])
    rawH = m.at(r_x1, "rawH", [P, 3, CH])

    retM = m.at(r_x1, "retM", [P, HEADS, NT, TOKENS])
    retS = m.at(r_x1 + 8 * KB, "retS", [P, HEADS, NT, TOKENS])
    g0 = m.at(r_x1, "g0", [P, 4, 4, TOKENS])
    g1 = m.at(r_in, "g1", [P, 4, 4, TOKENS])

    rqk = m.at(r_in, "rqk", [P, 4, TOKENS])
    dqT = m.at(r_in, "dqT", [P, 4, TOKENS])
    rv = m.at(r_in + 4 * KB, "rv", [P, NT, 256])
    rg = m.at(r_in + 6 * KB, "rg", [P, NT, 256])
    nqk = m.at(r_in + 8 * KB, "nqk", [P, 4, TOKENS])
    nv = m.at(r_in + 12 * KB, "nv", [P, NT, 256])
    dkT = m.at(r_in + 14 * KB, "dkT", [P, 4, TOKENS])
    dv = m.at(r_in + 18 * KB, "dv", [P, NT, 512])
    offd = m.at(r_in + 18 * KB, "offd", [P, 2, 2, 2, P])
    hq = m.at(r_in + 22 * KB, "hq", [P, 2, TOKENS])
    kc = m.at(r_in + 24 * KB, "kc", [P, 2, 2, TOKENS])
    logf = m.at(r_in + 28 * KB, "logf", [P, NT, 512])
    hv = m.at(r_in + 32 * KB, "hv", [P, NT, 256])
    hg = m.at(r_in + 34 * KB, "hg", [P, NT, 256])

    xin = m.at(r_in, "xin", [P, NT, D])
    h0 = m.at(r_in + 8 * KB, "h0", [P, NT, D])
    lnb = m.at(r_th, "lnb", [P, 2, D])
    hk = m.at(r_th, "hk", [P, HEADS, 7, 64])
    kTM = m.at(r_th, "kTM", [P, NT, 512])
    pp = m.at(r_th + 8 * KB, "pp", [P, HEADS, NT, TOKENS])
    ppT = m.at(r_th + 16 * KB, "ppT", [P, HEADS, NT, TOKENS])
    ee = m.at(r_th + 24 * KB, "ee", [P, 2, 2, NT, TOKENS])
    oo = m.at(r_th + 28 * KB, "oo", [P, NT * 512])
    osq = m.at(r_th + 24 * KB, "osq", [P, NT * 512])
    Eb = m.at(r_th, "Eb", [P, 2, 2, 2, TOKENS])
    Qb = m.at(r_th + 8 * KB, "Qb", [P, 2, 2, TOKENS])
    Kb = m.at(r_th + 16 * KB, "Kb", [P, 2, 2, TOKENS])
    tmpS = m.at(r_th + 24 * KB, "tmpS", [P, 2, 2, 2, P])
    accS = m.at(r_th + 28 * KB, "accS", [P, 2, 2, 2, P])
    yT = m.at(r_th, "yT", [P, 2, 10, TOKENS], F32R)
    y = m.at(r_y, "y", [P, NT, 1280])
    seg = m.at(r_c, "seg", [P, 2, LEVELS - 2, P])
    seg0 = m.at(r_c + 7 * KB, "seg0", [P, 2, NT, P])
    msk = m.at(r_c + 9 * KB, "msk", [P, LEVELS - 2, P])
    dist = m.at(r_c + 9 * KB + 3584, "dist", [P, NT, TOKENS])
    natm = m.at(r_c + 9 * KB + 3584 + 2 * KB, "natm", [P, TOKENS])
    rev = m.at(r_v, "rev", [P, 64])
    lamv = m.at(r_v + 256, "lamv", [P, 256])
    gnr = m.at(r_v + 1280, "gnr", [P, 256])
    gnh = m.at(r_v + 2304, "gnh", [P, 256])
    lb = m.at(r_x1, "lb", [P, 512])
    om = m.at(r_x1 + 2 * KB, "om", [P, 512])
    lbv = m.at(r_x1 + 4 * KB, "lbv", [P, 512])
    gnd = m.new("gnd", [P, 512])
    bg = m.new("bg", [P, 32])
    assert m.top <= nc.sbuf_usable_end, (m.top, nc.sbuf_usable_end)
    mg = m.at(r_y, "mg", [P, KD, TOKENS])
    mgt = m.at(r_c, "mgt", [P, 2, 2, TOKENS])
    h0b = m.at(r_in + 24 * KB, "h0b", [P, NT, D])
    ln1b = m.at(r_th + 24 * KB, "ln1b", [P, 2, D])
    zz = m.at(r_c, "zz", [P, NT, D])
    wr = m.at(r_in + 8 * KB, "wr", [P, KD, 64])
    wrs = m.at(r_in + 10 * KB, "wrs", [P, 2, KD, 64], F32R)
    rbb = m.at(r_in + 14 * KB, "rbb", [P, 64])
    tri = m.at(r_in + 14 * KB + 256, "tri", [P, 64])
    tk = m.at(r_in + 15 * KB, "tk", [P, 1024])
    comb = m.at(r_in + 19 * KB, "comb", [P, NT, 64])
    place = m.at(r_in + 19 * KB + 512, "place", [P, NT, 64])
    comb_over = m.at(r_in + 20 * KB, "comb_over", [P, NT, 64])
    slot_no = m.at(r_in + 20 * KB + 512, "slot_no", [P, P + 1])
    wc = m.at(r_in + 8 * KB, "wc", [P, NT, PAIRS, 6], F32R)
    up_ones = m.at(r_in + 21 * KB + 544, "up_ones", [P, 2, P])
    over = m.at(r_in + 22 * KB + 576, "over", [P, 8], mybir.dt.int32)
    ys = m.at(r_in + 24 * KB, "ys", [P, 2, D], F32R)
    hTs = m.at(r_in + 32 * KB, "hTs", [P, 2, 2, 2, P], F32R)
    xg = [m.at(r_y, "xg0", [P, 2, KD, P], F32R), m.at(r_th + 16 * KB, "xg1", [P, 2, KD, P], F32R)]
    sil = m.at(r_y + 8 * KB, "sil", [P, 2, HID])
    scT = m.at(r_c + 8 * KB, "scT", [P, TOKENS])
    hid = m.at(r_c + 8 * KB, "hid", [P, 2, HID])
    sel_one = m.at(r_in + 10 * KB, "sel_one", [P, 2, NT, P])
    sel = m.at(r_c + 10 * KB, "sel", [P, 2, NT, P], F32R)
    selT = m.at(r_c + 12 * KB, "selT", [P, 2, NT, P], F32R)
    ident_r = m.at(r_c + 14 * KB, "ident_r", [P, P], F32R)
    h1s = m.at(r_th, "h1s", [P, 2, NT, D], F32R)
    outb = m.at(r_th + 16 * KB, "outb", [P, NT, D])
    ln2b = m.at(r_th + 24 * KB, "ln2b", [P, 2, D])
    cw = small[:, 400:402]
    cw_parts = small[:, 404:410]

    ps = nc.alloc_psum_tensor("ps", [P, 8, 512], F32)

    h_spill = nc.dram_tensor("h_spill", [P, NT, D], F32, kind="Internal").ap()

    names = """x_landed0 x_landed1 lnin_landed ret_landed nat_landed seg_landed vec_landed lb_landed ident_landed
    h0_spilled h0_back ln1_landed ln2_landed router_landed out_stored
    raw0 raw1 raw2 raw3 raw4 raw5 hi_done lo_done pe_used pair0 pair1
    dve_step act_step pool_step mv_ready rstd_ready h_ready h_turned aT_hi aT_lo
    ret_scores ret_decayed ret_out ret_copied nat_scores nat_masked nat_max nat_exp nat_p nat_turned nat_pT nat_out nat_y
    dif_scores dif_biased dif_max dif_exp dif_a dif_turned dif_aT dif_out dif_copied lam_sums lam_exps
    sig_ready f_ready logf_ready km_ready kc_turned kc_ready seg_sums seg_exp qk_ready hg_scores hg_off hg_masked hg_added
    hg_out hg_copied sq_mean rms_ready gate_mul y_ready y_turned yT_hi yT_lo br_ready br_read mul_ready mg_hi mg_lo bank_ready out_first
    lb_shift lb_exp z_ready out_read
    wr_hi wr_lo logits scores_expert scores_turned scores_ready comb_ready mask_ready ranks ranks_read h1s_hi h1s_lo wc_hi wc_lo ident_ready over_ready
    sh_gate_up sh_silu sh_hid sh_turned sh_hi sh_lo sh_down
    places_compared sel_ready gathered gather_hi gather_lo weights_summed parts_ready cw_step cw_ready slots_turned selT_ready
    pair_silu pair_hid hid_hi hid_lo y_hi y_lo scattered
    fb_landed fb_split_hi fb_split_lo fb_gate_up fb_silu fb_hid fb_turned fb_hi fb_lo fb_down""".split()
    S = {n: nc.alloc_semaphore(n) for n in names}
    raw_landed = [S["raw0"], S["raw1"], S["raw2"], S["raw3"], S["raw4"], S["raw5"]]
    pair_free = [S["pair0"], S["pair1"]]
    x_landed = [S["x_landed0"], S["x_landed1"]]

    def raw_slot(n):
        return n % 3 if n < NM else (n - NM + 1) % 6

    mixer_loads = [sum(1 for n in range(NM) if n % 3 == s) if s < 3 else 0 for s in range(6)]

    def raw_count(n):
        if n < NM:
            return 32 * (n // 3 + 1)
        s = raw_slot(n)
        return 32 * (mixer_loads[s] + (n - NM + 1) // 6 + (s > 0))

    def raw(slot):
        return rawL[:, slot] if slot < 3 else rawH[:, slot - 3]

    def dram(ap, offset, dims):
        return bass.AP(ap.tensor, offset, dims)

    w_in, w_gate, w_out = A["w_in"], A["w_gate"], A["w_out"]
    IN_W = w_in.shape[-1]

    def mixer_sources(n):
        if n < N_PROJ:
            blk, half = n // 2, n % 2
            if blk < len(W_IN_ORDER):
                src, width, col = w_in, IN_W, 512 * W_IN_ORDER[blk]
            else:
                src, width, col = w_gate, 4 * D, 512 * (blk - len(W_IN_ORDER))
            return [(k * 512, 1024, dram(src, (4 * half + k) * width + col, [[KD * width, P], [width, 2], [1, 512]]))
                    for k in (0, 2)]
        if n < N_PROJ + N_BR:
            b = n - N_PROJ
            src = A[("w_br_ret", "w_br_nat", "w_br_hgrn", "w_br_diff", "w_br_diff")[b]]
            base = 256 * D if b == 4 else 0
            return [(j * D, D, dram(src, base + j * D, [[2 * D, P], [1, D]])) for j in range(2)]
        c = n - N_PROJ - N_BR
        return [(k * D, D, dram(w_out, (2 * c + k) * P * D, [[D, P], [1, D]])) for k in range(2)]

    def slot_view(slot, o, w, src):
        v = raw(slot)[:, o:o + w]
        return v.rearrange("p (a b) -> p a b", a=2) if len(src.shape) == 3 else v

    def step_chunk(q, v):
        return q * 6 + (NM + 1 + v)

    def step_slot(v):
        return raw_slot(NM + 1 + v)

    def split_slot(v):
        return (NM + 1 + v) % 3

    def if_over(eng):
        eng.wait_ge(S["over_ready"], 1)
        return eng.If(eng.value_load(over[0:1, 0:1], min_val=0, max_val=1) > 0)

    def add_level(pool, lv):
        pool.wait_ge(S["hg_masked"], 2 * lv)
        nc.gpsimd.tensor_tensor(accS[:].rearrange("p a x h i -> p (a x h i)"), accS[:].rearrange("p a x h i -> p (a x h i)"),
                                tmpS[:].rearrange("p a x h i -> p (a x h i)"), ALU.add).then_inc(S["hg_added"], 1)
        pool.wait_ge(S["hg_added"], lv - 1)

    ctx = ExitStack()
    block = ctx.enter_context(nc.Block())

    @block.sync
    def _(sp):
        for t in range(NT):
            sp.dma_start(xin[:, t], A["x"][0, t * P:(t + 1) * P, :]).then_inc(x_landed[t], 16)
        for n in range(NM):
            if n >= 3:
                sp.wait_ge(S["lo_done"], n - 2)
            for o, w, src in mixer_sources(n):
                sp.dma_start(slot_view(n % 3, o, w, src), src).then_inc(raw_landed[n % 3], 16)
            if n == 1:
                sp.wait_ge(S["h_ready"], NT)
                sp.dma_start(h_spill, h0[:]).then_inc(S["h0_spilled"], 16)
            if n == NM - 1:
                sp.wait_ge(S["h0_spilled"], 16)
                sp.wait_ge(S["mul_ready"], 16)
                sp.dma_start(h0b[:], h_spill).then_inc(S["h0_back"], 16)
                sp.dma_start(wr[:], dram(A["w_router"], 0, [[KD * 64, P], [64, KD], [1, 64]])).then_inc(S["router_landed"], 16)
                sp.dma_start(rbb[:], dram(A["router_bias"], 0, [[0, P], [1, 64]])).then_inc(S["router_landed"], 16)
                sp.dma_start(tri[:], A["c_tri"]).then_inc(S["router_landed"], 16)
                sp.dma_start(slot_no[:], A["c_slot"]).then_inc(S["router_landed"], 16)
                sp.dma_start(up_ones[:], A["c_up"]).then_inc(S["router_landed"], 16)
                for j, v in enumerate(("ln1_g", "ln1_b")):
                    sp.dma_start(ln1b[:, j], dram(A[v], 0, [[0, P], [1, D]])).then_inc(S["ln1_landed"], 16)

        def expert(w, e):
            return w[0, e] if isinstance(e, int) else w[0, bass.ds(e, 1)].rearrange("a r c -> (a r) c")

        def load_gate_up(gate, up, half, slot, landed):
            v = raw(slot).rearrange("p (k c) -> p k c", k=4)
            for j, src in enumerate((gate, up)):
                sv = src.rearrange("(p k) c -> p k c", k=KD)[:, 4 * half:4 * half + 4, :]
                sp.dma_start(v[:, :, j * HID:(j + 1) * HID], sv).then_inc(landed, 16)

        def load_down(src, slot, landed):
            sv = src.rearrange("(p j) c -> p j c", j=2)
            v = raw(slot).rearrange("p (j c) -> p j c", j=2)
            for j in range(2):
                sp.dma_start(v[:, j], sv[:, j]).then_inc(landed, 16)

        def load_chunk(q, v, kind, e):
            sp.wait_ge(S["lo_done"], step_chunk(q, v) - 5)
            slot = step_slot(v)
            if kind is None:
                load_down(expert(A["w_e_down"], e), slot, raw_landed[slot])
            else:
                load_gate_up(expert(A["w_e_gate"], e), expert(A["w_e_up"], e), kind, slot, raw_landed[slot])

        sp.wait_ge(S["lo_done"], NM - 1)
        for half in range(2):
            slot = raw_slot(NM + half)
            load_gate_up(A["w_s_gate"][0], A["w_s_up"][0], half, slot, raw_landed[slot])
        sp.wait_ge(S["lo_done"], NM)
        load_down(A["w_s_down"][0], raw_slot(NM + 2), raw_landed[raw_slot(NM + 2)])
        for v in range(2, 6):
            load_chunk(0, v, v % 2, v // 2 - 1)
        with sp.Fori(1, PAIRS) as q:
            for v, kind, e in ((0, 0, 0), (1, 1, 0), (2, None, -2), (3, None, -1), (4, 0, 1), (5, 1, 1)):
                load_chunk(q, v, kind, q * 2 + e)
        for v in range(2):
            load_chunk(PAIRS, v, None, 2 * (PAIRS - 1) + v)
        sp.wait_ge(S["h_ready"], 2 * NT)
        for j, v in enumerate(("ln2_g", "ln2_b")):
            sp.dma_start(ln2b[:, j], dram(A[v], 0, [[0, P], [1, D]])).then_inc(S["ln2_landed"], 16)
        with if_over(sp):
            with sp.Fori(0, N_EXPERTS) as e:
                sp.wait_ge(S["fb_down"], e + 1)
                for half in range(2):
                    load_gate_up(expert(A["w_e_gate"], e), expert(A["w_e_up"], e), half, half, S["fb_landed"])
                load_down(expert(A["w_e_down"], e), 2, S["fb_landed"])
        for t in range(NT):
            sp.wait_ge(S["z_ready"], t + 1)
            sp.dma_start(out[0, t * P:(t + 1) * P, :], outb[:, t]).then_inc(S["out_stored"], 16)
        sp.wait_ge(S["out_stored"], 16 * NT)
        sp.wait_ge(S["h0_spilled"], 16)

    @block.tensor
    def _(pe):
        mm = nc.tensor.matmul

        def split_part(part, slot):
            return (whi if part == 0 else wlo)[:, slot]

        def project(n):
            blk, half = n // 2, n % 2
            pair, slot = blk % 2, n % 3
            if half == 0 and blk >= 2:
                pe.wait_ge(pair_free[pair], 2 * (blk // 2))
            pe.wait_ge(S["lo_done"], n + 1)
            wv = [split_part(i, slot).rearrange("p (k c) -> p k c", k=4) for i in range(2)]
            b = W_IN_ORDER[blk] if blk < len(W_IN_ORDER) else 99
            seen = set()

            def token_major(bank, off, t, c0, width):
                for k in range(4):
                    for a, w in PASSES:
                        first = half == 0 and bank not in seen
                        seen.add(bank)
                        last = mm(ps[:, bank, off:off + width], aT[:, a, 4 * half + k, t * P:(t + 1) * P],
                                  wv[w][:, k, c0:c0 + width], start=first,
                                  stop=half == 1 and k == 3 and (a, w) == PASSES[-1], skip_group_check=True)
                return last

            def channel_major(bank, off, c0):
                for k in range(4):
                    for a, w in PASSES:
                        first = half == 0 and bank not in seen
                        seen.add(bank)
                        last = mm(ps[:, bank, off:off + TOKENS], wv[w][:, k, c0:c0 + P], aT[:, a, 4 * half + k, :],
                                  start=first, stop=half == 1 and k == 3 and (a, w) == PASSES[-1],
                                  skip_group_check=True)
                return last

            if b in (1, 4, 5, 8):
                for t in range(NT):
                    last = token_major(2 * pair + t, 0, t, 0, 512)
            elif b == 3:
                for t in range(NT):
                    last = token_major(2 * pair, 256 * t, t, 0, 256)
                for c in range(2):
                    last = channel_major(2 * pair + 1, 256 * c, 256 + P * c)
            else:
                for c in range(4):
                    last = channel_major(2 * pair + c // 2, 256 * (c % 2), P * c)
            last.then_inc(S["pe_used"], 1)

        def head(t, h):
            return t[64 * (h % 2):64 * (h % 2) + 64, h // 2]

        def turn(src, first_sem, done, count):
            for t in range(NT):
                pe.wait_ge(first_sem, count + t + 1)
                for k in range(KD):
                    last = nc.tensor.transpose(ps[:, 4 + 2 * t + k // 4, (k % 4) * P:(k % 4 + 1) * P],
                                               src[:, t, k::KD], ident[:])
                last.then_inc(done, 1)

        def ret_scores():
            pe.wait_ge(pair_free[0], 2)
            pe.wait_ge(S["aT_lo"], NT)
            for h in range(HEADS):
                q, k = head(rqk, h), rqk[64 * (h % 2):64 * (h % 2) + 64, 2 + h // 2]
                for j in range(NT):
                    last = mm(ps[:, 4 + h, j * TOKENS:(j + 1) * TOKENS], k[:, j * P:(j + 1) * P], q, start=True, stop=True)
                last.then_inc(S["ret_scores"], 1)

        def ret_out():
            pe.wait_ge(S["ret_decayed"], HEADS)
            pe.wait_ge(pair_free[1], 2)
            for h in range(HEADS):
                for i in range(NT):
                    for j in range(NT):
                        last = mm(ps[:, 4, i * 256 + h * 64:i * 256 + h * 64 + 64], retS[:, h, j, i * P:(i + 1) * P],
                                  rv[:, j, h * 64:h * 64 + 64], start=j == 0, stop=j == NT - 1)
            last.then_inc(S["ret_out"], 1)

        def nat_scores(h):
            bank = 5 + h % 2
            if h == 0:
                pe.wait_ge(pair_free[0], 4)
                pe.wait_ge(S["nat_landed"], 80)
            if h < 2:
                pe.wait_ge(S["ret_decayed"], HEADS)
            else:
                pe.wait_ge(S["nat_masked"], h - 1)
            q, k = head(nqk, h), nqk[64 * (h % 2):64 * (h % 2) + 64, 2 + h // 2]
            rows = slice(64 * (h % 2), 64 * (h % 2) + 64)
            for i in range(NT):
                o = i * TOKENS
                for r in range(2):
                    row = 2 * i + r
                    mm(ps[64 * r:64 * r + 64, bank, o:o + TOKENS], rev[rows], hk[rows, h, 3 - row:7 - row, :],
                       start=True, stop=False)
                    last = mm(ps[64 * r:64 * r + 64, bank, o:o + TOKENS], q[:, row * 64:row * 64 + 64], k,
                              start=False, stop=True)
            last.then_inc(S["nat_scores"], 1)

        def turn_probs(src, h, bank, done):
            for i in range(NT):
                for j in range(NT):
                    last = nc.tensor.transpose(ps[:, bank, j * TOKENS + i * P:j * TOKENS + i * P + P],
                                               src[:, h, i, j * P:(j + 1) * P], ident[:])
            last.then_inc(done, 1)

        def nat_turn(h):
            pe.wait_ge(S["nat_p"], h + 1)
            if h == 0:
                pe.wait_ge(S["ret_copied"], 1)
            if h >= 2:
                pe.wait_ge(S["nat_pT"], h - 1)
            turn_probs(pp, h, 7 if h % 2 == 0 else 4, S["nat_turned"])

        def nat_out():
            pe.wait_ge(S["nat_pT"], HEADS)
            pe.wait_ge(pair_free[1], 4)
            pe.wait_ge(S["nat_masked"], HEADS)
            for h in range(HEADS):
                for i in range(NT):
                    for j in range(NT):
                        last = mm(ps[:, 5, i * 256 + h * 64:i * 256 + h * 64 + 64], ppT[:, h, j, i * P:(i + 1) * P],
                                  nv[:, j, h * 64:h * 64 + 64], start=j == 0, stop=j == NT - 1)
            last.then_inc(S["nat_out"], 1)

        def dif_scores(h):
            b0 = 6 if h == 0 else 4
            if h == 0:
                pe.wait_ge(pair_free[0], 6)
                pe.wait_ge(pair_free[1], 6)
                pe.wait_ge(S["nat_masked"], HEADS)
                pe.wait_ge(S["nat_pT"], HEADS)
            elif h == 1:
                pe.wait_ge(S["nat_y"], 1)
            else:
                pe.wait_ge(S["dif_biased"], 2 * h)
            for s in range(2):
                for i in range(NT):
                    last = mm(ps[:, b0 + s, i * TOKENS:(i + 1) * TOKENS], dqT[64 * s:64 * s + 64, h, i * P:(i + 1) * P],
                              dkT[64 * s:64 * s + 64, h, :], start=True, stop=True)
            last.then_inc(S["dif_scores"], 1)

        def dif_turn(h):
            pe.wait_ge(S["dif_a"], h + 1)
            if h >= 2:
                pe.wait_ge(S["dif_aT"], h - 1)
            turn_probs(pp, h, 6 + h % 2, S["dif_turned"])

        def dif_out():
            pe.wait_ge(S["dif_aT"], HEADS)
            pe.wait_ge(S["dif_biased"], 2 * HEADS)
            pe.wait_ge(pair_free[0], 8)
            for i in range(NT):
                for h in range(HEADS):
                    for j in range(NT):
                        last = mm(ps[:, 4 + i, h * P:(h + 1) * P], ppT[:, h, j, i * P:(i + 1) * P],
                                  dv[:, j, h * P:(h + 1) * P], start=j == 0, stop=j == NT - 1)
            last.then_inc(S["dif_out"], 1)

        def kc_turn():
            pe.wait_ge(S["km_ready"], 1)
            pe.wait_ge(S["dif_aT"], HEADS)
            for d in range(2):
                for c in range(2):
                    for t in range(NT):
                        last = nc.tensor.transpose(ps[:, 6 + d, c * TOKENS + t * P:c * TOKENS + t * P + P],
                                                   kTM[:, t, d * 256 + c * P:d * 256 + c * P + P], ident[:])
            last.then_inc(S["kc_turned"], 1)

        def seg_sums(lv):
            if lv == 0:
                pe.wait_ge(S["seg_landed"], 48)
                pe.wait_ge(S["logf_ready"], NT)
                pe.wait_ge(S["dif_copied"], NT)
            else:
                pe.wait_ge(S["seg_exp"], 2 * lv)
            for d in range(2):
                for c in range(2):
                    for t in range(NT):
                        last = mm(ps[:, 4 + d, c * TOKENS + t * P:c * TOKENS + t * P + P],
                                  logf[:, t, d * 256 + c * P:d * 256 + c * P + P],
                                  seg0[:, d, t] if lv == 0 else seg[:, d, lv - 1], start=True, stop=True)
            last.then_inc(S["seg_sums"], 1)

        def hg_scores(lv):
            pe.wait_ge(S["qk_ready"], lv + 1)
            if lv == 0:
                pe.wait_ge(S["kc_ready"], 2)
            elif lv == 1:
                pe.wait_ge(S["hg_off"], 2)
            else:
                pe.wait_ge(S["hg_masked"], 2 * (lv - 1))
            for x in range(2):
                ti = 1 - x if lv == 0 else x
                for h in range(HEADS):
                    o = (2 * x + h // 2) * P
                    dst = ps[:, 6 + h % 2, o:o + P]
                    rows = slice(64 * (h % 2), 64 * (h % 2) + 64)
                    kk, qq = slice(x * P, (x + 1) * P), slice(ti * P, (ti + 1) * P)
                    q = hq[rows, h // 2, qq] if lv == DIAG else Qb[rows, lv % 2, h // 2, qq]
                    last = mm(dst, Kb[rows, lv % 2, h // 2, kk], q, start=True, stop=True)
            last.then_inc(S["hg_scores"], 1)

        def hg_out():
            pe.wait_ge(S["hg_added"], LEVELS - 2)
            pe.wait_ge(S["seg_exp"], 2 * DIAG)
            for h in range(HEADS):
                for i in range(NT):
                    for j in range(NT):
                        s = (accS if i == j else offd)[:, h % 2, j, h // 2]
                        last = mm(ps[:, 4, i * 256 + h * 64:i * 256 + h * 64 + 64], s, hv[:, j, h * 64:h * 64 + 64],
                                  start=j == 0, stop=j == NT - 1)
            last.then_inc(S["hg_out"], 1)

        after = {
            2: [ret_scores], 4: [ret_out], 6: [lambda: nat_scores(0), lambda: nat_scores(1)],
            8: [lambda: nat_turn(0), lambda: nat_turn(1)], 9: [lambda: nat_scores(2), lambda: nat_scores(3)],
            11: [lambda: nat_turn(2), lambda: nat_turn(3)], 12: [nat_out],
            14: [lambda: dif_scores(0)], 15: [lambda: dif_scores(1)], 16: [lambda: dif_turn(0)],
            17: [lambda: dif_turn(1), lambda: dif_scores(2)], 18: [lambda: dif_turn(2)], 19: [lambda: dif_scores(3)],
            20: [lambda: dif_turn(3)], 21: [dif_out], 22: [kc_turn, lambda: seg_sums(0)], 32: [hg_out],
        }
        pe.wait_ge(S["ident_landed"], 16)
        turn(h0, S["h_ready"], S["h_turned"], 0)
        pe.wait_ge(S["aT_lo"], NT)
        for n in range(N_PROJ):
            project(n)
            for task in after.get(n, ()):
                task()
            if 23 <= n < 23 + LEVELS:
                hg_scores(n - 23)
                if n - 22 < DIAG:
                    seg_sums(n - 22)

        for rnd in range(3):
            tiles = range(4 * rnd, min(4 * rnd + 4, 10))
            if rnd == 0:
                pe.wait_ge(S["y_ready"], 3)
                pe.wait_ge(S["nat_y"], 1)
                pe.wait_ge(S["hg_copied"], 1)
            if rnd == 2:
                pe.wait_ge(S["yT_lo"], 1)
            for q in tiles:
                for t in range(NT):
                    b0 = 4 + 2 * (rnd % 2)
                    last = nc.tensor.transpose(ps[:, b0 + (q % 4) // 2, (q % 2) * TOKENS + t * P:(q % 2) * TOKENS + t * P + P],
                                               y[:, t, 256 * (q // 2) + q % 2:256 * (q // 2) + 256:2], ident[:])
            last.then_inc(S["y_turned"], 1)
        pe.wait_ge(S["yT_lo"], 3)
        for c in range(N_BR):
            n = N_PROJ + c
            b = min(c, 3)
            pe.wait_ge(S["lo_done"], n + 1)
            if c == 0:
                pe.wait_ge(pair_free[0], 2 * ((NB + 1) // 2))
                pe.wait_ge(pair_free[1], 2 * (NB // 2))
            elif 2 <= c <= 3:
                pe.wait_ge(S["mul_ready"], 4 * (c - 1))
            wv = [split_part(i, n % 3).rearrange("p (j c) -> p j c", j=2) for i in range(2)]
            for dt in range(KD):
                bank = 4 * (b % 2) + dt // 2
                for j in range(2):
                    for a, w in PASSES:
                        last = mm(ps[:, bank, (dt % 2) * TOKENS:(dt % 2 + 1) * TOKENS], wv[w][:, j, dt * P:(dt + 1) * P],
                                  yT[:, a, 2 * c + j, :], start=c != 4 and dt % 2 == 0 and j == 0 and (a, w) == PASSES[0],
                                  stop=c != 3 and j == 1 and (a, w) == PASSES[-1], skip_group_check=True)
                if c == 4 and dt in (1, 3, 5):
                    last.then_inc(S["bank_ready"], 1)
            last.then_inc(S["pe_used"], 1)
        for c in range(N_OUT):
            n = N_PROJ + N_BR + c
            pe.wait_ge(S["lo_done"], n + 1)
            pe.wait_ge(S["mg_lo"], c + 1)
            wv = [split_part(i, n % 3).rearrange("p (k c) -> p k c", k=2) for i in range(2)]
            for t in range(NT):
                for half in range(2):
                    for k in range(2):
                        for a, w in PASSES:
                            last = mm(ps[:, 2 * t + half, :], aT[:, a, 2 * c + k, t * P:(t + 1) * P],
                                      wv[w][:, k, half * 512:(half + 1) * 512],
                                      start=c == 0 and k == 0 and (a, w) == PASSES[0],
                                      stop=c == N_OUT - 1 and k == 1 and (a, w) == PASSES[-1], skip_group_check=True)
                if c == N_OUT - 1 and t == 0:
                    last.then_inc(S["out_first"], 1)
            last.then_inc(S["pe_used"], 1)

        turn(zz, S["h_ready"], S["h_turned"], NT)
        pe.wait_ge(S["aT_lo"], 2 * NT)
        pe.wait_ge(S["wr_lo"], 1)
        for k in range(KD):
            for a, w in PASSES:
                last = mm(ps[0:64, 6, 0:TOKENS], wrs[:, w, k, :], aT[:, a, k, :],
                          start=k == 0 and (a, w) == PASSES[0], stop=k == KD - 1 and (a, w) == PASSES[-1])
        last.then_inc(S["logits"], 1)

        def gate_up(bank, lhs, half, slot):
            for k in range(4):
                for a, w in PASSES:
                    wv = split_part(w, slot).rearrange("p (k c) -> p k c", k=4)
                    last = mm(ps[:, bank, :], lhs(a, 4 * half + k), wv[:, k, :],
                              start=half == 0 and k == 0 and (a, w) == PASSES[0],
                              stop=half == 1 and k == 3 and (a, w) == PASSES[-1], skip_group_check=True)
            return last

        def dense_gate_up(t, half, slot):
            return gate_up(4 + t, lambda a, k: aT[:, a, k, t * P:(t + 1) * P], half, slot)

        def dense_turn(hid_done, done, count):
            for t in range(NT):
                pe.wait_ge(hid_done, count * 2 + t - 1)
                for j in range(2):
                    last = nc.tensor.transpose(ps[:, 6 + t, j * P:(j + 1) * P], hid[:, t, j::2], ident[:])
                last.then_inc(done, 1)

        def dense_down(slot, first):
            for t in range(NT):
                for half in range(2):
                    for j in range(2):
                        for a, w in PASSES:
                            wv = split_part(w, slot).rearrange("p (j c) -> p j c", j=2)
                            last = mm(ps[:, 2 * t + half, :], hTs[:, a, t, j, :], wv[:, j, half * 512:(half + 1) * 512],
                                      start=first and j == 0 and (a, w) == PASSES[0],
                                      stop=j == 1 and (a, w) == PASSES[-1], skip_group_check=True)
            return last

        for half in range(2):
            pe.wait_ge(S["lo_done"], NM + half + 1)
            for t in range(NT):
                last = dense_gate_up(t, half, (NM + half) % 3)
            last.then_inc(S["pe_used"], 1)
            if half == 0:
                pe.wait_ge(S["scores_expert"], 1)
                for t in range(NT):
                    last = nc.tensor.transpose(ps[:, 6, 256 + t * 64:320 + t * 64], scT[0:64, t * P:(t + 1) * P], ident[0:64, 0:64])
                last.then_inc(S["scores_turned"], 1)
        pe.wait_ge(S["mask_ready"], 1)
        pe.wait_ge(S["out_read"], NT)
        pe.wait_ge(S["router_landed"], 80)
        msk0, msk1 = tk[:, 640:704], tk[:, 704:768]
        up, ones = up_ones[:, 0], up_ones[:, 1]
        mm(ps[:, 0, 0:64], up, msk0, start=True, stop=True)
        mm(ps[:, 0, 64:128], ones, msk0, start=True, stop=False)
        mm(ps[:, 0, 64:128], up, msk1, start=False, stop=True)
        mm(ps[:, 0, 128:192], ones, msk0, start=True, stop=False)
        mm(ps[:, 0, 128:192], ones, msk1, start=False, stop=True).then_inc(S["ranks"], 1)
        pe.wait_ge(S["scores_ready"], 1)
        dense_turn(S["sh_hid"], S["sh_turned"], 1)
        pe.wait_ge(S["sh_lo"], NT)
        pe.wait_ge(S["lo_done"], NM + 3)
        pe.wait_ge(S["ranks_read"], 1)
        dense_down((NM + 2) % 3, first=True).then_inc(S["pe_used"], 1)

        def gather(q, piece, parity):
            a, k0 = piece % 2, 4 * (piece // 2)
            for k in range(4):
                for t in range(NT):
                    last = mm(ps[:, (4, 6, 7, 6)[piece], k * P:(k + 1) * P], h1s[:, a, t, k0 + k::KD], sel[:, parity, t],
                              start=t == 0, stop=t == NT - 1)
            last.then_inc(S["gathered"], 1)

        def turn_hidden(e, bank):
            for j in range(2):
                last = nc.tensor.transpose(ps[:, bank, j * P:(j + 1) * P], hid[:, e, j::2], ident[:])
            return last

        def sum_weights(q, parity):
            for t in range(NT):
                w = wc[:, t].rearrange("p q c -> p (q c)")
                w = w[:, 0:6] if isinstance(q, int) and q == 0 else w[:, bass.ds(q * 6, 6)]
                last = mm(ps[:, 5, 256:262], sel[:, parity, t], w, start=t == 0, stop=t == NT - 1)
            last.then_inc(S["weights_summed"], 1)

        def scatter(parity):
            for t in range(NT):
                for half in range(2):
                    for a in range(2):
                        last = mm(ps[:, 2 * t + half, :], selT[:, parity, t], ys[:, a, half * 512:(half + 1) * 512],
                                  start=False, stop=a == 1, skip_group_check=True)
            last.then_inc(S["scattered"], 1)

        def half_gate_up(q, v, bank, half, parity):
            pe.wait_ge(S["lo_done"], step_chunk(q, v) + 1)
            gate_up(bank, lambda a, k: xg[parity][:, a, k, :], half, split_slot(v)).then_inc(S["pe_used"], 1)

        def down(q, v0):
            for e in range(2):
                pe.wait_ge(S["hid_lo"], q * 2 + (e - 1))
                pe.wait_ge(S["lo_done"], step_chunk(q, v0 + e) + 1)
                wv = [split_part(i, split_slot(v0 + e)).rearrange("p (j c) -> p j c", j=2) for i in range(2)]
                for half in range(2):
                    for j in range(2):
                        for a, w in PASSES:
                            last = mm(ps[:, 6 + half, :], hTs[:, a, e, j, :], wv[w][:, j, half * 512:(half + 1) * 512],
                                      start=e == 0 and j == 0 and (a, w) == PASSES[0],
                                      stop=e == 1 and j == 1 and (a, w) == PASSES[-1], skip_group_check=True)
                last.then_inc(S["pe_used"], 1)

        def pair_step(q, parity, first=False, final=False):
            a1 = 2 if first else 0
            pe.wait_ge(S["gather_hi"], q * 2 + 1)
            pe.wait_ge(S["gather_lo"], q * 2 + 1)
            half_gate_up(q, a1, 4, 0, parity)
            if not first:
                pe.wait_ge(S["pair_hid"], q * 2)
                turn_hidden(1, 5)
            else:
                pe.wait_ge(S["wc_lo"], 1)
            sum_weights(q, parity)
            pe.wait_ge(S["gather_hi"], q * 2 + 2)
            pe.wait_ge(S["gather_lo"], q * 2 + 2)
            half_gate_up(q, a1 + 1, 4, 1, parity)
            if not first:
                down(q, 2)
            pe.wait_ge(S["pair_hid"], q * 2 + 1)
            turn_hidden(0, 4)
            for t in range(NT):
                last = mm(ps[:, 4, 256 + t * P:256 + (t + 1) * P], sel[:, parity, t], ident_r[:], start=True, stop=True)
            last.then_inc(S["slots_turned"], 1)
            pe.wait_ge(S["parts_ready"], q + 1)
            half_gate_up(q, 4, 5, 0, parity)
            if not final:
                pe.wait_ge(S["sel_ready"], q + 2)
                pe.wait_ge(S["hid_lo"], q * 2 + 1)
                pe.wait_ge(S["selT_ready"], q + 1)
                gather(q + 1, 0, 1 - parity)
                if not first:
                    pe.wait_ge(S["y_lo"], q * 2 - 1)
                gather(q + 1, 1, 1 - parity)
            half_gate_up(q, 5, 5, 1, parity)
            if not final:
                if not first:
                    pe.wait_ge(S["y_lo"], q * 2)
                gather(q + 1, 2, 1 - parity)
                pe.wait_ge(S["gather_lo"], q * 2 + 3)
                gather(q + 1, 3, 1 - parity)
            if not first:
                pe.wait_ge(S["y_lo"], q * 2)
                pe.wait_ge(S["selT_ready"], q)
                scatter(1 - parity)

        pe.wait_ge(S["sel_ready"], 1)
        pe.wait_ge(S["ident_ready"], 1)
        pe.wait_ge(S["h1s_lo"], 1)
        pe.wait_ge(S["sh_hid"], NT)
        pe.wait_ge(S["sh_lo"], NT)
        for piece in range(4):
            if piece == 3:
                pe.wait_ge(S["gather_lo"], 1)
            gather(0, piece, 0)

        pair_step(0, 0, first=True)
        with pe.Fori(0, (PAIRS - 2) // 2) as i:
            for u in range(2):
                pair_step(i * 2 + (1 + u), (1 + u) % 2)
        pair_step(PAIRS - 1, (PAIRS - 1) % 2, final=True)
        pe.wait_ge(S["pair_hid"], 2 * PAIRS)
        turn_hidden(1, 5).then_inc(S["weights_summed"], 1)
        pe.wait_ge(S["y_lo"], 2 * PAIRS - 2)
        down(PAIRS, 0)
        pe.wait_ge(S["y_lo"], 2 * PAIRS)
        pe.wait_ge(S["selT_ready"], PAIRS)
        scatter((PAIRS - 1) % 2)

        with if_over(pe):
            with pe.Fori(0, N_EXPERTS) as e:
                pe.wait_ge(S["fb_split_lo"], e + 1)
                for half in range(2):
                    for t in range(NT):
                        last = dense_gate_up(t, half, half)
                last.then_inc(S["fb_gate_up"], 1)
                dense_turn(S["fb_hid"], S["fb_turned"], e + 1)
                pe.wait_ge(S["fb_lo"], e * 2 + 2)
                dense_down(2, first=False).then_inc(S["fb_down"], 1)

    @block.scalar
    def _(act):
        one = Steps(act, S["act_step"])
        A_ = nc.scalar.activation

        act.dma_start(ident[:], A["c_ident"]).then_inc(S["ident_landed"], 16)
        for j, v in enumerate(("ln_in_g", "ln_in_b")):
            act.dma_start(lnb[:, j], dram(A[v], 0, [[0, P], [1, D]])).then_inc(S["lnin_landed"], 16)
        act.dma_start(retM[:], A["c_ret"]).then_inc(S["ret_landed"], 16)
        for dst, src in ((lamv[:], dram(A["diff_lambda"], 0, [[0, P], [1, 256]])),
                         (gnr[:], dram(A["ret_gn"], 0, [[0, P], [1, 256]])),
                         (gnh[:], dram(A["hgrn_gn"], 0, [[0, P], [1, 256]])),
                         (gnd[:], dram(A["diff_subln"], 0, [[0, P], [1, 512]])),
                         (bg[:], A["b_gate"])):
            act.dma_start(dst, src).then_inc(S["vec_landed"], 16)
        act.dma_start(seg[:], A["c_seg"]).then_inc(S["seg_landed"], 16)
        act.dma_start(seg0[:], A["c_seg0"]).then_inc(S["seg_landed"], 16)
        act.dma_start(msk[:], A["c_mask"]).then_inc(S["seg_landed"], 16)
        act.dma_start(dist[:], A["c_dist"]).then_inc(S["nat_landed"], 16)
        act.dma_start(natm[:], A["c_nat"]).then_inc(S["nat_landed"], 16)
        act.dma_start(rev[:], A["c_rev"]).then_inc(S["nat_landed"], 16)

        def high(n, rslot, slot, landed):
            act.wait_ge(raw_landed[rslot], landed)
            if not isinstance(n, int) or n >= 3:
                act.wait_ge(S["pe_used"], n - 2)
            nc.scalar.copy(whi[:, slot], raw(rslot)).then_inc(S["hi_done"], 1)

        def high_m(n):
            if n < NM:
                high(n, raw_slot(n), n % 3, raw_count(n))

        def high_turned(count):
            for t in range(NT):
                act.wait_ge(S["h_turned"], count + t + 1)
                if count:
                    act.wait_ge(S["pe_used"], NM)
                for b in range(2):
                    last = nc.scalar.copy(aT[:, 0, 4 * b:4 * b + 4, t * P:(t + 1) * P],
                                          ps[:, 4 + 2 * t + b, :].rearrange("p (k c) -> p k c", k=4))
                last.then_inc(S["aT_hi"], 1)

        def tm(bank):
            return ps[:, bank, :]

        def evacuate(blk):
            pair = blk % 2
            b0, free = 2 * pair, pair_free[pair]
            b = W_IN_ORDER[blk] if blk < len(W_IN_ORDER) else 100 + blk - len(W_IN_ORDER)
            if b in (0, 2, 6, 7):
                return
            act.wait_ge(S["pe_used"], 2 * blk + 2)
            if b == 1:
                for t in range(NT):
                    nc.scalar.copy(rv[:, t], ps[:, b0 + t, 0:256])
                    A_(rg[:, t], ps[:, b0 + t, 256:512], ACT.Silu).then_inc(free, 1)
            elif b == 3:
                nc.scalar.copy(nv[:].rearrange("p t c -> p (t c)"), tm(b0)).then_inc(free, 1)
                A_(hq[:].rearrange("p t c -> p (t c)"), tm(b0 + 1), ACT.Silu).then_inc(free, 1)
            elif b == 8:
                for t in range(NT):
                    nc.scalar.copy(dv[:, t], tm(b0 + t)).then_inc(free, 1)
            elif b == 4:
                for t in range(NT):
                    A_(kTM[:, t], tm(b0 + t), ACT.Sigmoid, scale=-1.0)
                    A_(logf[:, t], tm(b0 + t), ACT.Sigmoid).then_inc(free, 1)
            elif b == 5:
                for t in range(NT):
                    nc.scalar.copy(hv[:, t], ps[:, b0 + t, 0:256])
                    A_(hg[:, t], ps[:, b0 + t, 256:512], ACT.Silu).then_inc(free, 1)
            elif b >= 100:
                q = b - 100
                if q == 0:
                    act.wait_ge(S["km_ready"], 1)
                if q == 4:
                    act.wait_ge(S["dif_out"], 1)
                dst = (g0 if q < 4 else g1)
                for c in range(4):
                    ins = A_(dst[:, q % 4, c], ps[:, b0 + c // 2, (c % 2) * TOKENS:(c % 2 + 1) * TOKENS], ACT.Sigmoid,
                             bias=bg[:, 4 * q + c:4 * q + c + 1])
                    if c % 2 == 1:
                        ins.then_inc(free, 1)

        def copy_bank(dst, bank, wait, count, sem):
            act.wait_ge(wait, count)
            nc.scalar.copy(dst, ps[:, bank, :]).then_inc(sem, 1)

        def ret_copy():
            copy_bank(oo[:, 0:512], 4, S["ret_out"], 1, S["ret_copied"])
            act.dma_start(lbv[:], dram(A["hgrn_lb"], 0, [[0, P], [1, 512]])).then_inc(S["lb_landed"], 16)

        def lower_exp():
            act.wait_ge(S["lb_shift"], 1)
            A_(lb[:], lb[:], ACT.Exp).then_inc(S["lb_exp"], 1)

        def nat_exp(h):
            act.wait_ge(S["nat_max"], h + 1)
            for i in range(NT):
                last = A_(pp[:, h, i], pp[:, h, i], ACT.Exp, bias=small[:, 2 * h + i:2 * h + i + 1],
                          accum_out=small[:, 8 + 2 * h + i:9 + 2 * h + i])
            last.then_inc(S["nat_exp"], 1)

        def nat_copy(h):
            copy_bank(ppT[:, h].rearrange("p j i -> p (j i)"), 7 if h % 2 == 0 else 4, S["nat_turned"], h + 1, S["nat_pT"])

        def nat_y():
            act.wait_ge(S["nat_out"], 1)
            nc.scalar.copy(y[:, :, 256:512], ps[:, 5, :].rearrange("p (t c) -> p t c", t=2)).then_inc(S["nat_y"], 1)

        def dif_exp(h):
            act.wait_ge(S["dif_max"], h + 1)
            for s in range(2):
                for i in range(NT):
                    c = 32 + 8 * h + 2 * s + i
                    last = A_(ee[:, h % 2, s, i], ee[:, h % 2, s, i], ACT.Exp, bias=small[:, c:c + 1],
                              accum_out=small[:, c + 4:c + 5])
            last.then_inc(S["dif_exp"], 1)

        def dif_copy(h):
            copy_bank(ppT[:, h].rearrange("p j i -> p (j i)"), 6 + h % 2, S["dif_turned"], h + 1, S["dif_aT"])

        def dif_o():
            act.wait_ge(S["dif_out"], 1)
            act.wait_ge(S["y_ready"], 1)
            for i in range(NT):
                nc.scalar.copy(oo[:, 512 * i:512 * i + 512], ps[:, 4 + i, :]).then_inc(S["dif_copied"], 1)

        def lam_exp():
            act.wait_ge(S["lam_sums"], 2)
            A_(small[:, 66:68], small[:, 64:66], ACT.Exp).then_inc(S["lam_exps"], 1)

        def log_f():
            for t in range(NT):
                act.wait_ge(S["f_ready"], t + 1)
                A_(logf[:, t], logf[:, t], ACT.Ln).then_inc(S["logf_ready"], 1)

        def kc_copy():
            act.wait_ge(S["kc_turned"], 1)
            for d in range(2):
                nc.scalar.copy(kc[:, d].rearrange("p c t -> p (c t)"), ps[:, 6 + d, :]).then_inc(S["kc_ready"], 1)

        def seg_exp(lv):
            if lv == 0:
                act.wait_ge(S["kc_ready"], 2)
                act.wait_ge(S["y_ready"], 2)
                act.wait_ge(S["kc_turned"], 1)
            if lv >= 2:
                act.wait_ge(S["qk_ready"], lv - 1)
            act.wait_ge(S["seg_sums"], lv + 1)
            for d in range(2):
                A_(Eb[:, lv % 2, d].rearrange("p c t -> p (c t)"), ps[:, 4 + d, :], ACT.Exp).then_inc(S["seg_exp"], 1)

        def hg_off():
            act.wait_ge(S["hg_scores"], 1)
            act.wait_ge(S["dif_out"], 1)
            for x in range(2):
                nc.scalar.copy(offd[:, x].rearrange("p x h i -> p (x h i)"), ps[:, 6 + x, :]).then_inc(S["hg_off"], 1)

        def hg_copy():
            act.wait_ge(S["qk_ready"], LEVELS)
            act.wait_ge(S["hg_out"], 1)
            nc.scalar.copy(oo[:, 0:512], ps[:, 4, :]).then_inc(S["hg_copied"], 1)

        after = {
            4: [ret_copy], 6: [lambda: nat_exp(0), lambda: nat_exp(1)], 8: [lambda: nat_copy(0), lambda: nat_copy(1)],
            9: [lambda: nat_exp(2), lambda: nat_exp(3)], 11: [lambda: nat_copy(2), lambda: nat_copy(3)],
            12: [nat_y, lam_exp, lower_exp], 14: [lambda: dif_exp(0)],
            15: [lambda: dif_exp(1)], 16: [lambda: dif_copy(0)], 17: [lambda: dif_copy(1), lambda: dif_exp(2)],
            18: [lambda: dif_copy(2), log_f], 19: [lambda: dif_exp(3)], 20: [lambda: dif_copy(3)], 21: [dif_o],
            22: [kc_copy, lambda: seg_exp(0)], 23: [hg_off], 32: [hg_copy],
        }
        high_m(0)
        high_turned(0)
        high_m(1)
        act.wait_ge(S["h_ready"], NT)
        for r in (0, 64):
            act.dma_start(hk[r:r + 64], dram(A["rpb"], 0, [[1, 64], [127, HEADS * 7], [1, 64]])).then_inc(S["nat_landed"], 16)
        for n in range(N_PROJ):
            high_m(n + 2)
            if n % 2 == 1:
                evacuate(n // 2)
            for task in after.get(n, ()):
                task()
            if 23 <= n < 23 + DIAG - 1:
                seg_exp(n - 22)

        def high_y(rnd):
            act.wait_ge(S["y_turned"], rnd + 1)
            nq = min(4, 10 - 4 * rnd)
            b0 = 4 + 2 * (rnd % 2)
            for b in range((nq + 1) // 2):
                last = nc.scalar.copy(yT[:, 0, 4 * rnd + 2 * b:4 * rnd + 2 * b + 2, :],
                                      ps[:, b0 + b, :].rearrange("p (q t) -> p q t", q=2))
            last.then_inc(S["yT_hi"], 1)

        for rnd in range(3):
            high_y(rnd)
        for n in range(N_PROJ + 2, NM):
            high_m(n)
            if n == N_PROJ + N_BR + 1:
                act.wait_ge(S["pe_used"], N_PROJ)
                for g in range(4):
                    act.wait_ge(S["br_read"], 9 + g)
                    nc.scalar.copy(aT[:, 0, 2 * g:2 * g + 2].rearrange("p k t -> p (k t)"),
                                   mg[:, 2 * g:2 * g + 2].rearrange("p k t -> p (k t)")).then_inc(S["mg_hi"], 1)
        act.wait_ge(S["router_landed"], 80)
        nc.scalar.copy(wrs[:, 0], wr[:]).then_inc(S["wr_hi"], 1)
        for n in range(NM, NM + 3):
            high(n, raw_slot(n), n % 3, raw_count(n))
        high_turned(NT)
        nc.scalar.copy(h1s[:, 0].rearrange("p t c -> p (t c)"), zz[:].rearrange("p t c -> p (t c)")).then_inc(S["h1s_hi"], 1)
        act.wait_ge(S["logits"], 1)
        A_(scT[0:64], ps[0:64, 6, 0:TOKENS], ACT.Sigmoid).then_inc(S["scores_expert"], 1)
        act.wait_ge(S["scores_turned"], 1)
        nc.scalar.copy(tk[:, 0:128], ps[:, 6, 256:384]).then_inc(S["scores_ready"], 1)

        def dense_silu(done, count):
            for t in range(NT):
                A_(sil[:, t], ps[:, 4 + t, 0:HID], ACT.Silu).then_inc(done, 1)

        def dense_high(turned, done, count):
            for t in range(NT):
                act.wait_ge(turned, count * 2 + t - 1)
                nc.scalar.copy(hTs[:, 0, t], ps[:, 6 + t, 0:256].rearrange("p (j c) -> p j c", j=2)).then_inc(done, 1)

        act.wait_ge(S["pe_used"], NM + 2)
        dense_silu(S["sh_silu"], 1)
        dense_high(S["sh_turned"], S["sh_hi"], 1)
        for n in range(NM + 3, NM + 5):
            high(n, raw_slot(n), n % 3, raw_count(n))
        act.wait_ge(S["comb_ready"], 1)
        nc.scalar.copy(wc[:, :, :, 0:2], comb[:].rearrange("p t (q e) -> p t q e", e=2)).then_inc(S["wc_hi"], 1)
        nc.scalar.copy(ident_r[:], ident[:]).then_inc(S["ident_ready"], 1)

        def gather_high(q, piece, parity):
            act.wait_ge(S["gathered"], q * 4 + (1 + piece))
            k0 = 4 * (piece // 2)
            nc.scalar.copy(xg[parity][:, 0, k0:k0 + 4, :].rearrange("p k s -> p (k s)"),
                           ps[:, (4, 6, 7, 6)[piece], :]).then_inc(S["gather_hi"], 1)

        def step_high(q, v):
            slot = step_slot(v)
            high(step_chunk(q, v), slot, split_slot(v), q * 32 + raw_count(NM + 1 + v))

        def hidden_high(q, e):
            act.wait_ge(S["weights_summed" if e else "slots_turned"], q + (1 + e))
            nc.scalar.copy(hTs[:, 0, e].rearrange("p j c -> p (j c)"), ps[:, 4 + e, 0:256]).then_inc(S["hid_hi"], 1)

        def outputs_high(used):
            act.wait_ge(S["pe_used"], used)
            for half in range(2):
                nc.scalar.copy(ys[:, 0, half * 512:(half + 1) * 512], ps[:, 6 + half, :]).then_inc(S["y_hi"], 1)

        def silu(q, e, used):
            act.wait_ge(S["pe_used"], used)
            A_(sil[:, e], ps[:, 4 + e, 0:HID], ACT.Silu).then_inc(S["pair_silu"], 1)

        def pair_step(q, parity, first=False):
            if not first:
                silu(q + (-1), 1, step_chunk(q, 0))
                gather_high(q, 2, parity)
                step_high(q, 2)
                act.wait_ge(S["cw_ready"], q)
            act.wait_ge(S["weights_summed"], q + 1)
            nc.scalar.copy(cw_parts, ps[:, 5, 256:262]).then_inc(S["parts_ready"], 1)
            if not first:
                hidden_high(q + (-1), 1)
                step_high(q, 3)
            else:
                step_high(q, 4)
            silu(q, 0, step_chunk(q, 4 if first else 2))
            if not first:
                step_high(q, 4)
            step_high(q, 5)
            if not first:
                outputs_high(step_chunk(q, 4))
            act.wait_ge(S["slots_turned"], q + 1)
            nc.scalar.copy(selT[:, parity].rearrange("p t c -> p (t c)"), ps[:, 4, 256:512]).then_inc(S["selT_ready"], 1)
            hidden_high(q, 0)
            step_high(q + 1, 0)

        def next_slots(q, parity):
            gather_high(q + 1, 0, 1 - parity)
            step_high(q + 1, 1)

        gather_high(0, 0, 0)
        gather_high(0, 2, 0)
        pair_step(0, 0, first=True)
        next_slots(0, 0)
        with act.Fori(0, (PAIRS - 2) // 2) as i:
            for u in range(2):
                pair_step(i * 2 + (1 + u), (1 + u) % 2)
                next_slots(i * 2 + (1 + u), (1 + u) % 2)
        pair_step(PAIRS - 1, (PAIRS - 1) % 2)
        step_high(PAIRS, 1)
        silu(PAIRS - 1, 1, step_chunk(PAIRS, 0))
        hidden_high(PAIRS - 1, 1)
        outputs_high(step_chunk(PAIRS, 2))

        with if_over(act):
            with act.Fori(0, N_EXPERTS) as e:
                act.wait_ge(S["fb_landed"], e * 96 + 96)
                for c in range(3):
                    last = nc.scalar.copy(whi[:, c], rawL[:, c])
                last.then_inc(S["fb_split_hi"], 1)
                act.wait_ge(S["fb_gate_up"], e + 1)
                dense_silu(S["fb_silu"], e + 1)
                dense_high(S["fb_turned"], S["fb_hi"], e + 1)

    @block.gpsimd
    def _(pool):
        nc.gpsimd.memset(pow_c[:], -0.5).then_inc(S["pool_step"], 1)
        pool.wait_ge(S["pool_step"], 1)
        norms = [0]

        def power(dst, src, w):
            norms[0] += 1
            pool.wait_ge(S["mv_ready"], norms[0])
            nc.gpsimd.tensor_tensor(dst, src, pow_c[:, 0:w], ALU.pow).then_inc(S["rstd_ready"], 1)

        power(small[:, 76:78], small[:, 74:76], 2)
        pool.wait_ge(S["vec_landed"], 80)
        pool.wait_ge(pair_free[1], 2)
        for t in range(NT):
            last = nc.gpsimd.tensor_tensor(rg[:, t], rg[:, t], gnr[:], ALU.mult)
        last.then_inc(S["gate_mul"], 1)
        power(small[:, 88:96], small[:, 80:88], 8)
        power(small[:, 88:96], small[:, 80:88], 8)
        pool.wait_ge(pair_free[0], 2 * 5)
        for t in range(NT):
            last = nc.gpsimd.tensor_tensor(hg[:, t], hg[:, t], gnh[:], ALU.mult)
        last.then_inc(S["gate_mul"], 1)
        for lv in range(2, DIAG + 1):
            add_level(pool, lv)
        power(small[:, 88:96], small[:, 80:88], 8)
        for b in range(1, 4):
            for g in range(4):
                pool.wait_ge(S["mul_ready"], 4 * b + g + 1)
                src = mgt[:, g % 2].rearrange("p a t -> p (a t)")
                dst = mg[:, 2 * g:2 * g + 2].rearrange("p a t -> p (a t)")
                nc.gpsimd.tensor_tensor(dst, dst, src, ALU.add).then_inc(S["br_read"], 1)
        power(small[:, 76:78], small[:, 74:76], 2)
        def one_hot(q, parity):
            pool.wait_ge(S["places_compared"], q + 1)
            nc.gpsimd.tensor_tensor(sel[:, parity], sel_one[:, 0], sel_one[:, 1], ALU.add).then_inc(S["sel_ready"], 1)

        def slot_weights(q, first=False):
            pool.wait_ge(S["parts_ready"], q + 1)
            parts = cw_parts
            nc.gpsimd.tensor_tensor(small[:, 412:414], parts[:, 0:2], parts[:, 2:4], ALU.add)
            nc.gpsimd.tensor_scalar(small[:, 414:416], parts[:, 4:6], slot_no[:, P:P + 1], None, ALU.is_equal).then_inc(S["cw_step"], 1)
            pool.wait_ge(S["cw_step"], q + 1)
            if not first:
                pool.wait_ge(S["pair_hid"], q * 2)
            nc.gpsimd.tensor_tensor(cw, small[:, 412:414], small[:, 414:416], ALU.mult).then_inc(S["cw_ready"], 1)

        pool.wait_ge(S["router_landed"], 80)
        one_hot(0, 0)
        slot_weights(0, first=True)
        one_hot(1, 1)
        with pool.Fori(0, (PAIRS - 2) // 2) as i:
            for u in range(2):
                q = i * 2 + (1 + u)
                slot_weights(q)
                pool.wait_ge(S["slots_turned"], q)
                one_hot(q + 1, u % 2)
        slot_weights(PAIRS - 1)
        power(small[:, 76:78], small[:, 74:76], 2)

    @block.vector
    def _(dve):
        one = Steps(dve, S["dve_step"])
        V = nc.vector
        norms = [0]

        def low(n, rslot, slot):
            dve.wait_ge(S["hi_done"], n + 1)
            V.tensor_tensor(wlo[:, slot], raw(rslot), whi[:, slot].bitcast(F32), ALU.subtract).then_inc(S["lo_done"], 1)

        def low_m(n):
            if n < NM:
                low(n, raw_slot(n), n % 3)

        def layer_norm(src, dst, gb, landed, landed_count, ready, waits=None):
            st = small[:, 128:128 + 24].rearrange("p (t s) -> p t s", t=NT)
            mv = small[:, 68:72].rearrange("p (t s) -> p t s", t=NT)
            for t in range(NT):
                if waits:
                    waits(t)
                for q in range(2):
                    one(V.bn_stats(st[:, t, 6 * q:6 * q + 6], src[:, t, 512 * q:512 * q + 512]))
                one(V.bn_aggr(mv[:, t], st[:, t]))
            norms[0] += 1
            V.tensor_scalar(small[:, 74:76], mv[:, :, 1], EPS, None, ALU.add).then_inc(S["mv_ready"], 1)
            dve.wait_ge(S["rstd_ready"], norms[0])
            dve.wait_ge(landed, landed_count)
            for t in range(NT):
                one(V.scalar_tensor_tensor(out=dst[:, t], in0=src[:, t], scalar=mv[:, t, 0:1], in1=gb[:, 0], op0=ALU.subtract, op1=ALU.mult))
                V.scalar_tensor_tensor(out=dst[:, t], in0=dst[:, t], scalar=small[:, 76 + t:77 + t], in1=gb[:, 1], op0=ALU.mult,
                                       op1=ALU.add).then_inc(ready, 1)

        def low_turned(count):
            for t in range(NT):
                dve.wait_ge(S["aT_hi"], count + t + 1)
                for b in range(2):
                    last = V.tensor_tensor(aT[:, 1, 4 * b:4 * b + 4, t * P:(t + 1) * P],
                                           ps[:, 4 + 2 * t + b, :].rearrange("p (k c) -> p k c", k=4),
                                           aT[:, 0, 4 * b:4 * b + 4, t * P:(t + 1) * P].bitcast(F32), ALU.subtract)
                last.then_inc(S["aT_lo"], 1)

        def evacuate(blk):
            pair = blk % 2
            b0, free = 2 * pair, pair_free[pair]
            if blk >= len(W_IN_ORDER):
                return
            b = W_IN_ORDER[blk]
            dst = {0: rqk, 2: nqk, 6: dqT, 7: dkT}.get(b)
            if dst is None:
                return
            dve.wait_ge(S["pe_used"], 2 * blk + 2)
            if b == 6:
                dve.wait_ge(S["ret_scores"], HEADS)
            for c in range(2):
                d = dst[:, 2 * c:2 * c + 2].rearrange("p c t -> p (c t)")
                f = SCALE if (b == 2 and c == 0) or b == 6 else 1.0
                V.tensor_scalar(d, ps[:, b0 + c, :], f, None, ALU.mult).then_inc(free, 1)

        def ret_decay():
            dve.wait_ge(S["ret_landed"], 16)
            for h in range(HEADS):
                dve.wait_ge(S["ret_scores"], h + 1)
                V.tensor_tensor(retS[:, h].rearrange("p j i -> p (j i)"), ps[:, 4 + h, :],
                                retM[:, h].rearrange("p j i -> p (j i)"), ALU.mult).then_inc(S["ret_decayed"], 1)

        def rms(width, gain, col, gains_ready):
            n = NT * HEADS * width
            o, sq = oo[:, 0:n], osq[:, 0:n]
            one(V.tensor_tensor(sq, o, o, ALU.mult))
            one(V.tensor_reduce(small[:, 96:104], sq.rearrange("p (g c) -> p g c", c=width), AX.X, ALU.add))
            norms[0] += 1
            V.tensor_scalar(small[:, 80:88], small[:, 96:104], 1.0 / width, EPS, ALU.mult, ALU.add).then_inc(S["mv_ready"], 1)
            dve.wait_ge(S["rstd_ready"], norms[0])
            r = small[:, 88:96].unsqueeze(2).to_broadcast([P, NT * HEADS, width])
            one(V.tensor_tensor(sq.rearrange("p (g c) -> p g c", c=width), o.rearrange("p (g c) -> p g c", c=width), r, ALU.mult))
            if gains_ready is not None:
                dve.wait_ge(S["gate_mul"], gains_ready)
            w = HEADS * width
            V.tensor_tensor(y[:, :, col:col + w], sq.rearrange("p (t c) -> p t c", t=NT), gain, ALU.mult).then_inc(S["y_ready"], 1)

        def ret_norm():
            dve.wait_ge(S["ret_copied"], 1)
            rms(64, rg[:], 0, 1)

        def nat_mask(h):
            dve.wait_ge(S["nat_scores"], h + 1)
            V.tensor_tensor(pp[:, h], ps[:, 5 + h % 2, :].rearrange("p (i k) -> p i k", i=NT),
                            natm[:].unsqueeze(1).to_broadcast([P, NT, TOKENS]), ALU.add).then_inc(S["nat_masked"], 1)
            dve.wait_ge(S["nat_masked"], h + 1)
            V.tensor_reduce(small[:, 2 * h:2 * h + 2], pp[:, h], AX.X, ALU.max, negate=True).then_inc(S["nat_max"], 1)

        def nat_norm(h):
            dve.wait_ge(S["nat_exp"], h + 1)
            one(V.reciprocal(small[:, 16 + 2 * h:18 + 2 * h], small[:, 8 + 2 * h:10 + 2 * h]))
            for i in range(NT):
                last = V.tensor_scalar(pp[:, h, i], pp[:, h, i], small[:, 16 + 2 * h + i:17 + 2 * h + i], None, ALU.mult)
            last.then_inc(S["nat_p"], 1)

        def dif_bias(h):
            dve.wait_ge(S["dif_scores"], h + 1)
            b0 = 6 if h == 0 else 4
            slope = 2.0 ** (-8.0 * (h + 1) / HEADS)
            if h == 0:
                dve.wait_ge(S["nat_landed"], 80)
                dve.wait_ge(S["y_ready"], 1)
            if h >= 2:
                dve.wait_ge(S["dif_a"], h - 1)
            for s in range(2):
                V.scalar_tensor_tensor(out=ee[:, h % 2, s].rearrange("p i k -> p (i k)"), in0=dist[:].rearrange("p i k -> p (i k)"),
                                       scalar=-slope, in1=ps[:, b0 + s, :], op0=ALU.mult, op1=ALU.add).then_inc(S["dif_biased"], 1)
            dve.wait_ge(S["dif_biased"], 2 * h + 2)
            c = 32 + 8 * h
            V.tensor_reduce(small[:, c:c + 4], ee[:, h % 2].rearrange("p s i k -> p (s i) k"), AX.X, ALU.max,
                            negate=True).then_inc(S["dif_max"], 1)

        def dif_combine(h):
            dve.wait_ge(S["dif_exp"], h + 1)
            if h == 0:
                dve.wait_ge(S["nat_turned"], HEADS)
            c = 36 + 8 * h
            one(V.reciprocal(small[:, 104:108], small[:, c:c + 4]))
            one(V.tensor_scalar(small[:, 108:110], small[:, 106:108], small[:, 64:65], None, ALU.mult))
            for i in range(NT):
                last = V.tensor_scalar(ee[:, h % 2, 1, i], ee[:, h % 2, 1, i], small[:, 108 + i:109 + i], None, ALU.mult)
            one(last)
            for i in range(NT):
                last = V.scalar_tensor_tensor(out=pp[:, h, i], in0=ee[:, h % 2, 0, i], scalar=small[:, 104 + i:105 + i],
                                              in1=ee[:, h % 2, 1, i], op0=ALU.mult, op1=ALU.subtract)
            last.then_inc(S["dif_a"], 1)
            dve.wait_ge(S["dif_a"], h + 1)

        def lam_sums():
            dve.wait_ge(S["vec_landed"], 80)
            v = lamv[:].rearrange("p (a b c) -> p a b c", a=2, b=2)
            w = small[:, 256:384].rearrange("p (a c) -> p a c", a=2)
            one(V.tensor_tensor(w, v[:, :, 0], v[:, :, 1], ALU.mult))
            V.tensor_reduce(small[:, 64:66], w, AX.X, ALU.add).then_inc(S["lam_sums"], 2)
            one(V.tensor_scalar(gnd[:], gnd[:], 1.0 - LAM_INIT, None, ALU.mult))

        def lam():
            dve.wait_ge(S["lam_exps"], 1)
            one(V.tensor_tensor(small[:, 64:65], small[:, 66:67], small[:, 67:68], ALU.subtract))
            one(V.tensor_scalar(small[:, 64:65], small[:, 64:65], LAM_INIT, None, ALU.add))

        def dif_norm():
            dve.wait_ge(S["dif_copied"], NT)
            rms(P, gnd[:].unsqueeze(1).to_broadcast([P, NT, 512]), 768, None)

        def lower_shift():
            dve.wait_ge(S["lb_landed"], 16)
            V.tensor_tensor(lb[:], lbv[:], lbv[:], ALU.subtract).then_inc(S["lb_shift"], 1)

        def lower():
            dve.wait_ge(S["lb_exp"], 1)
            one(V.reciprocal(lbv[:], lb[:]))
            one(V.tensor_tensor(lbv[:], lb[:], lbv[:], ALU.mult))
            one(V.tensor_tensor(lb[:], lbv[:], lbv[:], ALU.subtract))
            one(V.tensor_scalar(om[:], lb[:], -1.0, 1.0, ALU.mult, ALU.add))

        def forget():
            dve.wait_ge(pair_free[1], 2 * 4)
            for t in range(NT):
                one(V.tensor_tensor(logf[:, t], logf[:, t], om[:], ALU.mult))
                one(V.tensor_tensor(logf[:, t], logf[:, t], lb[:], ALU.add))
                V.tensor_scalar(logf[:, t], logf[:, t], LOG_FLOOR, None, ALU.max).then_inc(S["f_ready"], 1)
            for t in range(NT):
                last = V.tensor_tensor(kTM[:, t], kTM[:, t], om[:], ALU.mult)
            last.then_inc(S["km_ready"], 1)

        def queries_keys(lv):
            if lv == 0:
                dve.wait_ge(S["kc_ready"], 2)
            if lv == DIAG:
                dve.wait_ge(S["hg_scores"], lv - 1)
                V.tensor_tensor(Kb[:, lv % 2], kc[:, 0], kc[:, 1], ALU.add).then_inc(S["qk_ready"], 1)
                return
            dve.wait_ge(S["seg_exp"], 2 * lv + 2)
            if lv >= 2:
                dve.wait_ge(S["hg_scores"], lv - 1)
            half = P >> lv
            E, Q, K = Eb[:, lv % 2], Qb[:, lv % 2], Kb[:, lv % 2]
            for half_no in range(2):
                for src, e, dst in ((kc[:, half_no], E[:, half_no], K), (hq[:], E[:, 1 - half_no], Q)):
                    a, b, o = (v.rearrange("p c (b s m) -> p (c b) s m", s=2, m=half)[:, :, half_no] for v in (src, e, dst))
                    last = V.tensor_tensor(o, a, b, ALU.mult)
            last.then_inc(S["qk_ready"], 1)

        def mask_level(lv):
            dve.wait_ge(S["hg_scores"], lv + 1)
            if lv == 1:
                dve.wait_ge(S["y_ready"], 2)
            if lv >= 3:
                dve.wait_ge(S["hg_added"], lv - 2)
            mk = (ident[:] if lv == DIAG else msk[:, lv - 1]).unsqueeze(1).to_broadcast([P, HEADS, P])
            dst = accS if lv == 1 else tmpS
            for x in range(2):
                V.tensor_tensor(dst[:, x].rearrange("p x h i -> p (x h) i"), ps[:, 6 + x, :].rearrange("p (h i) -> p h i", h=HEADS), mk, ALU.mult).then_inc(S["hg_masked"], 1)

        def hg_norm():
            dve.wait_ge(S["hg_copied"], 1)
            rms(64, hg[:], 512, 2)

        after = {
            2: [ret_decay, lam_sums], 4: [ret_norm],
            6: [lambda: nat_mask(0), lambda: nat_mask(1), lambda: nat_norm(0), lambda: nat_norm(1)],
            9: [lambda: nat_mask(2), lambda: nat_mask(3), lambda: nat_norm(2), lambda: nat_norm(3)],
            8: [lower_shift], 13: [lam, lower], 14: [lambda: dif_bias(0), lambda: dif_combine(0)], 15: [forget, lambda: dif_bias(1), lambda: dif_combine(1)],
            17: [lambda: dif_bias(2), lambda: dif_combine(2)], 19: [lambda: dif_bias(3), lambda: dif_combine(3)],
            21: [dif_norm], 32: [hg_norm],
        }
        layer_norm(xin, h0, lnb, S["lnin_landed"], 32, S["h_ready"], lambda t: dve.wait_ge(x_landed[t], 16))
        low_m(0)
        low_turned(0)
        low_m(1)
        for n in range(N_PROJ):
            low_m(n + 2)
            if n % 2 == 1:
                evacuate(n // 2)
            for task in after.get(n, ()):
                task()
            if 22 <= n < 22 + LEVELS:
                queries_keys(n - 22)
            if 24 <= n < 24 + DIAG:
                mask_level(n - 23)

        for rnd in range(3):
            dve.wait_ge(S["yT_hi"], rnd + 1)
            nq = min(4, 10 - 4 * rnd)
            b0 = 4 + 2 * (rnd % 2)
            for b in range((nq + 1) // 2):
                q = slice(4 * rnd + 2 * b, 4 * rnd + 2 * b + 2)
                last = V.tensor_tensor(yT[:, 1, q, :], ps[:, b0 + b, :].rearrange("p (q t) -> p q t", q=2),
                                       yT[:, 0, q, :].bitcast(F32), ALU.subtract)
            last.then_inc(S["yT_lo"], 1)

        def merged_low(g):
            dve.wait_ge(S["mg_hi"], g + 1)
            V.tensor_tensor(aT[:, 1, 2 * g:2 * g + 2].rearrange("p k t -> p (k t)"), mg[:, 2 * g:2 * g + 2].rearrange("p k t -> p (k t)"),
                            aT[:, 0, 2 * g:2 * g + 2].rearrange("p k t -> p (k t)").bitcast(F32), ALU.subtract).then_inc(S["mg_lo"], 1)

        def merge(b):
            if b < 3:
                dve.wait_ge(S["pe_used"], N_PROJ + b + 1)
            for g in range(4):
                if b == 3 and g < 3:
                    dve.wait_ge(S["bank_ready"], g + 1)
                elif b == 3:
                    dve.wait_ge(S["pe_used"], N_PROJ + N_BR)
                gates = (g0 if b < 2 else g1)[:, (2 * b + g // 2) % 4, 2 * (g % 2):2 * (g % 2) + 2]
                if b == 0:
                    dst = mg[:, 2 * g:2 * g + 2]
                    if g == 0:
                        dve.wait_ge(S["y_turned"], 3)
                else:
                    if 4 * (b - 1) + g >= 2:
                        dve.wait_ge(S["br_read"], 4 * (b - 1) + g - 1)
                    dst = mgt[:, g % 2]
                V.tensor_tensor(dst.rearrange("p a t -> p (a t)"), ps[:, 4 * (b % 2) + g, :],
                                gates.rearrange("p a t -> p (a t)"), ALU.mult).then_inc(S["mul_ready"], 1)
                if b == 3 and g > 0:
                    merged_low(g - 1)
            if b == 3:
                merged_low(3)

        for n in range(N_PROJ + 2, NM):
            low_m(n)
            if n < N_PROJ + N_BR:
                merge(n - N_PROJ - 2)
            if n == N_PROJ + N_BR:
                merge(3)
        dve.wait_ge(S["wr_hi"], 1)
        V.tensor_tensor(wrs[:, 1], wr[:], wrs[:, 0].bitcast(F32), ALU.subtract).then_inc(S["wr_lo"], 1)
        for n in range(NM, NM + 2):
            low(n, raw_slot(n), n % 3)
        dve.wait_ge(S["h0_back"], 16)

        def add_residual(src, t, count):
            for half in range(2):
                last = V.scalar_tensor_tensor(out=src[1][:, t, half * 512:(half + 1) * 512],
                                              in0=src[0][:, t, half * 512:(half + 1) * 512], scalar=ALPHA,
                                              in1=ps[:, 2 * t + half, :], op0=ALU.mult, op1=ALU.add)
            last.then_inc(S["out_read"], 1)
            dve.wait_ge(S["out_read"], count + t + 1)

        def mixed(t):
            if t == 0:
                dve.wait_ge(S["out_first"], 1)
            else:
                dve.wait_ge(S["pe_used"], NM)
            add_residual((h0b, zz), t, 0)

        layer_norm(zz, zz, ln1b, S["ln1_landed"], 32, S["h_ready"], mixed)
        low_turned(NT)
        low(NM + 2, raw_slot(NM + 2), (NM + 2) % 3)
        dve.wait_ge(S["h1s_hi"], 1)
        V.tensor_tensor(h1s[:, 1].rearrange("p t c -> p (t c)"), zz[:].rearrange("p t c -> p (t c)"),
                        h1s[:, 0].rearrange("p t c -> p (t c)").bitcast(F32), ALU.subtract).then_inc(S["h1s_lo"], 1)

        dve.wait_ge(S["scores_ready"], 1)
        sc = tk[:, 0:128].rearrange("p (t e) -> p t e", t=NT)
        biased = tk[:, 128:256].rearrange("p (t e) -> p t e", t=NT)
        one(V.tensor_tensor(biased, sc, rbb[:].unsqueeze(1).to_broadcast([P, NT, 64]), ALU.add))
        top = tk[:, 256:384].rearrange("p (t g k) -> p t g k", t=NT, g=N_GROUPS)
        for t in range(NT):
            for g in range(N_GROUPS):
                last = V.max(top[:, t, g], biased[:, t, 8 * g:8 * g + 8])
        one(last)

        def vec(i):
            return tk[:, 896 + 16 * i:912 + 16 * i].rearrange("p (t g) -> p t g", t=NT)

        gs, rank, keep, drop, best = (vec(i) for i in range(5))
        one(V.tensor_tensor(gs, top[:, :, :, 0], top[:, :, :, 1], ALU.add))
        other = gs.unsqueeze(2).to_broadcast([P, NT, 8, 8])
        own = gs.unsqueeze(3).to_broadcast([P, NT, 8, 8])
        gt = tk[:, 384:512].rearrange("p (t a b) -> p t a b", t=NT, a=8)
        eq = tk[:, 512:640].rearrange("p (t a b) -> p t a b", t=NT, a=8)
        V.tensor_tensor(gt, other, own, ALU.is_gt)
        one(V.tensor_tensor(eq, other, own, ALU.is_equal))
        one(V.tensor_tensor(eq, eq, tri[:].rearrange("p (a b) -> p a b", a=8).unsqueeze(1).to_broadcast([P, NT, 8, 8]), ALU.mult))
        one(V.tensor_tensor(gt, gt, eq, ALU.add))
        one(V.tensor_reduce(rank, gt, AX.X, ALU.add))
        one(V.tensor_scalar(keep, rank, TOPK_GROUPS - 0.5, None, ALU.is_lt))
        one(V.tensor_scalar(drop, keep, -MASK, MASK, ALU.mult, ALU.add))
        cand = tk[:, 512:640].rearrange("p (t g k) -> p t g k", t=NT, g=8)
        one(V.tensor_tensor(cand, biased.rearrange("p t (g k) -> p t g k", g=8), keep.unsqueeze(3).to_broadcast([P, NT, 8, 8]), ALU.mult))
        one(V.tensor_tensor(cand, cand, drop.unsqueeze(3).to_broadcast([P, NT, 8, 8]), ALU.add))
        cv = tk[:, 512:640].rearrange("p (t e) -> p t e", t=NT)
        left = tk[:, 384:512].rearrange("p (t e) -> p t e", t=NT)
        for t in range(NT):
            last = V.max(best[:, t], cv[:, t])
        one(last)
        for t in range(NT):
            last = V.match_replace(left[:, t], best[:, t], cv[:, t], 3.0 * MASK)
        one(last)
        chosen = tk[:, 640:768].rearrange("p (t e) -> p t e", t=NT)
        V.tensor_tensor(chosen, cv, left, ALU.not_equal).then_inc(S["mask_ready"], 1)
        dve.wait_ge(S["mask_ready"], 1)
        wts = tk[:, 768:896].rearrange("p (t e) -> p t e", t=NT)
        one(V.tensor_tensor(wts, chosen, sc, ALU.mult))
        one(V.tensor_reduce(tk[:, 976:978], wts, AX.X, ALU.add))
        one(V.tensor_scalar(tk[:, 978:980], tk[:, 976:978], 1e-20, None, ALU.add))
        one(V.reciprocal(tk[:, 980:982], tk[:, 978:980]))
        for t in range(NT):
            last = V.tensor_scalar(comb[:, t], wts[:, t], tk[:, 980 + t:981 + t], ROUTED_SCALE, ALU.mult, ALU.mult)
        last.then_inc(S["comb_ready"], 1)
        dve.wait_ge(S["comb_ready"], 1)

        def dense_hidden(silu_done, done, count, weight):
            for t in range(NT):
                dve.wait_ge(silu_done, count * 2 + t - 1)
                up = ps[:, 4 + t, HID:2 * HID]
                if weight is None:
                    V.tensor_tensor(hid[:, t], up, sil[:, t], ALU.mult).then_inc(done, 1)
                else:
                    V.scalar_tensor_tensor(out=hid[:, t], in0=up, scalar=weight(t), in1=sil[:, t], op0=ALU.mult,
                                           op1=ALU.mult).then_inc(done, 1)

        def dense_low(hi_done, done, count):
            for t in range(NT):
                dve.wait_ge(hi_done, count * 2 + t - 1)
                V.tensor_tensor(hTs[:, 1, t], ps[:, 6 + t, 0:256].rearrange("p (j c) -> p j c", j=2),
                                hTs[:, 0, t].bitcast(F32), ALU.subtract).then_inc(done, 1)

        dense_hidden(S["sh_silu"], S["sh_hid"], 1, None)
        dve.wait_ge(S["ranks"], 1)
        rk = tk[:, 0:192].rearrange("p (t e) -> p t e", t=3)
        V.tensor_copy(tk[:, 0:192], ps[:, 0, 0:192]).then_inc(S["ranks_read"], 1)
        dense_low(S["sh_hi"], S["sh_lo"], 1)
        dve.wait_ge(S["ranks_read"], 1)
        total = tk[:, 128:192].rearrange("p (q e) -> p q e", e=2)
        ranks = tk[:, 0:128].rearrange("p (t q e) -> p t q e", t=NT, e=2)
        for t in range(NT):
            one(V.tensor_tensor(ranks[:, t, :, 1], ranks[:, t, :, 1], total[:, :, 0], ALU.add))
        one(V.scalar_tensor_tensor(out=place[:], in0=rk[:, 0:2], scalar=1.0, in1=chosen, op0=ALU.add, op1=ALU.mult))
        one(V.tensor_scalar(place[:], place[:], -1.0, None, ALU.add))
        one(V.tensor_scalar(comb_over[:], place[:], P - 0.5, None, ALU.is_gt))
        one(V.tensor_tensor(comb_over[:], comb_over[:], comb[:], ALU.mult))
        one(V.tensor_tensor(tk[:, 192:224], total[:, :, 0], total[:, :, 1], ALU.add))
        one(V.tensor_reduce(tk[:, 224:225], tk[:, 192:224], AX.X, ALU.max))
        V.tensor_scalar(over[:, 0:1], tk[:, 224:225], P + 0.5, None, ALU.is_gt).then_inc(S["over_ready"], 1)
        V.tensor_copy(wc[:, :, :, 4:6], place[:].rearrange("p t (q e) -> p t q e", e=2))
        dve.wait_ge(S["wc_hi"], 1)
        V.tensor_tensor(wc[:, :, :, 2:4], comb[:].rearrange("p t (q e) -> p t q e", e=2), wc[:, :, :, 0:2].bitcast(F32),
                        ALU.subtract).then_inc(S["wc_lo"], 1)

        def gather_low(q, piece, parity):
            dve.wait_ge(S["gathered"], q * 4 + (1 + piece))
            k0 = 4 * (piece // 2)
            V.tensor_copy(xg[parity][:, 1, k0:k0 + 4, :].rearrange("p k s -> p (k s)"), ps[:, 6, :]).then_inc(S["gather_lo"], 1)

        def step_low(q, v):
            low(step_chunk(q, v), step_slot(v), split_slot(v))

        def hidden(q, e):
            dve.wait_ge(S["cw_ready"], q + 1)
            dve.wait_ge(S["pair_silu"], q * 2 + (1 + e))
            V.scalar_tensor_tensor(out=hid[:, e], in0=ps[:, 4 + e, HID:2 * HID], scalar=cw[:, e:e + 1], in1=sil[:, e],
                                   op0=ALU.mult, op1=ALU.mult).then_inc(S["pair_hid"], 1)

        def hidden_low(q, e):
            dve.wait_ge(S["hid_hi"], q * 2 + (1 + e))
            V.tensor_tensor(hTs[:, 1, e].rearrange("p j c -> p (j c)"), ps[:, 4 + e, 0:256],
                            hTs[:, 0, e].rearrange("p j c -> p (j c)").bitcast(F32), ALU.subtract).then_inc(S["hid_lo"], 1)

        def outputs_low(q):
            for half in range(2):
                dve.wait_ge(S["y_hi"], q * 2 + (1 + half))
                V.tensor_tensor(ys[:, 1, half * 512:(half + 1) * 512], ps[:, 6 + half, :],
                                ys[:, 0, half * 512:(half + 1) * 512].bitcast(F32), ALU.subtract).then_inc(S["y_lo"], 1)

        def compare_places(q, first=False):
            if not first:
                dve.wait_ge(S["sel_ready"], q)
            for e in range(2):
                c = q * 2 + e
                pl = place[:, :, c:c + 1] if isinstance(c, int) else place[:, :, bass.ds(c, 1)]
                last = V.tensor_tensor(sel_one[:, e], slot_no[:, 0:P].unsqueeze(1).to_broadcast([P, NT, P]),
                                       pl.to_broadcast([P, NT, P]), ALU.is_equal)
            last.then_inc(S["places_compared"], 1)

        def pair_step(q, parity, first=False, final=False):
            if not first:
                hidden(q + (-1), 1)
                gather_low(q, 3, parity)
                step_low(q, 2)
                if not final:
                    compare_places(q + 1)
                hidden_low(q + (-1), 1)
                step_low(q, 3)
            else:
                compare_places(q + 1)
                step_low(q, 4)
            hidden(q, 0)
            if not first:
                step_low(q, 4)
            step_low(q, 5)
            hidden_low(q, 0)
            if not first:
                outputs_low(q + (-1))
            step_low(q + 1, 0)

        def next_slots(q, parity):
            gather_low(q + 1, 1, 1 - parity)
            step_low(q + 1, 1)

        compare_places(0, first=True)
        for n in range(NM + 3, NM + 5):
            low(n, raw_slot(n), n % 3)
        gather_low(0, 1, 0)
        gather_low(0, 3, 0)
        pair_step(0, 0, first=True)
        next_slots(0, 0)
        with dve.Fori(0, (PAIRS - 2) // 2) as i:
            for u in range(2):
                pair_step(i * 2 + (1 + u), (1 + u) % 2)
                next_slots(i * 2 + (1 + u), (1 + u) % 2)
        pair_step(PAIRS - 1, (PAIRS - 1) % 2, final=True)
        step_low(PAIRS, 1)
        hidden(PAIRS - 1, 1)
        hidden_low(PAIRS - 1, 1)
        outputs_low(PAIRS - 1)

        with if_over(dve):
            V.memset(tk[:, 1:2], 0.0).then_inc(S["fb_down"], 1)
            with dve.Fori(0, N_EXPERTS) as e:
                dve.wait_ge(S["fb_split_hi"], e + 1)
                for c in range(3):
                    last = V.tensor_tensor(wlo[:, c], rawL[:, c], whi[:, c].bitcast(F32), ALU.subtract)
                last.then_inc(S["fb_split_lo"], 1)
                dense_hidden(S["fb_silu"], S["fb_hid"], e + 1, lambda t: comb_over[:, t, bass.ds(e, 1)])
                dense_low(S["fb_hi"], S["fb_lo"], e + 1)
            dve.wait_ge(S["fb_down"], N_EXPERTS + 1)
        dve.wait_ge(S["scattered"], PAIRS)
        layer_norm(outb, outb, ln2b, S["ln2_landed"], 32, S["z_ready"], lambda t: add_residual((zz, outb), t, NT))

    ctx.close()


_INPUTS = ["x", "ln_in_g", "ln_in_b", "w_in", "w_gate", "b_gate", "w_br_ret", "w_br_nat", "w_br_hgrn", "w_br_diff",
           "w_out", "ret_gn", "rpb", "hgrn_lb", "hgrn_gn", "diff_lambda", "diff_subln", "ln1_g", "ln1_b", "w_router",
           "router_bias", "w_e_gate", "w_e_up", "w_e_down", "w_s_gate", "w_s_up", "w_s_down", "ln2_g", "ln2_b"]


def kernel(**inputs):
    import concourse.bacc as bacc
    from concourse.bass_utils import run_bass_kernel_spmd

    a = {k: np.asarray(v) for k, v in inputs.items()}
    a["b_gate"] = np.ascontiguousarray(a["b_gate"].reshape(32, P).T)
    rpb = a.pop("nat_rpb")[0]
    pad = np.zeros((HEADS, 7, 127), rpb.dtype)
    pad[:, :, 48:79] = rpb[:, 4:11]
    a["rpb"] = pad
    arrays = {k: np.ascontiguousarray(a[k]) for k in _INPUTS}
    arrays.update(constants())
    nc = bacc.Bacc("TRN2", target_bir_lowering=False, num_devices=1)
    args = {k: nc.dram_tensor("in_" + k, v.shape, mybir.dt.from_np(v.dtype), kind="ExternalInput").ap() for k, v in arrays.items()}
    out = nc.dram_tensor("out_0", (1, TOKENS, D), F32, kind="ExternalOutput").ap()
    build(nc, args, out)
    r = run_bass_kernel_spmd(nc, [{"in_" + k: v for k, v in arrays.items()}], core_ids=[0])
    return r.results[0]["out_0"]
```

```python
from contextlib import ExitStack

import numpy as np

import concourse.bass as bass
from concourse import mybir

F32 = mybir.dt.float32
F32R = mybir.dt.float32r
ACT = mybir.ActivationFunctionType
ALU = mybir.AluOpType
AX = mybir.AxisListType

P = 128
TOKENS, D = 256, 1024
NT = TOKENS // P
KD = D // P
HEADS = 4
GRID_W, ROWS = 64, 4
N_EXPERTS, N_GROUPS, TOPK_GROUPS = 64, 8, 4
HID = 256
SCALE = 64 ** -0.5
EPS = 1e-5
ALPHA = 2.0 ** 0.25
ROUTED_SCALE = 2.5
LAM_INIT = 0.2
MASK = -1e30
LOG_FLOOR = 2.0 ** -64
PASSES = ((0, 0), (0, 1), (1, 0))

CH = 2048
W_IN_ORDER = (0, 1, 2, 3, 6, 7, 8, 4, 5)
NB = len(W_IN_ORDER) + 8
N_PROJ = 2 * NB
N_BR = 5
N_OUT = 4
NM = N_PROJ + N_BR + N_OUT
PAIRS = N_EXPERTS // 2
FIRST_BANKS = ((4, 7), (6, 5))
LEVELS = 9
DIAG = LEVELS - 1
Y_ROUNDS = ((0, 4), (2, 5), (6, 6), (8, 7), (4, 4))


def constants():
    i = np.arange(TOKENS)
    dist = np.abs(i[:, None] - i[None, :]).astype(np.float64)
    ret = np.zeros((HEADS, TOKENS, TOKENS))
    for h in range(HEADS):
        lf, lb = np.log1p(-2.0 ** (-5 - 2 * h)), np.log1p(-2.0 ** (-6 - 2 * h))
        d = i[None, :] - i[:, None]
        ret[h] = np.where(d > 0, np.exp(lf * d), np.where(d < 0, np.exp(-lb * d), 2.0)) * SCALE
    ret = ret.reshape(HEADS, NT, P, TOKENS).transpose(2, 0, 1, 3)
    c = np.arange(GRID_W)
    start = np.clip(c - 8, 0, GRID_W - 16)
    ok = (c[None, :] >= start[:, None]) & (c[None, :] < start[:, None] + 16)
    nat = np.tile(np.where(ok, 0.0, MASK), (2, ROWS))
    t = np.arange(P)
    seg = np.zeros((P, 2, LEVELS - 2, P))
    mask = np.zeros((P, LEVELS - 2, P))
    for lv in range(1, DIAG):
        m = P >> lv
        blk, half = t // (2 * m), (t // m) % 2
        b = blk * 2 * m + m - 1
        u = t[:, None]
        fwd = np.where(half[None] == 1, (u > b[None]) & (u <= t[None]), (u > t[None]) & (u <= b[None]))
        bwd = np.where(half[None] == 0, (u >= t[None]) & (u <= b[None]), (u > b[None]) & (u < t[None]))
        seg[:, 0, lv - 1], seg[:, 1, lv - 1] = fwd, bwd
        mask[:, lv - 1] = (blk[:, None] == blk[None]) & (half[:, None] != half[None])
    seg0 = np.zeros((P, 2, NT, P))
    u = t[:, None]
    seg0[:, 0, 0], seg0[:, 0, 1] = u > t[None], u <= t[None]
    seg0[:, 1, 0], seg0[:, 1, 1] = u >= t[None], u < t[None]
    rev = np.zeros((64, 64))
    rev[np.arange(64), 63 - np.arange(64)] = 1.0
    rev = np.concatenate([rev, rev])
    tri = (np.arange(8)[None, :] < np.arange(8)[:, None]).astype(np.float64)
    up = (np.arange(P)[:, None] < np.arange(P)[None, :]).astype(np.float64)
    out = {
        "c_up": np.stack([up, np.ones((P, P))], 1), "c_slot": np.concatenate([np.tile(np.arange(P, dtype=np.float64), (P, 1)), np.arange(P)[:, None]], 1),
        "c_ret": ret, "c_dist": dist.reshape(NT, P, TOKENS).transpose(1, 0, 2), "c_nat": nat,
        "c_seg": seg, "c_seg0": seg0, "c_mask": mask, "c_ident": np.eye(P), "c_rev": rev,
        "c_tri": np.tile(tri.reshape(1, 64), (P, 1)),
    }
    return {k: np.ascontiguousarray(v, dtype=np.float32) for k, v in out.items()}


class Map:

    def __init__(self, nc):
        self.nc, self.top = nc, (nc.sbuf_base + 63) // 64 * 64

    def at(self, offset, name, shape, dt=F32):
        return self.nc.alloc_sbuf_tensor_at(name, [shape[0], *shape[1:]], dt, offset=offset)

    def new(self, name, shape, dt=F32):
        t = self.at(self.top, name, shape, dt)
        self.top += (4 * int(np.prod(shape[1:])) + 31) // 32 * 32
        return t

    def region(self, nbytes):
        r = self.top
        self.top += nbytes
        return r


class Steps:

    def __init__(self, eng, sem):
        self.eng, self.sem, self.n = eng, sem, 0

    def __call__(self, ins):
        ins.then_inc(self.sem, 1)
        self.n += 1
        self.eng.wait_ge(self.sem, self.n)


def build(nc, A, out):
    m = Map(nc)
    KB = 1024
    whi = m.new("whi", [P, 3, CH], F32R)
    wlo = m.new("wlo", [P, 3, CH], F32R)
    aT = m.new("aT", [P, 2, KD, TOKENS], F32R)
    raw_lo = m.region(3 * 8 * KB)
    ident = m.new("ident", [P, P])
    small = m.new("small", [P, 512])
    pow_c = m.new("pow_c", [P, 16])
    r_x1 = m.region(16 * KB)
    r_in = m.region(36 * KB)
    r_th = m.region(32 * KB)
    r_y = m.region(10 * KB)
    r_c = m.region(16 * KB)
    r_v = m.region(4 * KB)
    assert m.top <= nc.sbuf_usable_end, (m.top, nc.sbuf_usable_end)

    rawL = m.at(raw_lo, "rawL", [P, 3, CH])
    rawH = m.at(r_x1, "rawH", [P, 3, CH])

    retM = m.at(r_x1, "retM", [P, HEADS, NT, TOKENS])
    retS = m.at(r_x1 + 8 * KB, "retS", [P, HEADS, NT, TOKENS])
    g0 = m.at(r_x1, "g0", [P, 4, 4, TOKENS])
    g1 = m.at(r_in, "g1", [P, 4, 4, TOKENS])

    rqk = m.at(r_in, "rqk", [P, 4, TOKENS])
    dqT = m.at(r_in, "dqT", [P, 4, TOKENS])
    rv = m.at(r_in + 4 * KB, "rv", [P, NT, 256])
    rg = m.at(r_in + 6 * KB, "rg", [P, NT, 256])
    nqk = m.at(r_in + 8 * KB, "nqk", [P, 4, TOKENS])
    nv = m.at(r_in + 12 * KB, "nv", [P, NT, 256])
    dkT = m.at(r_in + 14 * KB, "dkT", [P, 4, TOKENS])
    dv = m.at(r_in + 18 * KB, "dv", [P, NT, 512])
    offd = m.at(r_in + 18 * KB, "offd", [P, 2, 2, 2, P])
    hq = m.at(r_in + 22 * KB, "hq", [P, 2, TOKENS])
    kc = m.at(r_in + 24 * KB, "kc", [P, 2, 2, TOKENS])
    logf = m.at(r_in + 28 * KB, "logf", [P, NT, 512])
    hv = m.at(r_in + 32 * KB, "hv", [P, NT, 256])
    hg = m.at(r_in + 34 * KB, "hg", [P, NT, 256])

    xin = m.at(r_in, "xin", [P, NT, D])
    h0 = m.at(r_in + 8 * KB, "h0", [P, NT, D])
    lnb = m.at(r_th, "lnb", [P, 2, D])
    hk = m.at(r_th, "hk", [P, HEADS, 7, 64])
    kTM = m.at(r_th, "kTM", [P, NT, 512])
    pp = m.at(r_th + 8 * KB, "pp", [P, HEADS, NT, TOKENS])
    ppT = m.at(r_th + 16 * KB, "ppT", [P, HEADS, NT, TOKENS])
    ee = m.at(r_th + 24 * KB, "ee", [P, 2, 2, NT, TOKENS])
    oo = m.at(r_th + 28 * KB, "oo", [P, NT * 512])
    osq = m.at(r_th + 24 * KB, "osq", [P, NT * 512])
    Eb = m.at(r_th, "Eb", [P, 2, 2, 2, TOKENS])
    Qb = m.at(r_th + 8 * KB, "Qb", [P, 2, 2, TOKENS])
    Kb = m.at(r_th + 16 * KB, "Kb", [P, 2, 2, TOKENS])
    tmpS = m.at(r_th + 24 * KB, "tmpS", [P, 2, 2, 2, P])
    accS = m.at(r_th + 28 * KB, "accS", [P, 2, 2, 2, P])
    yT = m.at(r_th, "yT", [P, 2, 10, TOKENS], F32R)
    y = m.at(r_y, "y", [P, NT, 1280])
    seg = m.at(r_c, "seg", [P, 2, LEVELS - 2, P])
    seg0 = m.at(r_c + 7 * KB, "seg0", [P, 2, NT, P])
    msk = m.at(r_c + 9 * KB, "msk", [P, LEVELS - 2, P])
    dist = m.at(r_c + 9 * KB + 3584, "dist", [P, NT, TOKENS])
    natm = m.at(r_c + 9 * KB + 3584 + 2 * KB, "natm", [P, TOKENS])
    rev = m.at(r_v, "rev", [P, 64])
    lamv = m.at(r_v + 256, "lamv", [P, 256])
    gnr = m.at(r_v + 1280, "gnr", [P, 256])
    gnh = m.at(r_v + 2304, "gnh", [P, 256])
    lb = m.at(r_x1, "lb", [P, 512])
    om = m.at(r_x1 + 2 * KB, "om", [P, 512])
    lbv = m.at(r_x1 + 4 * KB, "lbv", [P, 512])
    gnd = m.new("gnd", [P, 512])
    bg = m.new("bg", [P, 32])
    assert m.top <= nc.sbuf_usable_end, (m.top, nc.sbuf_usable_end)
    mg = m.at(r_y, "mg", [P, KD, TOKENS])
    mgt = m.at(r_c, "mgt", [P, 2, 2, TOKENS])
    h0b = m.at(r_in + 24 * KB, "h0b", [P, NT, D])
    ln1b = m.at(r_th + 24 * KB, "ln1b", [P, 2, D])
    zz = m.at(r_y, "zz", [P, NT, D])
    wr = m.at(r_in + 8 * KB, "wr", [P, KD, 64])
    wrs = m.at(r_in + 10 * KB, "wrs", [P, 2, KD, 64], F32R)
    rbb = m.at(r_in + 14 * KB, "rbb", [P, 64])
    tri = m.at(r_in + 14 * KB + 256, "tri", [P, 64])
    tk = m.at(r_in + 15 * KB, "tk", [P, 1024])
    comb = m.at(r_in + 19 * KB, "comb", [P, NT, 64])
    place = m.at(r_in + 19 * KB + 512, "place", [P, NT, 64])
    comb_over = m.at(r_in + 20 * KB, "comb_over", [P, NT, 64])
    slot_no = m.at(r_in + 20 * KB + 512, "slot_no", [P, P + 1])
    wc = m.at(r_in + 8 * KB, "wc", [P, NT, PAIRS, 6], F32R)
    up_ones = m.at(r_in + 21 * KB + 544, "up_ones", [P, 2, P])
    over = m.at(r_in + 22 * KB + 576, "over", [P, 8], mybir.dt.int32)
    ys = m.at(r_in + 24 * KB, "ys", [P, 2, D], F32R)
    hTs = m.at(r_in + 32 * KB, "hTs", [P, 2, 2, 2, P], F32R)
    xg = [m.at(r_th + 16 * KB, "xg0", [P, 2, KD, 2 * P], F32R), m.at(r_c, "xg1", [P, 2, KD, 2 * P], F32R)]
    sil = m.at(r_y + 8 * KB, "sil", [P, 2, HID])
    scT = m.at(r_v, "scT", [P, TOKENS])
    hid = m.at(r_v, "hid", [P, 2, HID])
    sel_one = m.at(r_in + 10 * KB, "sel_one", [P, 2, NT, P])
    sel = m.at(r_v + 2 * KB, "sel", [P, 2, NT, 2 * P], F32R)
    selT = m.at(r_in + 12 * KB, "selT", [P, 2, NT, P], F32R)
    ident_r = m.at(r_in + 23 * KB, "ident_r", [P, P], F32R)
    h1s = m.at(r_th, "h1s", [P, 2, NT, D], F32R)
    outb = m.at(r_th + 16 * KB, "outb", [P, NT, D])
    ln2b = m.at(r_th + 24 * KB, "ln2b", [P, 2, D])
    cw = small[:, 400:402]
    cw_parts = small[:, 404:410]

    ps = nc.alloc_psum_tensor("ps", [P, 8, 512], F32)

    h_spill = nc.dram_tensor("h_spill", [P, NT, D], F32, kind="Internal").ap()

    names = """x_landed0 x_landed1 lnin_landed ret_landed nat_landed seg_landed vec_landed lb_landed ident_landed
    h0_spilled h0_back ln1_landed ln2_landed router_landed out_stored
    raw0 raw1 raw2 raw3 raw4 raw5 hi_done lo_done pe_used pair0 pair1
    dve_step act_step pool_step mv_ready rstd_ready h_ready h_turned aT_hi aT_lo
    ret_scores ret_decayed ret_out ret_copied nat_scores nat_masked nat_max nat_exp nat_p nat_turned nat_pT nat_out nat_y
    dif_scores dif_biased dif_max dif_exp dif_a dif_turned dif_aT dif_out dif_copied lam_sums lam_exps
    lower_ready forget_ready f_ready logf_ready km_ready kc_turned kc_ready seg_sums seg_exp qk_ready hg_scores hg_off hg_masked hg_added
    hg_out hg_copied gate_mul y_ready y_turned yT_hi yT_lo br_read mul_ready mg_hi mg_lo bank_ready out_first
    lb_shift lb_exp z_ready out_read
    wr_hi wr_lo logits scores_expert scores_turned scores_ready comb_ready mask_ready ranks ranks_read h1s_hi h1s_lo wc_hi wc_lo ident_ready over_ready
    sh_silu sh_hid sh_turned sh_hi sh_lo
    places_compared sel_ready gathered gather_hi gather_lo weights_summed parts_ready cw_step cw_ready slots_turned selT_ready
    pair_silu pair_hid hid_hi hid_lo y_hi y_lo half_down scattered
    fb_landed fb_split_hi fb_split_lo fb_gate_up fb_silu fb_hid fb_turned fb_hi fb_lo fb_down""".split()
    S = {n: nc.alloc_semaphore(n) for n in names}
    raw_landed = [S["raw0"], S["raw1"], S["raw2"], S["raw3"], S["raw4"], S["raw5"]]
    pair_free = [S["pair0"], S["pair1"]]
    x_landed = [S["x_landed0"], S["x_landed1"]]

    def raw_slot(n):
        return n % 3 if n < NM else (n - NM + 1) % 6

    mixer_loads = [sum(1 for n in range(NM) if n % 3 == s) if s < 3 else 0 for s in range(6)]

    def raw_count(n):
        if n < NM:
            return 32 * (n // 3 + 1)
        s = raw_slot(n)
        return 32 * (mixer_loads[s] + (n - NM + 1) // 6 + (s > 0))

    def raw(slot):
        return rawL[:, slot] if slot < 3 else rawH[:, slot - 3]

    def dram(ap, offset, dims):
        return bass.AP(ap.tensor, offset, dims)

    w_in, w_gate, w_out = A["w_in"], A["w_gate"], A["w_out"]
    IN_W = w_in.shape[-1]

    def mixer_sources(n):
        if n < N_PROJ:
            blk, half = n // 2, n % 2
            if blk < len(W_IN_ORDER):
                src, width, col = w_in, IN_W, 512 * W_IN_ORDER[blk]
            else:
                src, width, col = w_gate, 4 * D, 512 * (blk - len(W_IN_ORDER))
            return [(k * 512, 1024, dram(src, (4 * half + k) * width + col, [[KD * width, P], [width, 2], [1, 512]]))
                    for k in (0, 2)]
        if n < N_PROJ + N_BR:
            b = n - N_PROJ
            src = A[("w_br_ret", "w_br_nat", "w_br_hgrn", "w_br_diff", "w_br_diff")[b]]
            base = 256 * D if b == 4 else 0
            return [(j * D, D, dram(src, base + j * D, [[2 * D, P], [1, D]])) for j in range(2)]
        c = n - N_PROJ - N_BR
        return [(k * D, D, dram(w_out, (2 * c + k) * P * D, [[D, P], [1, D]])) for k in range(2)]

    def slot_view(slot, o, w, src):
        v = raw(slot)[:, o:o + w]
        return v.rearrange("p (a b) -> p a b", a=2) if len(src.shape) == 3 else v

    def step_chunk(q, v):
        return q * 6 + (NM + 1 + v)

    def step_slot(v):
        return raw_slot(NM + 1 + v)

    def split_slot(v):
        return (NM + 1 + v) % 3

    def if_over(eng):
        eng.wait_ge(S["over_ready"], 1)
        return eng.If(eng.value_load(over[0:1, 0:1], min_val=0, max_val=1) > 0)

    def add_level(pool, lv):
        pool.wait_ge(S["hg_masked"], 2 * lv)
        nc.gpsimd.tensor_tensor(accS[:].rearrange("p a x h i -> p (a x h i)"), accS[:].rearrange("p a x h i -> p (a x h i)"),
                                tmpS[:].rearrange("p a x h i -> p (a x h i)"), ALU.add).then_inc(S["hg_added"], 1)
        pool.wait_ge(S["hg_added"], lv - 1)

    ctx = ExitStack()
    block = ctx.enter_context(nc.Block())

    @block.sync
    def _(sp):
        for t in range(NT):
            sp.dma_start(xin[:, t], A["x"][0, t * P:(t + 1) * P, :]).then_inc(x_landed[t], 16)
        for n in range(NM):
            if n >= 3:
                sp.wait_ge(S["lo_done"], n - 2)
            for o, w, src in mixer_sources(n):
                sp.dma_start(slot_view(n % 3, o, w, src), src).then_inc(raw_landed[n % 3], 16)
            if n == 2:
                sp.wait_ge(S["h_ready"], NT)
                sp.dma_start(h_spill, h0[:]).then_inc(S["h0_spilled"], 16)
            if n == NM - 1:
                sp.wait_ge(S["h0_spilled"], 16)
                sp.wait_ge(S["mul_ready"], 16)
                sp.dma_start(h0b[:], h_spill).then_inc(S["h0_back"], 16)
                sp.dma_start(wr[:], dram(A["w_router"], 0, [[KD * 64, P], [64, KD], [1, 64]])).then_inc(S["router_landed"], 16)
                sp.dma_start(rbb[:], dram(A["router_bias"], 0, [[0, P], [1, 64]])).then_inc(S["router_landed"], 16)
                sp.dma_start(tri[:], A["c_tri"]).then_inc(S["router_landed"], 16)
                sp.dma_start(slot_no[:], A["c_slot"]).then_inc(S["router_landed"], 16)
                sp.dma_start(up_ones[:], A["c_up"]).then_inc(S["router_landed"], 16)
                for j, v in enumerate(("ln1_g", "ln1_b")):
                    sp.dma_start(ln1b[:, j], dram(A[v], 0, [[0, P], [1, D]])).then_inc(S["ln1_landed"], 16)

        def expert(w, e):
            return w[0, e] if isinstance(e, int) else w[0, bass.ds(e, 1)].rearrange("a r c -> (a r) c")

        def load_gate_up(gate, up, half, slot, landed):
            v = raw(slot).rearrange("p (j k c) -> p j k c", j=2, k=4)
            for j, src in enumerate((gate, up)):
                sv = src.rearrange("(p k) c -> p k c", k=KD)[:, 4 * half:4 * half + 4, :]
                sp.dma_start(v[:, j], sv).then_inc(landed, 16)

        def load_down(src, slot, landed):
            sv = src.rearrange("(p j) c -> p j c", j=2)
            v = raw(slot).rearrange("p (j c) -> p j c", j=2)
            for j in range(2):
                sp.dma_start(v[:, j], sv[:, j]).then_inc(landed, 16)

        def load_chunk(q, v, kind, e):
            sp.wait_ge(S["lo_done"], step_chunk(q, v) - 5)
            slot = step_slot(v)
            if kind is None:
                load_down(expert(A["w_e_down"], e), slot, raw_landed[slot])
            else:
                load_gate_up(expert(A["w_e_gate"], e), expert(A["w_e_up"], e), kind, slot, raw_landed[slot])

        sp.wait_ge(S["lo_done"], NM - 1)
        for half in range(2):
            slot = raw_slot(NM + half)
            load_gate_up(A["w_s_gate"][0], A["w_s_up"][0], half, slot, raw_landed[slot])
        sp.wait_ge(S["lo_done"], NM)
        load_down(A["w_s_down"][0], raw_slot(NM + 2), raw_landed[raw_slot(NM + 2)])
        for v in range(2, 6):
            load_chunk(0, v, v % 2, v // 2 - 1)
        with sp.Fori(1, PAIRS) as q:
            for v, kind, e in ((0, 0, 0), (1, 1, 0), (2, None, -2), (3, None, -1), (4, 0, 1), (5, 1, 1)):
                load_chunk(q, v, kind, q * 2 + e)
        for v in range(2):
            load_chunk(PAIRS, v, None, 2 * (PAIRS - 1) + v)
        sp.wait_ge(S["pe_used"], step_chunk(PAIRS, 0))
        for j, v in enumerate(("ln2_g", "ln2_b")):
            sp.dma_start(ln2b[:, j], dram(A[v], 0, [[0, P], [1, D]])).then_inc(S["ln2_landed"], 16)
        with if_over(sp):
            with sp.Fori(0, N_EXPERTS) as e:
                sp.wait_ge(S["fb_down"], e + 1)
                for half in range(2):
                    load_gate_up(expert(A["w_e_gate"], e), expert(A["w_e_up"], e), half, half, S["fb_landed"])
                load_down(expert(A["w_e_down"], e), 2, S["fb_landed"])
        for t in range(NT):
            sp.wait_ge(S["z_ready"], t + 1)
            sp.dma_start(out[0, t * P:(t + 1) * P, :], outb[:, t]).then_inc(S["out_stored"], 16)
        sp.wait_ge(S["out_stored"], 16 * NT)
        sp.wait_ge(S["h0_spilled"], 16)

    @block.tensor
    def _(pe):
        mm = nc.tensor.matmul

        def split_part(part, slot):
            return (whi if part == 0 else wlo)[:, slot]

        def project(n):
            blk, half = n // 2, n % 2
            pair, slot = blk % 2, n % 3
            if half == 0 and blk >= 2:
                pe.wait_ge(pair_free[pair], 2 * (blk // 2))
            pe.wait_ge(S["lo_done"], n + 1)
            wv = [split_part(i, slot).rearrange("p (k c) -> p k c", k=4) for i in range(2)]
            b = W_IN_ORDER[blk] if blk < len(W_IN_ORDER) else 99
            seen = set()

            def token_major(bank, off, t, c0, width):
                for k in range(4):
                    for a, w in PASSES:
                        first = half == 0 and bank not in seen
                        seen.add(bank)
                        last = mm(ps[:, bank, off:off + width], aT[:, a, 4 * half + k, t * P:(t + 1) * P],
                                  wv[w][:, k, c0:c0 + width], start=first,
                                  stop=half == 1 and k == 3 and (a, w) == PASSES[-1], skip_group_check=True)
                return last

            def channel_major(bank, off, c0):
                for k in range(4):
                    for a, w in PASSES:
                        first = half == 0 and bank not in seen
                        seen.add(bank)
                        last = mm(ps[:, bank, off:off + TOKENS], wv[w][:, k, c0:c0 + P], aT[:, a, 4 * half + k, :],
                                  start=first, stop=half == 1 and k == 3 and (a, w) == PASSES[-1],
                                  skip_group_check=True)
                return last

            if b in (1, 4, 5, 8):
                for t in range(NT):
                    last = token_major(2 * pair + t, 0, t, 0, 512)
            elif b == 3:
                for t in range(NT):
                    last = token_major(2 * pair, 256 * t, t, 0, 256)
                for c in range(2):
                    last = channel_major(2 * pair + 1, 256 * c, 256 + P * c)
            else:
                for c in range(4):
                    last = channel_major(2 * pair + c // 2, 256 * (c % 2), P * c)
            last.then_inc(S["pe_used"], 1)

        def head(t, h):
            return t[64 * (h % 2):64 * (h % 2) + 64, h // 2]

        def turn(src, first_sem, done, count):
            for t in range(NT):
                pe.wait_ge(first_sem, count + t + 1)
                for k in range(KD):
                    last = nc.tensor.transpose(ps[:, 4 + 2 * t + k // 4, (k % 4) * P:(k % 4 + 1) * P],
                                               src[:, t, k::KD], ident[:])
                last.then_inc(done, 1)

        def ret_scores():
            pe.wait_ge(pair_free[0], 2)
            pe.wait_ge(S["aT_lo"], NT)
            for h in range(HEADS):
                q, k = head(rqk, h), rqk[64 * (h % 2):64 * (h % 2) + 64, 2 + h // 2]
                for j in range(NT):
                    last = mm(ps[:, 4 + h, j * TOKENS:(j + 1) * TOKENS], k[:, j * P:(j + 1) * P], q, start=True, stop=True)
                last.then_inc(S["ret_scores"], 1)

        def ret_out():
            pe.wait_ge(S["ret_decayed"], HEADS)
            pe.wait_ge(pair_free[1], 2)
            for h in range(HEADS):
                for i in range(NT):
                    for j in range(NT):
                        last = mm(ps[:, 4, i * 256 + h * 64:i * 256 + h * 64 + 64], retS[:, h, j, i * P:(i + 1) * P],
                                  rv[:, j, h * 64:h * 64 + 64], start=j == 0, stop=j == NT - 1)
            last.then_inc(S["ret_out"], 1)

        def nat_scores(h):
            bank = 5 + h % 2
            if h == 0:
                pe.wait_ge(pair_free[0], 4)
                pe.wait_ge(S["nat_landed"], 80)
            if h < 2:
                pe.wait_ge(S["ret_decayed"], HEADS)
            else:
                pe.wait_ge(S["nat_masked"], h - 1)
            q, k = head(nqk, h), nqk[64 * (h % 2):64 * (h % 2) + 64, 2 + h // 2]
            rows = slice(64 * (h % 2), 64 * (h % 2) + 64)
            for i in range(NT):
                o = i * TOKENS
                for r in range(2):
                    row = 2 * i + r
                    mm(ps[64 * r:64 * r + 64, bank, o:o + TOKENS], rev[rows], hk[rows, h, 3 - row:7 - row, :],
                       start=True, stop=False)
                    last = mm(ps[64 * r:64 * r + 64, bank, o:o + TOKENS], q[:, row * 64:row * 64 + 64], k,
                              start=False, stop=True)
            last.then_inc(S["nat_scores"], 1)

        def turn_probs(src, h, bank, done):
            for i in range(NT):
                for j in range(NT):
                    last = nc.tensor.transpose(ps[:, bank, j * TOKENS + i * P:j * TOKENS + i * P + P],
                                               src[:, h, i, j * P:(j + 1) * P], ident[:])
            last.then_inc(done, 1)

        def nat_turn(h):
            pe.wait_ge(S["nat_p"], h + 1)
            if h == 0:
                pe.wait_ge(S["ret_copied"], 1)
            if h >= 2:
                pe.wait_ge(S["nat_pT"], h - 1)
            turn_probs(pp, h, 7 if h % 2 == 0 else 4, S["nat_turned"])

        def nat_out():
            pe.wait_ge(S["nat_pT"], HEADS)
            pe.wait_ge(pair_free[1], 4)
            pe.wait_ge(S["nat_masked"], HEADS)
            for h in range(HEADS):
                for i in range(NT):
                    for j in range(NT):
                        last = mm(ps[:, 5, i * 256 + h * 64:i * 256 + h * 64 + 64], ppT[:, h, j, i * P:(i + 1) * P],
                                  nv[:, j, h * 64:h * 64 + 64], start=j == 0, stop=j == NT - 1)
            last.then_inc(S["nat_out"], 1)

        def dif_scores(h):
            b0 = 6 if h == 0 else 4
            if h == 0:
                pe.wait_ge(pair_free[0], 6)
                pe.wait_ge(pair_free[1], 6)
                pe.wait_ge(S["nat_masked"], HEADS)
                pe.wait_ge(S["nat_pT"], HEADS)
            elif h == 1:
                pe.wait_ge(S["nat_y"], 1)
            else:
                pe.wait_ge(S["dif_biased"], 2 * h)
            for s in range(2):
                for i in range(NT):
                    last = mm(ps[:, b0 + s, i * TOKENS:(i + 1) * TOKENS], dqT[64 * s:64 * s + 64, h, i * P:(i + 1) * P],
                              dkT[64 * s:64 * s + 64, h, :], start=True, stop=True)
            last.then_inc(S["dif_scores"], 1)

        def dif_turn(h):
            pe.wait_ge(S["dif_a"], h + 1)
            if h >= 2:
                pe.wait_ge(S["dif_aT"], h - 1)
            turn_probs(pp, h, 6 + h % 2, S["dif_turned"])

        def dif_out():
            pe.wait_ge(S["dif_aT"], HEADS)
            pe.wait_ge(S["dif_biased"], 2 * HEADS)
            pe.wait_ge(pair_free[0], 8)
            for i in range(NT):
                for h in range(HEADS):
                    for j in range(NT):
                        last = mm(ps[:, 4 + i, h * P:(h + 1) * P], ppT[:, h, j, i * P:(i + 1) * P],
                                  dv[:, j, h * P:(h + 1) * P], start=j == 0, stop=j == NT - 1)
            last.then_inc(S["dif_out"], 1)

        def kc_turn():
            pe.wait_ge(S["km_ready"], 1)
            pe.wait_ge(S["dif_aT"], HEADS)
            for d in range(2):
                for c in range(2):
                    for t in range(NT):
                        last = nc.tensor.transpose(ps[:, 6 + d, c * TOKENS + t * P:c * TOKENS + t * P + P],
                                                   kTM[:, t, d * 256 + c * P:d * 256 + c * P + P], ident[:])
            last.then_inc(S["kc_turned"], 1)

        def seg_sums(lv):
            if lv == 0:
                pe.wait_ge(S["seg_landed"], 48)
                pe.wait_ge(S["logf_ready"], NT)
                pe.wait_ge(S["dif_copied"], NT)
            else:
                pe.wait_ge(S["seg_exp"], 2 * lv)
            for d in range(2):
                for c in range(2):
                    for t in range(NT):
                        last = mm(ps[:, 4 + d, c * TOKENS + t * P:c * TOKENS + t * P + P],
                                  logf[:, t, d * 256 + c * P:d * 256 + c * P + P],
                                  seg0[:, d, t] if lv == 0 else seg[:, d, lv - 1], start=True, stop=True)
            last.then_inc(S["seg_sums"], 1)

        def hg_scores(lv):
            pe.wait_ge(S["qk_ready"], lv + 1)
            if lv == 0:
                pe.wait_ge(S["kc_ready"], 2)
            elif lv == 1:
                pe.wait_ge(S["hg_off"], 2)
            else:
                pe.wait_ge(S["hg_masked"], 2 * (lv - 1))
            for x in range(2):
                ti = 1 - x if lv == 0 else x
                for h in range(HEADS):
                    o = (2 * x + h // 2) * P
                    dst = ps[:, 6 + h % 2, o:o + P]
                    rows = slice(64 * (h % 2), 64 * (h % 2) + 64)
                    kk, qq = slice(x * P, (x + 1) * P), slice(ti * P, (ti + 1) * P)
                    q = hq[rows, h // 2, qq] if lv == DIAG else Qb[rows, lv % 2, h // 2, qq]
                    last = mm(dst, Kb[rows, lv % 2, h // 2, kk], q, start=True, stop=True)
            last.then_inc(S["hg_scores"], 1)

        def hg_out():
            pe.wait_ge(S["hg_added"], LEVELS - 2)
            pe.wait_ge(S["seg_exp"], 2 * DIAG)
            for h in range(HEADS):
                for i in range(NT):
                    for j in range(NT):
                        s = (accS if i == j else offd)[:, h % 2, j, h // 2]
                        last = mm(ps[:, 4, i * 256 + h * 64:i * 256 + h * 64 + 64], s, hv[:, j, h * 64:h * 64 + 64],
                                  start=j == 0, stop=j == NT - 1)
            last.then_inc(S["hg_out"], 1)

        after = {
            2: [ret_scores], 4: [ret_out], 6: [lambda: nat_scores(0), lambda: nat_scores(1)],
            8: [lambda: nat_turn(0), lambda: nat_turn(1)], 9: [lambda: nat_scores(2), lambda: nat_scores(3)],
            11: [lambda: nat_turn(2), lambda: nat_turn(3)], 12: [nat_out],
            13: [lambda: dif_scores(0)], 14: [lambda: dif_scores(1)], 16: [lambda: dif_turn(0), lambda: dif_scores(2)],
            17: [lambda: dif_turn(1)], 18: [lambda: dif_scores(3)], 20: [lambda: dif_turn(2)],
            21: [lambda: dif_turn(3)], 22: [dif_out, kc_turn, lambda: seg_sums(0)], 32: [hg_out],
        }
        pe.wait_ge(S["ident_landed"], 16)
        turn(h0, S["h_ready"], S["h_turned"], 0)
        pe.wait_ge(S["aT_lo"], NT)
        for n in range(N_PROJ):
            project(n)
            for task in after.get(n, ()):
                task()
            if 23 <= n < 23 + LEVELS:
                hg_scores(n - 23)
                if n - 22 < DIAG:
                    seg_sums(n - 22)

        def turn_y(rnd):
            tile, bank = Y_ROUNDS[rnd]
            for q in (tile, tile + 1):
                for t in range(NT):
                    last = nc.tensor.transpose(ps[:, bank, (q % 2) * TOKENS + t * P:(q % 2) * TOKENS + t * P + P],
                                               y[:, t, 256 * (q // 2) + q % 2:256 * (q // 2) + 256:2], ident[:])
            last.then_inc(S["y_turned"], 1)

        pe.wait_ge(S["y_ready"], 2)
        pe.wait_ge(S["nat_y"], 1)
        pe.wait_ge(S["hg_copied"], 1)
        for rnd in range(len(Y_ROUNDS) - 1):
            turn_y(rnd)
        pe.wait_ge(S["yT_lo"], 1)
        for c in range(N_BR):
            n = N_PROJ + c
            b = min(c, 3)
            pe.wait_ge(S["lo_done"], n + 1)
            if c == 0:
                pe.wait_ge(pair_free[0], 2 * ((NB + 1) // 2))
                pe.wait_ge(pair_free[1], 2 * (NB // 2))
            elif c == 1:
                pe.wait_ge(S["yT_lo"], len(Y_ROUNDS))
            elif 2 <= c <= 3:
                pe.wait_ge(S["mul_ready"], 4 * (c - 1))
            wv = [split_part(i, n % 3).rearrange("p (j c) -> p j c", j=2) for i in range(2)]
            for dt in range(KD):
                bank = 4 * (b % 2) + dt // 2
                for j in range(2):
                    for a, w in PASSES:
                        last = mm(ps[:, bank, (dt % 2) * TOKENS:(dt % 2 + 1) * TOKENS], wv[w][:, j, dt * P:(dt + 1) * P],
                                  yT[:, a, 2 * c + j, :], start=c != 4 and dt % 2 == 0 and j == 0 and (a, w) == PASSES[0],
                                  stop=c != 3 and j == 1 and (a, w) == PASSES[-1], skip_group_check=True)
                if c == 0 and dt == 3:
                    pe.wait_ge(S["y_ready"], 3)
                    turn_y(len(Y_ROUNDS) - 1)
                if c == 4 and dt in (1, 3, 5):
                    last.then_inc(S["bank_ready"], 1)
            last.then_inc(S["pe_used"], 1)
        for c in range(N_OUT):
            n = N_PROJ + N_BR + c
            pe.wait_ge(S["lo_done"], n + 1)
            pe.wait_ge(S["mg_lo"], c + 1)
            wv = [split_part(i, n % 3).rearrange("p (k c) -> p k c", k=2) for i in range(2)]
            for t in range(NT):
                for half in range(2):
                    for k in range(2):
                        for a, w in PASSES:
                            last = mm(ps[:, 2 * t + half, :], aT[:, a, 2 * c + k, t * P:(t + 1) * P],
                                      wv[w][:, k, half * 512:(half + 1) * 512],
                                      start=c == 0 and k == 0 and (a, w) == PASSES[0],
                                      stop=c == N_OUT - 1 and k == 1 and (a, w) == PASSES[-1], skip_group_check=True)
                if c == N_OUT - 1 and t == 0:
                    last.then_inc(S["out_first"], 1)
            last.then_inc(S["pe_used"], 1)

        turn(zz, S["h_ready"], S["h_turned"], NT)
        def gate_up(bank, lhs, half, slot):
            for k in range(4):
                for a, w in PASSES:
                    wv = split_part(w, slot).rearrange("p (j k c) -> p k j c", j=2, k=4)
                    last = mm(ps[:, bank, :].rearrange("p (j c) -> p j c", j=2), lhs(a, 4 * half + k), wv[:, k],
                              start=half == 0 and k == 0 and (a, w) == PASSES[0],
                              stop=half == 1 and k == 3 and (a, w) == PASSES[-1], skip_group_check=True)
            return last

        def dense_gate_up(t, half, slot):
            return gate_up(4 + t, lambda a, k: aT[:, a, k, t * P:(t + 1) * P], half, slot)

        def dense_turn(hid_done, done, count):
            for t in range(NT):
                pe.wait_ge(hid_done, count * 2 + t - 1)
                for j in range(2):
                    last = nc.tensor.transpose(ps[:, 6 + t, j * P:(j + 1) * P], hid[:, t, j::2], ident[:])
                last.then_inc(done, 1)

        def dense_down(slot, first):
            for t in range(NT):
                for half in range(2):
                    for j in range(2):
                        for a, w in PASSES:
                            wv = split_part(w, slot).rearrange("p (j c) -> p j c", j=2)
                            last = mm(ps[:, 2 * t + half, :], hTs[:, a, t, j, :], wv[:, j, half * 512:(half + 1) * 512],
                                      start=first and j == 0 and (a, w) == PASSES[0],
                                      stop=j == 1 and (a, w) == PASSES[-1], skip_group_check=True)
            return last

        def route():
            pe.wait_ge(S["wr_lo"], 1)
            for k in range(KD):
                for a, w in PASSES:
                    last = mm(ps[0:64, 6, 0:TOKENS], wrs[:, w, k, :], aT[:, a, k, :],
                              start=k == 0 and (a, w) == PASSES[0], stop=k == KD - 1 and (a, w) == PASSES[-1])
            last.then_inc(S["logits"], 1)

        pe.wait_ge(S["aT_lo"], 2 * NT)
        route()
        for half in range(2):
            pe.wait_ge(S["lo_done"], NM + half + 1)
            for t in range(NT):
                last = dense_gate_up(t, half, (NM + half) % 3)
                if half == 0 and t == 0:
                    pe.wait_ge(S["scores_expert"], 1)
                    for u in range(NT):
                        turned = nc.tensor.transpose(ps[:, 6, 256 + u * 64:320 + u * 64], scT[0:64, u * P:(u + 1) * P], ident[0:64, 0:64])
                    turned.then_inc(S["scores_turned"], 1)
            last.then_inc(S["pe_used"], 1)
        pe.wait_ge(S["mask_ready"], 1)
        pe.wait_ge(S["out_read"], NT)
        pe.wait_ge(S["router_landed"], 80)
        msk0, msk1 = tk[:, 640:704], tk[:, 704:768]
        up, ones = up_ones[:, 0], up_ones[:, 1]
        mm(ps[:, 0, 0:64], up, msk0, start=True, stop=True)
        mm(ps[:, 0, 64:128], ones, msk0, start=True, stop=False)
        mm(ps[:, 0, 64:128], up, msk1, start=False, stop=True)
        mm(ps[:, 0, 128:192], ones, msk0, start=True, stop=False)
        mm(ps[:, 0, 128:192], ones, msk1, start=False, stop=True).then_inc(S["ranks"], 1)
        pe.wait_ge(S["scores_ready"], 1)
        dense_turn(S["sh_hid"], S["sh_turned"], 1)
        pe.wait_ge(S["sh_lo"], NT)
        pe.wait_ge(S["lo_done"], NM + 3)
        pe.wait_ge(S["ranks_read"], 1)
        dense_down((NM + 2) % 3, first=True).then_inc(S["pe_used"], 1)

        def gather(group, kk, a, bank):
            for k in range(2):
                for t in range(NT):
                    last = mm(ps[:, bank, k * 2 * P:(k + 1) * 2 * P], h1s[:, a, t, 2 * kk + k::KD], sel[:, group, t],
                              start=t == 0, stop=t == NT - 1)
            last.then_inc(S["gathered"], 1)

        def turn_hidden(e, bank):
            for j in range(2):
                last = nc.tensor.transpose(ps[:, bank, j * P:(j + 1) * P], hid[:, e, j::2], ident[:])
            return last

        def own_sel(r, t):
            return sel[:, r // 2, t, (r % 2) * P:(r % 2 + 1) * P]

        def sum_weights(q, r):
            for t in range(NT):
                w = wc[:, t].rearrange("p q c -> p (q c)")
                w = w[:, 0:6] if isinstance(q, int) and q == 0 else w[:, bass.ds(q * 6, 6)]
                last = mm(ps[:, 5, 256:262], own_sel(r, t), w, start=t == 0, stop=t == NT - 1)
            last.then_inc(S["weights_summed"], 1)

        def scatter_half(parity, half):
            for t in range(NT):
                for a in range(2):
                    last = mm(ps[:, 2 * t + half, :], selT[:, parity, t], ys[:, a, half * 512:(half + 1) * 512],
                              start=False, stop=a == 1, skip_group_check=True)
            return last

        def scatter(parity):
            scatter_half(parity, 0)
            scatter_half(parity, 1).then_inc(S["scattered"], 1)

        def half_gate_up(q, v, bank, half, r):
            pe.wait_ge(S["lo_done"], step_chunk(q, v) + 1)
            gate_up(bank, lambda a, k: xg[r // 2][:, a, k, (r % 2) * P:(r % 2 + 1) * P], half, split_slot(v)).then_inc(S["pe_used"], 1)

        def down(q, v0, experts=(0, 1)):
            for e in experts:
                pe.wait_ge(S["hid_lo"], q * 2 + (e - 1))
                pe.wait_ge(S["lo_done"], step_chunk(q, v0 + e) + 1)
                wv = [split_part(i, split_slot(v0 + e)).rearrange("p (j c) -> p j c", j=2) for i in range(2)]
                for half in range(2):
                    for j in range(2):
                        for a, w in PASSES:
                            last = mm(ps[:, 6 + half, :], hTs[:, a, e, j, :], wv[w][:, j, half * 512:(half + 1) * 512],
                                      start=e == 0 and j == 0 and (a, w) == PASSES[0],
                                      stop=e == 1 and j == 1 and (a, w) == PASSES[-1], skip_group_check=True)
                    if experts == (1,) and half == 0:
                        last.then_inc(S["half_down"], 1)
                last.then_inc(S["pe_used"], 1)

        def pair_step(q, r, first=False, gathers=True, last=False):
            a1 = 2 if first else 0
            nxt, kk = 1 - r // 2, 2 * (r % 2)
            if not last:
                pe.wait_ge(S["gather_hi"], 4 if first else q * 2 + 3)
                pe.wait_ge(S["gather_lo"], 4 if first else q * 2 + 3)
            else:
                pe.wait_ge(S["hid_lo"], q * 2 - 1)
                pe.wait_ge(S["selT_ready"], q)
            half_gate_up(q, a1, 4, 0, r)
            if not first:
                pe.wait_ge(S["pair_hid"], q * 2)
                turn_hidden(1, 5)
            else:
                pe.wait_ge(S["wc_lo"], 1)
            sum_weights(q, r)
            if not last:
                pe.wait_ge(S["gather_hi"], q * 2 + 4)
                pe.wait_ge(S["gather_lo"], q * 2 + 4)
            half_gate_up(q, a1 + 1, 4, 1, r)
            if not first:
                down(q, 2)
            if first:
                pe.wait_ge(S["parts_ready"], 1)
                half_gate_up(q, 4, 5, 0, r)
            pe.wait_ge(S["pair_hid"], q * 2 + 1)
            turn_hidden(0, 4)
            for t in range(NT):
                turned = mm(ps[:, 4, 256 + t * P:256 + (t + 1) * P], own_sel(r, t), ident_r[:], start=True, stop=True)
            turned.then_inc(S["slots_turned"], 1)
            if not first:
                pe.wait_ge(S["parts_ready"], q + 1)
                half_gate_up(q, 4, 5, 0, r)
            if gathers:
                if r % 2 == 0:
                    pe.wait_ge(S["sel_ready"], q + 4)
                pe.wait_ge(S["hid_lo"], q * 2 + 1)
                pe.wait_ge(S["selT_ready"], q + 1)
                gather(nxt, kk, 0, 4)
                if not first:
                    pe.wait_ge(S["y_lo"], q * 2 - 1)
                gather(nxt, kk, 1, 6)
            half_gate_up(q, 5, 5, 1, r)
            if gathers:
                if not first:
                    pe.wait_ge(S["y_lo"], q * 2)
                gather(nxt, kk + 1, 0, 7)
                pe.wait_ge(S["gather_lo"], q * 2 + 5)
                gather(nxt, kk + 1, 1, 6)
            if not first:
                pe.wait_ge(S["y_lo"], q * 2)
                pe.wait_ge(S["selT_ready"], q)
                scatter((r + 1) % 2)

        pe.wait_ge(S["sel_ready"], 2)
        pe.wait_ge(S["ident_ready"], 1)
        pe.wait_ge(S["h1s_lo"], 1)
        pe.wait_ge(S["sh_hid"], NT)
        pe.wait_ge(S["sh_lo"], NT)
        for kk in range(4):
            for a in range(2):
                if kk >= 2:
                    pe.wait_ge(S["gather_lo" if a else "gather_hi"], kk - 1)
                gather(0, kk, a, FIRST_BANKS[a][kk % 2])

        pair_step(0, 0, first=True)
        with pe.Fori(0, (PAIRS - 4) // 4) as i:
            for u in range(4):
                pair_step(i * 4 + (1 + u), (1 + u) % 4)
        for q in range(PAIRS - 3, PAIRS):
            pair_step(q, q % 4, gathers=q < PAIRS - 2, last=q == PAIRS - 1)
        pe.wait_ge(S["y_lo"], 2 * PAIRS - 2)
        down(PAIRS, 0, experts=(0,))
        pe.wait_ge(S["pair_hid"], 2 * PAIRS)
        turn_hidden(1, 5).then_inc(S["weights_summed"], 1)
        down(PAIRS, 0, experts=(1,))
        pe.wait_ge(S["selT_ready"], PAIRS)
        for half in range(2):
            pe.wait_ge(S["y_lo"], 2 * PAIRS - 1 + half)
            last = scatter_half((PAIRS - 1) % 2, half)
        last.then_inc(S["scattered"], 1)

        with if_over(pe):
            with pe.Fori(0, N_EXPERTS) as e:
                pe.wait_ge(S["fb_split_lo"], e + 1)
                for half in range(2):
                    for t in range(NT):
                        last = dense_gate_up(t, half, half)
                last.then_inc(S["fb_gate_up"], 1)
                dense_turn(S["fb_hid"], S["fb_turned"], e + 1)
                pe.wait_ge(S["fb_lo"], e * 2 + 2)
                dense_down(2, first=False).then_inc(S["fb_down"], 1)

    @block.scalar
    def _(act):
        one = Steps(act, S["act_step"])
        A_ = nc.scalar.activation

        for j, v in enumerate(("ln_in_g", "ln_in_b")):
            act.dma_start(lnb[:, j], dram(A[v], 0, [[0, P], [1, D]])).then_inc(S["lnin_landed"], 16)
        act.dma_start(ident[:], A["c_ident"]).then_inc(S["ident_landed"], 16)
        act.dma_start(retM[:], A["c_ret"]).then_inc(S["ret_landed"], 16)
        for dst, src in ((lamv[:], dram(A["diff_lambda"], 0, [[0, P], [1, 256]])),
                         (gnr[:], dram(A["ret_gn"], 0, [[0, P], [1, 256]])),
                         (gnh[:], dram(A["hgrn_gn"], 0, [[0, P], [1, 256]])),
                         (gnd[:], dram(A["diff_subln"], 0, [[0, P], [1, 512]])),
                         (bg[:], A["b_gate"])):
            act.dma_start(dst, src).then_inc(S["vec_landed"], 16)
        act.dma_start(dist[:], A["c_dist"]).then_inc(S["nat_landed"], 16)
        act.dma_start(natm[:], A["c_nat"]).then_inc(S["nat_landed"], 16)
        act.dma_start(rev[:], A["c_rev"]).then_inc(S["nat_landed"], 16)

        def high(n, rslot, slot, landed):
            act.wait_ge(raw_landed[rslot], landed)
            if not isinstance(n, int) or n >= 3:
                act.wait_ge(S["pe_used"], n - 2)
            nc.scalar.copy(whi[:, slot], raw(rslot)).then_inc(S["hi_done"], 1)

        def high_m(n):
            if n < NM:
                high(n, raw_slot(n), n % 3, raw_count(n))

        def high_turned(count):
            for t in range(NT):
                act.wait_ge(S["h_turned"], count + t + 1)
                if count:
                    act.wait_ge(S["pe_used"], NM)
                for b in range(2):
                    last = nc.scalar.copy(aT[:, 0, 4 * b:4 * b + 4, t * P:(t + 1) * P],
                                          ps[:, 4 + 2 * t + b, :].rearrange("p (k c) -> p k c", k=4))
                last.then_inc(S["aT_hi"], 1)

        def tm(bank):
            return ps[:, bank, :]

        def evacuate(blk):
            pair = blk % 2
            b0, free = 2 * pair, pair_free[pair]
            b = W_IN_ORDER[blk] if blk < len(W_IN_ORDER) else 100 + blk - len(W_IN_ORDER)
            if b in (0, 2, 6, 7):
                return
            act.wait_ge(S["pe_used"], 2 * blk + 2)
            if b == 1:
                for t in range(NT):
                    nc.scalar.copy(rv[:, t], ps[:, b0 + t, 0:256])
                    A_(rg[:, t], ps[:, b0 + t, 256:512], ACT.Silu).then_inc(free, 1)
            elif b == 3:
                nc.scalar.copy(nv[:].rearrange("p t c -> p (t c)"), tm(b0)).then_inc(free, 1)
                A_(hq[:].rearrange("p t c -> p (t c)"), tm(b0 + 1), ACT.Silu).then_inc(free, 1)
            elif b == 8:
                for t in range(NT):
                    nc.scalar.copy(dv[:, t], tm(b0 + t)).then_inc(free, 1)
            elif b == 4:
                for t in range(NT):
                    A_(kTM[:, t], tm(b0 + t), ACT.Sigmoid, scale=-1.0)
                    A_(logf[:, t], tm(b0 + t), ACT.Sigmoid).then_inc(free, 1)
            elif b == 5:
                for t in range(NT):
                    nc.scalar.copy(hv[:, t], ps[:, b0 + t, 0:256])
                    A_(hg[:, t], ps[:, b0 + t, 256:512], ACT.Silu).then_inc(free, 1)
            elif b >= 100:
                q = b - 100
                if q == 0:
                    act.wait_ge(S["km_ready"], 1)
                if q == 4:
                    act.wait_ge(S["dif_out"], 1)
                dst = (g0 if q < 4 else g1)
                for c in range(4):
                    ins = A_(dst[:, q % 4, c], ps[:, b0 + c // 2, (c % 2) * TOKENS:(c % 2 + 1) * TOKENS], ACT.Sigmoid,
                             bias=bg[:, 4 * q + c:4 * q + c + 1])
                    if c % 2 == 1:
                        ins.then_inc(free, 1)

        def copy_bank(dst, bank, wait, count, sem):
            act.wait_ge(wait, count)
            nc.scalar.copy(dst, ps[:, bank, :]).then_inc(sem, 1)

        def ret_copy():
            copy_bank(oo[:, 0:512], 4, S["ret_out"], 1, S["ret_copied"])
            act.dma_start(lbv[:], dram(A["hgrn_lb"], 0, [[0, P], [1, 512]])).then_inc(S["lb_landed"], 16)
            act.dma_start(seg[:], A["c_seg"]).then_inc(S["seg_landed"], 16)
            act.dma_start(seg0[:], A["c_seg0"]).then_inc(S["seg_landed"], 16)
            act.dma_start(msk[:], A["c_mask"]).then_inc(S["seg_landed"], 16)

        def lower_exp():
            act.wait_ge(S["lb_shift"], 1)
            A_(lb[:], lb[:], ACT.Exp).then_inc(S["lb_exp"], 1)

        def nat_exp(h):
            act.wait_ge(S["nat_max"], h + 1)
            for i in range(NT):
                last = A_(pp[:, h, i], pp[:, h, i], ACT.Exp, bias=small[:, 2 * h + i:2 * h + i + 1],
                          accum_out=small[:, 8 + 2 * h + i:9 + 2 * h + i])
            last.then_inc(S["nat_exp"], 1)

        def nat_copy(h):
            copy_bank(ppT[:, h].rearrange("p j i -> p (j i)"), 7 if h % 2 == 0 else 4, S["nat_turned"], h + 1, S["nat_pT"])

        def nat_y():
            act.wait_ge(S["nat_out"], 1)
            nc.scalar.copy(y[:, :, 256:512], ps[:, 5, :].rearrange("p (t c) -> p t c", t=2)).then_inc(S["nat_y"], 1)

        def dif_exp(h):
            act.wait_ge(S["dif_max"], h + 1)
            for s in range(2):
                for i in range(NT):
                    c = 32 + 8 * h + 2 * s + i
                    last = A_(ee[:, h % 2, s, i], ee[:, h % 2, s, i], ACT.Exp, bias=small[:, c:c + 1],
                              accum_out=small[:, c + 4:c + 5])
            last.then_inc(S["dif_exp"], 1)

        def dif_copy(h):
            copy_bank(ppT[:, h].rearrange("p j i -> p (j i)"), 6 + h % 2, S["dif_turned"], h + 1, S["dif_aT"])

        def dif_o():
            act.wait_ge(S["dif_out"], 1)
            act.wait_ge(S["y_ready"], 1)
            for i in range(NT):
                nc.scalar.copy(oo[:, 512 * i:512 * i + 512], ps[:, 4 + i, :]).then_inc(S["dif_copied"], 1)

        def lam_exp():
            act.wait_ge(S["lam_sums"], 2)
            A_(small[:, 66:68], small[:, 64:66], ACT.Exp).then_inc(S["lam_exps"], 1)

        def log_f():
            for t in range(NT):
                act.wait_ge(S["f_ready"], t + 1)
                A_(logf[:, t], logf[:, t], ACT.Ln).then_inc(S["logf_ready"], 1)

        def kc_copy():
            act.wait_ge(S["kc_turned"], 1)
            for d in range(2):
                nc.scalar.copy(kc[:, d].rearrange("p c t -> p (c t)"), ps[:, 6 + d, :]).then_inc(S["kc_ready"], 1)

        def seg_exp(lv):
            if lv == 0:
                act.wait_ge(S["kc_ready"], 2)
                act.wait_ge(S["kc_turned"], 1)
            if lv >= 2:
                act.wait_ge(S["qk_ready"], lv - 1)
            act.wait_ge(S["seg_sums"], lv + 1)
            for d in range(2):
                A_(Eb[:, lv % 2, d].rearrange("p c t -> p (c t)"), ps[:, 4 + d, :], ACT.Exp).then_inc(S["seg_exp"], 1)

        def hg_off():
            act.wait_ge(S["hg_scores"], 1)
            act.wait_ge(S["dif_out"], 1)
            for x in range(2):
                nc.scalar.copy(offd[:, x].rearrange("p x h i -> p (x h i)"), ps[:, 6 + x, :]).then_inc(S["hg_off"], 1)

        def hg_copy():
            act.wait_ge(S["qk_ready"], LEVELS)
            act.wait_ge(S["hg_out"], 1)
            nc.scalar.copy(oo[:, 0:512], ps[:, 4, :]).then_inc(S["hg_copied"], 1)

        after = {
            4: [ret_copy], 6: [lambda: nat_exp(0), lambda: nat_exp(1)], 8: [lambda: nat_copy(0), lambda: nat_copy(1)],
            9: [lam_exp, lower_exp, lambda: nat_exp(2), lambda: nat_exp(3)], 11: [lambda: nat_copy(2), lambda: nat_copy(3)],
            12: [nat_y], 14: [lambda: dif_exp(0)],
            15: [lambda: dif_exp(1)], 17: [lambda: dif_copy(0), lambda: dif_exp(2)], 18: [lambda: dif_copy(1), lambda: dif_exp(3)],
            20: [log_f, lambda: dif_copy(2)], 21: [lambda: dif_copy(3)],
            22: [dif_o, kc_copy, lambda: seg_exp(0)], 23: [hg_off], 32: [hg_copy],
        }
        high_m(0)
        high_turned(0)
        high_m(1)
        act.wait_ge(S["h_ready"], NT)
        for r in (0, 64):
            act.dma_start(hk[r:r + 64], dram(A["rpb"], 0, [[1, 64], [127, HEADS * 7], [1, 64]])).then_inc(S["nat_landed"], 16)
        for n in range(N_PROJ):
            high_m(n + 2)
            if n % 2 == 1:
                evacuate(n // 2)
            for task in after.get(n, ()):
                task()
            if 23 <= n < 23 + DIAG - 1:
                seg_exp(n - 22)

        def high_y(rnd):
            act.wait_ge(S["y_turned"], rnd + 1)
            tile, bank = Y_ROUNDS[rnd]
            last = nc.scalar.copy(yT[:, 0, tile:tile + 2, :], ps[:, bank, :].rearrange("p (q t) -> p q t", q=2))
            last.then_inc(S["yT_hi"], 1)

        for rnd in range(len(Y_ROUNDS)):
            high_y(rnd)
        for n in range(N_PROJ + 2, NM):
            high_m(n)
            if n == N_PROJ + N_BR + 1:
                act.wait_ge(S["pe_used"], N_PROJ)
                for g in range(4):
                    act.wait_ge(S["br_read"], 9 + g)
                    nc.scalar.copy(aT[:, 0, 2 * g:2 * g + 2].rearrange("p k t -> p (k t)"),
                                   mg[:, 2 * g:2 * g + 2].rearrange("p k t -> p (k t)")).then_inc(S["mg_hi"], 1)
        act.wait_ge(S["router_landed"], 80)
        nc.scalar.copy(wrs[:, 0], wr[:]).then_inc(S["wr_hi"], 1)
        for n in range(NM, NM + 3):
            high(n, raw_slot(n), n % 3, raw_count(n))
        high_turned(NT)
        nc.scalar.copy(h1s[:, 0].rearrange("p t c -> p (t c)"), zz[:].rearrange("p t c -> p (t c)")).then_inc(S["h1s_hi"], 1)
        act.wait_ge(S["logits"], 1)
        A_(scT[0:64], ps[0:64, 6, 0:TOKENS], ACT.Sigmoid).then_inc(S["scores_expert"], 1)
        act.wait_ge(S["scores_turned"], 1)
        nc.scalar.copy(tk[:, 0:128], ps[:, 6, 256:384]).then_inc(S["scores_ready"], 1)

        def dense_silu(done, count):
            for t in range(NT):
                A_(sil[:, t], ps[:, 4 + t, 0:HID], ACT.Silu).then_inc(done, 1)

        def dense_high(turned, done, count):
            for t in range(NT):
                act.wait_ge(turned, count * 2 + t - 1)
                nc.scalar.copy(hTs[:, 0, t], ps[:, 6 + t, 0:256].rearrange("p (j c) -> p j c", j=2)).then_inc(done, 1)

        act.wait_ge(S["pe_used"], NM + 2)
        dense_silu(S["sh_silu"], 1)
        dense_high(S["sh_turned"], S["sh_hi"], 1)
        act.wait_ge(S["comb_ready"], 1)
        nc.scalar.copy(wc[:, :, :, 0:2], comb[:].rearrange("p t (q e) -> p t q e", e=2)).then_inc(S["wc_hi"], 1)
        nc.scalar.copy(ident_r[:], ident[:]).then_inc(S["ident_ready"], 1)
        for n in range(NM + 3, NM + 5):
            high(n, raw_slot(n), n % 3, raw_count(n))

        def gather_high(count, group, kk, bank):
            act.wait_ge(S["gathered"], count)
            nc.scalar.copy(xg[group][:, 0, 2 * kk:2 * kk + 2, :].rearrange("p k s -> p (k s)"), ps[:, bank, :]).then_inc(S["gather_hi"], 1)

        def step_high(q, v):
            slot = step_slot(v)
            high(step_chunk(q, v), slot, split_slot(v), q * 32 + raw_count(NM + 1 + v))

        def hidden_high(q, e):
            act.wait_ge(S["weights_summed" if e else "slots_turned"], q + (1 + e))
            nc.scalar.copy(hTs[:, 0, e].rearrange("p j c -> p (j c)"), ps[:, 4 + e, 0:256]).then_inc(S["hid_hi"], 1)

        def outputs_high(used, final=False):
            if not final:
                act.wait_ge(S["pe_used"], used)
            for half in range(2):
                if final and half == 0:
                    act.wait_ge(S["half_down"], 1)
                elif final:
                    act.wait_ge(S["pe_used"], used)
                nc.scalar.copy(ys[:, 0, half * 512:(half + 1) * 512], ps[:, 6 + half, :]).then_inc(S["y_hi"], 1)

        def silu(q, e, used):
            act.wait_ge(S["pe_used"], used)
            A_(sil[:, e], ps[:, 4 + e, 0:HID], ACT.Silu).then_inc(S["pair_silu"], 1)

        def pair_step(q, r, first=False, last=False):
            if not first:
                silu(q + (-1), 1, step_chunk(q, 0))
                if not last:
                    gather_high(q * 4 + 7, 1 - (r - 1) % 4 // 2, 2 * ((r + 1) % 2) + 1, 7)
                step_high(q, 2)
                act.wait_ge(S["cw_ready"], q)
            if first:
                step_high(q, 4)
            act.wait_ge(S["weights_summed"], q + 1)
            nc.scalar.copy(cw_parts, ps[:, 5, 256:262]).then_inc(S["parts_ready"], 1)
            if not first:
                hidden_high(q + (-1), 1)
                step_high(q, 3)
            silu(q, 0, step_chunk(q, 4 if first else 2))
            if not first:
                step_high(q, 4)
            step_high(q, 5)
            if not first:
                outputs_high(step_chunk(q, 4))
            act.wait_ge(S["slots_turned"], q + 1)
            nc.scalar.copy(selT[:, r % 2].rearrange("p t c -> p (t c)"), ps[:, 4, 256:512]).then_inc(S["selT_ready"], 1)
            hidden_high(q, 0)
            step_high(q + 1, 0)

        def next_slots(q, r):
            gather_high(q * 4 + 9, 1 - r // 2, 2 * (r % 2), 4)
            step_high(q + 1, 1)

        for kk in range(4):
            gather_high(2 * kk + 1, 0, kk, FIRST_BANKS[0][kk % 2])
        pair_step(0, 0, first=True)
        next_slots(0, 0)
        with act.Fori(0, (PAIRS - 4) // 4) as i:
            for u in range(4):
                pair_step(i * 4 + (1 + u), (1 + u) % 4)
                next_slots(i * 4 + (1 + u), (1 + u) % 4)
        for q in range(PAIRS - 3, PAIRS):
            pair_step(q, q % 4, last=q == PAIRS - 1)
            if q < PAIRS - 2:
                next_slots(q, q % 4)
            else:
                step_high(q + 1, 1)
        silu(PAIRS - 1, 1, step_chunk(PAIRS, 0))
        hidden_high(PAIRS - 1, 1)
        outputs_high(step_chunk(PAIRS, 2), final=True)

        with if_over(act):
            with act.Fori(0, N_EXPERTS) as e:
                act.wait_ge(S["fb_landed"], e * 96 + 96)
                for c in range(3):
                    last = nc.scalar.copy(whi[:, c], rawL[:, c])
                last.then_inc(S["fb_split_hi"], 1)
                act.wait_ge(S["fb_gate_up"], e + 1)
                dense_silu(S["fb_silu"], e + 1)
                dense_high(S["fb_turned"], S["fb_hi"], e + 1)

    @block.gpsimd
    def _(pool):
        nc.gpsimd.memset(pow_c[:], -0.5).then_inc(S["pool_step"], 1)
        pool.wait_ge(S["pool_step"], 1)
        norms = [0]

        def power(dst, src, w):
            norms[0] += 1
            pool.wait_ge(S["mv_ready"], norms[0])
            nc.gpsimd.tensor_tensor(dst, src, pow_c[:, 0:w], ALU.pow).then_inc(S["rstd_ready"], 1)

        for t in range(NT):
            power(small[:, 76 + t:77 + t], small[:, 74 + t:75 + t], 1)
        pool.wait_ge(S["vec_landed"], 80)
        pool.wait_ge(pair_free[1], 2)
        for t in range(NT):
            last = nc.gpsimd.tensor_tensor(rg[:, t], rg[:, t], gnr[:], ALU.mult)
        last.then_inc(S["gate_mul"], 1)
        power(small[:, 88:96], small[:, 80:88], 8)
        pool.wait_ge(S["lower_ready"], 1)
        pool.wait_ge(pair_free[1], 2 * 4)
        for t in range(NT):
            last = nc.gpsimd.tensor_tensor(logf[:, t], logf[:, t], om[:], ALU.mult)
        last.then_inc(S["pool_step"], 1)
        pool.wait_ge(S["pool_step"], 2)
        for t in range(NT):
            nc.gpsimd.tensor_tensor(logf[:, t], logf[:, t], lb[:], ALU.add).then_inc(S["forget_ready"], 1)
        for t in range(NT):
            last = nc.gpsimd.tensor_tensor(kTM[:, t], kTM[:, t], om[:], ALU.mult)
        last.then_inc(S["km_ready"], 1)
        power(small[:, 88:96], small[:, 80:88], 8)
        pool.wait_ge(pair_free[0], 2 * 5)
        for t in range(NT):
            last = nc.gpsimd.tensor_tensor(hg[:, t], hg[:, t], gnh[:], ALU.mult)
        last.then_inc(S["gate_mul"], 1)
        for lv in range(2, DIAG + 1):
            add_level(pool, lv)
        power(small[:, 88:96], small[:, 80:88], 8)
        for b in range(1, 4):
            for g in range(4):
                pool.wait_ge(S["mul_ready"], 4 * b + g + 1)
                src = mgt[:, g % 2].rearrange("p a t -> p (a t)")
                dst = mg[:, 2 * g:2 * g + 2].rearrange("p a t -> p (a t)")
                nc.gpsimd.tensor_tensor(dst, dst, src, ALU.add).then_inc(S["br_read"], 1)
        for t in range(NT):
            power(small[:, 76 + t:77 + t], small[:, 74 + t:75 + t], 1)
        def one_hot(q, r):
            pool.wait_ge(S["places_compared"], q + 1)
            nc.gpsimd.tensor_tensor(sel[:, r // 2, :, (r % 2) * P:(r % 2 + 1) * P], sel_one[:, 0], sel_one[:, 1], ALU.add).then_inc(S["sel_ready"], 1)

        def slot_weights(q, first=False):
            pool.wait_ge(S["parts_ready"], q + 1)
            parts = cw_parts
            nc.gpsimd.tensor_tensor(small[:, 412:414], parts[:, 0:2], parts[:, 2:4], ALU.add)
            nc.gpsimd.tensor_scalar(small[:, 414:416], parts[:, 4:6], slot_no[:, P:P + 1], None, ALU.is_equal).then_inc(S["cw_step"], 1)
            pool.wait_ge(S["cw_step"], q + 1)
            if not first:
                pool.wait_ge(S["pair_hid"], q * 2)
            nc.gpsimd.tensor_tensor(cw, small[:, 412:414], small[:, 414:416], ALU.mult).then_inc(S["cw_ready"], 1)

        pool.wait_ge(S["router_landed"], 80)
        for q in range(3):
            one_hot(q, q)
        slot_weights(0, first=True)
        one_hot(3, 3)
        with pool.Fori(0, (PAIRS - 4) // 4) as i:
            for u in range(4):
                q = i * 4 + (1 + u)
                slot_weights(q)
                pool.wait_ge(S["slots_turned"], q)
                one_hot(q + 3, u)
        for q in range(PAIRS - 3, PAIRS):
            slot_weights(q)
        for t in range(NT):
            power(small[:, 76 + t:77 + t], small[:, 74 + t:75 + t], 1)

    @block.vector
    def _(dve):
        one = Steps(dve, S["dve_step"])
        V = nc.vector
        norms = [0]

        def low(n, rslot, slot):
            dve.wait_ge(S["hi_done"], n + 1)
            V.tensor_tensor(wlo[:, slot], raw(rslot), whi[:, slot].bitcast(F32), ALU.subtract).then_inc(S["lo_done"], 1)

        def low_m(n):
            if n < NM:
                low(n, raw_slot(n), n % 3)

        def layer_norm(src, dst, gb, landed, landed_count, ready, waits=None):
            st = small[:, 128:128 + 24].rearrange("p (t s) -> p t s", t=NT)
            mv = small[:, 68:72].rearrange("p (t s) -> p t s", t=NT)
            for t in range(NT):
                if waits:
                    waits(t)
                for q in range(2):
                    one(V.bn_stats(st[:, t, 6 * q:6 * q + 6], src[:, t, 512 * q:512 * q + 512]))
                one(V.bn_aggr(mv[:, t], st[:, t]))
                V.tensor_scalar(small[:, 74 + t:75 + t], mv[:, t, 1:2], EPS, None, ALU.add).then_inc(S["mv_ready"], 1)
            dve.wait_ge(landed, landed_count)
            for t in range(NT):
                norms[0] += 1
                dve.wait_ge(S["rstd_ready"], norms[0])
                one(V.scalar_tensor_tensor(out=dst[:, t], in0=src[:, t], scalar=mv[:, t, 0:1], in1=gb[:, 0], op0=ALU.subtract, op1=ALU.mult))
                V.scalar_tensor_tensor(out=dst[:, t], in0=dst[:, t], scalar=small[:, 76 + t:77 + t], in1=gb[:, 1], op0=ALU.mult,
                                       op1=ALU.add).then_inc(ready, 1)

        def low_turned(count):
            for t in range(NT):
                dve.wait_ge(S["aT_hi"], count + t + 1)
                for b in range(2):
                    last = V.tensor_tensor(aT[:, 1, 4 * b:4 * b + 4, t * P:(t + 1) * P],
                                           ps[:, 4 + 2 * t + b, :].rearrange("p (k c) -> p k c", k=4),
                                           aT[:, 0, 4 * b:4 * b + 4, t * P:(t + 1) * P].bitcast(F32), ALU.subtract)
                last.then_inc(S["aT_lo"], 1)

        def evacuate(blk):
            pair = blk % 2
            b0, free = 2 * pair, pair_free[pair]
            if blk >= len(W_IN_ORDER):
                return
            b = W_IN_ORDER[blk]
            dst = {0: rqk, 2: nqk, 6: dqT, 7: dkT}.get(b)
            if dst is None:
                return
            dve.wait_ge(S["pe_used"], 2 * blk + 2)
            if b == 6:
                dve.wait_ge(S["ret_scores"], HEADS)
            for c in range(2):
                d = dst[:, 2 * c:2 * c + 2].rearrange("p c t -> p (c t)")
                f = SCALE if (b == 2 and c == 0) or b == 6 else 1.0
                V.tensor_scalar(d, ps[:, b0 + c, :], f, None, ALU.mult).then_inc(free, 1)

        def ret_decay():
            dve.wait_ge(S["ret_landed"], 16)
            for h in range(HEADS):
                dve.wait_ge(S["ret_scores"], h + 1)
                V.tensor_tensor(retS[:, h].rearrange("p j i -> p (j i)"), ps[:, 4 + h, :],
                                retM[:, h].rearrange("p j i -> p (j i)"), ALU.mult).then_inc(S["ret_decayed"], 1)

        def rms(width, gain, col, gains_ready):
            n = NT * HEADS * width
            o, sq = oo[:, 0:n], osq[:, 0:n]
            one(V.tensor_tensor(sq, o, o, ALU.mult))
            one(V.tensor_reduce(small[:, 96:104], sq.rearrange("p (g c) -> p g c", c=width), AX.X, ALU.add))
            norms[0] += 1
            V.tensor_scalar(small[:, 80:88], small[:, 96:104], 1.0 / width, EPS, ALU.mult, ALU.add).then_inc(S["mv_ready"], 1)
            dve.wait_ge(S["rstd_ready"], norms[0])
            r = small[:, 88:96].unsqueeze(2).to_broadcast([P, NT * HEADS, width])
            one(V.tensor_tensor(sq.rearrange("p (g c) -> p g c", c=width), o.rearrange("p (g c) -> p g c", c=width), r, ALU.mult))
            if gains_ready is not None:
                dve.wait_ge(S["gate_mul"], gains_ready)
            w = HEADS * width
            V.tensor_tensor(y[:, :, col:col + w], sq.rearrange("p (t c) -> p t c", t=NT), gain, ALU.mult).then_inc(S["y_ready"], 1)

        def ret_norm():
            dve.wait_ge(S["ret_copied"], 1)
            rms(64, rg[:], 0, 1)

        def nat_mask(h):
            dve.wait_ge(S["nat_scores"], h + 1)
            V.tensor_tensor(pp[:, h], ps[:, 5 + h % 2, :].rearrange("p (i k) -> p i k", i=NT),
                            natm[:].unsqueeze(1).to_broadcast([P, NT, TOKENS]), ALU.add).then_inc(S["nat_masked"], 1)
            dve.wait_ge(S["nat_masked"], h + 1)
            V.tensor_reduce(small[:, 2 * h:2 * h + 2], pp[:, h], AX.X, ALU.max, negate=True).then_inc(S["nat_max"], 1)

        def nat_norm(h):
            dve.wait_ge(S["nat_exp"], h + 1)
            one(V.reciprocal(small[:, 16 + 2 * h:18 + 2 * h], small[:, 8 + 2 * h:10 + 2 * h]))
            for i in range(NT):
                last = V.tensor_scalar(pp[:, h, i], pp[:, h, i], small[:, 16 + 2 * h + i:17 + 2 * h + i], None, ALU.mult)
            last.then_inc(S["nat_p"], 1)

        def dif_bias(h):
            dve.wait_ge(S["dif_scores"], h + 1)
            b0 = 6 if h == 0 else 4
            slope = 2.0 ** (-8.0 * (h + 1) / HEADS)
            if h == 0:
                dve.wait_ge(S["nat_landed"], 80)
                dve.wait_ge(S["y_ready"], 1)
            if h >= 2:
                dve.wait_ge(S["dif_a"], h - 1)
            for s in range(2):
                V.scalar_tensor_tensor(out=ee[:, h % 2, s].rearrange("p i k -> p (i k)"), in0=dist[:].rearrange("p i k -> p (i k)"),
                                       scalar=-slope, in1=ps[:, b0 + s, :], op0=ALU.mult, op1=ALU.add).then_inc(S["dif_biased"], 1)
            dve.wait_ge(S["dif_biased"], 2 * h + 2)
            c = 32 + 8 * h
            V.tensor_reduce(small[:, c:c + 4], ee[:, h % 2].rearrange("p s i k -> p (s i) k"), AX.X, ALU.max,
                            negate=True).then_inc(S["dif_max"], 1)

        def dif_combine(h):
            dve.wait_ge(S["dif_exp"], h + 1)
            if h == 0:
                dve.wait_ge(S["nat_turned"], HEADS)
            c = 36 + 8 * h
            one(V.reciprocal(small[:, 104:108], small[:, c:c + 4]))
            one(V.tensor_scalar(small[:, 108:110], small[:, 106:108], small[:, 64:65], None, ALU.mult))
            for i in range(NT):
                last = V.tensor_scalar(ee[:, h % 2, 1, i], ee[:, h % 2, 1, i], small[:, 108 + i:109 + i], None, ALU.mult)
            one(last)
            for i in range(NT):
                last = V.scalar_tensor_tensor(out=pp[:, h, i], in0=ee[:, h % 2, 0, i], scalar=small[:, 104 + i:105 + i],
                                              in1=ee[:, h % 2, 1, i], op0=ALU.mult, op1=ALU.subtract)
            last.then_inc(S["dif_a"], 1)
            dve.wait_ge(S["dif_a"], h + 1)

        def lam_sums():
            dve.wait_ge(S["vec_landed"], 80)
            v = lamv[:].rearrange("p (a b c) -> p a b c", a=2, b=2)
            w = small[:, 256:384].rearrange("p (a c) -> p a c", a=2)
            one(V.tensor_tensor(w, v[:, :, 0], v[:, :, 1], ALU.mult))
            V.tensor_reduce(small[:, 64:66], w, AX.X, ALU.add).then_inc(S["lam_sums"], 2)
            one(V.tensor_scalar(gnd[:], gnd[:], 1.0 - LAM_INIT, None, ALU.mult))

        def lam():
            dve.wait_ge(S["lam_exps"], 1)
            one(V.tensor_tensor(small[:, 64:65], small[:, 66:67], small[:, 67:68], ALU.subtract))
            one(V.tensor_scalar(small[:, 64:65], small[:, 64:65], LAM_INIT, None, ALU.add))

        def dif_norm():
            dve.wait_ge(S["dif_copied"], NT)
            rms(P, gnd[:].unsqueeze(1).to_broadcast([P, NT, 512]), 768, None)

        def lower_shift():
            dve.wait_ge(S["lb_landed"], 16)
            V.tensor_tensor(lb[:], lbv[:], lbv[:], ALU.subtract).then_inc(S["lb_shift"], 1)

        def lower():
            dve.wait_ge(S["lb_exp"], 1)
            one(V.reciprocal(lbv[:], lb[:]))
            one(V.tensor_tensor(lbv[:], lb[:], lbv[:], ALU.mult))
            one(V.tensor_tensor(lb[:], lbv[:], lbv[:], ALU.subtract))
            V.tensor_scalar(om[:], lb[:], -1.0, 1.0, ALU.mult, ALU.add).then_inc(S["lower_ready"], 1)

        def floor_forget():
            for t in range(NT):
                dve.wait_ge(S["forget_ready"], t + 1)
                V.tensor_scalar(logf[:, t], logf[:, t], LOG_FLOOR, None, ALU.max).then_inc(S["f_ready"], 1)

        def queries_keys(lv):
            if lv == 0:
                dve.wait_ge(S["kc_ready"], 2)
            if lv == DIAG:
                dve.wait_ge(S["hg_scores"], lv - 1)
                V.tensor_tensor(Kb[:, lv % 2], kc[:, 0], kc[:, 1], ALU.add).then_inc(S["qk_ready"], 1)
                return
            dve.wait_ge(S["seg_exp"], 2 * lv + 2)
            if lv >= 2:
                dve.wait_ge(S["hg_scores"], lv - 1)
            half = P >> lv
            E, Q, K = Eb[:, lv % 2], Qb[:, lv % 2], Kb[:, lv % 2]
            for half_no in range(2):
                for src, e, dst in ((kc[:, half_no], E[:, half_no], K), (hq[:], E[:, 1 - half_no], Q)):
                    a, b, o = (v.rearrange("p c (b s m) -> p (c b) s m", s=2, m=half)[:, :, half_no] for v in (src, e, dst))
                    last = V.tensor_tensor(o, a, b, ALU.mult)
            last.then_inc(S["qk_ready"], 1)

        def mask_level(lv):
            dve.wait_ge(S["hg_scores"], lv + 1)
            if lv == 1:
                dve.wait_ge(S["y_ready"], 2)
            if lv >= 3:
                dve.wait_ge(S["hg_added"], lv - 2)
            mk = (ident[:] if lv == DIAG else msk[:, lv - 1]).unsqueeze(1).to_broadcast([P, HEADS, P])
            dst = accS if lv == 1 else tmpS
            for x in range(2):
                V.tensor_tensor(dst[:, x].rearrange("p x h i -> p (x h) i"), ps[:, 6 + x, :].rearrange("p (h i) -> p h i", h=HEADS), mk, ALU.mult).then_inc(S["hg_masked"], 1)

        def hg_norm():
            dve.wait_ge(S["hg_copied"], 1)
            rms(64, hg[:], 512, 2)

        after = {
            2: [ret_decay, lam_sums], 4: [ret_norm],
            6: [lambda: nat_mask(0), lambda: nat_mask(1), lambda: nat_norm(0), lambda: nat_norm(1)],
            9: [lambda: nat_mask(2), lambda: nat_mask(3), lambda: nat_norm(2), lambda: nat_norm(3)],
            8: [lower_shift], 10: [lam, lower], 14: [lambda: dif_bias(0)], 15: [lambda: dif_bias(1), lambda: dif_combine(0)],
            16: [lambda: dif_combine(1)], 17: [lambda: dif_bias(2)], 18: [lambda: dif_bias(3), lambda: dif_combine(2)],
            19: [lambda: dif_combine(3), floor_forget],
            23: [dif_norm], 32: [hg_norm],
        }
        layer_norm(xin, h0, lnb, S["lnin_landed"], 32, S["h_ready"], lambda t: dve.wait_ge(x_landed[t], 16))
        low_m(0)
        low_turned(0)
        low_m(1)
        for n in range(N_PROJ):
            if n < N_PROJ - 1:
                low_m(n + 2)
            if n % 2 == 1:
                evacuate(n // 2)
            for task in after.get(n, ()):
                task()
            if 22 <= n < 22 + LEVELS:
                queries_keys(n - 22)
            if 24 <= n < 24 + DIAG:
                mask_level(n - 23)

        for rnd in range(len(Y_ROUNDS)):
            dve.wait_ge(S["yT_hi"], rnd + 1)
            tile, bank = Y_ROUNDS[rnd]
            q = slice(tile, tile + 2)
            last = V.tensor_tensor(yT[:, 1, q, :], ps[:, bank, :].rearrange("p (q t) -> p q t", q=2),
                                   yT[:, 0, q, :].bitcast(F32), ALU.subtract)
            last.then_inc(S["yT_lo"], 1)
            if rnd == len(Y_ROUNDS) - 2:
                low_m(N_PROJ + 1)

        def merged_low(g):
            dve.wait_ge(S["mg_hi"], g + 1)
            V.tensor_tensor(aT[:, 1, 2 * g:2 * g + 2].rearrange("p k t -> p (k t)"), mg[:, 2 * g:2 * g + 2].rearrange("p k t -> p (k t)"),
                            aT[:, 0, 2 * g:2 * g + 2].rearrange("p k t -> p (k t)").bitcast(F32), ALU.subtract).then_inc(S["mg_lo"], 1)

        def merge(b):
            if b < 3:
                dve.wait_ge(S["pe_used"], N_PROJ + b + 1)
            for g in range(4):
                if b == 3 and g < 3:
                    dve.wait_ge(S["bank_ready"], g + 1)
                elif b == 3:
                    dve.wait_ge(S["pe_used"], N_PROJ + N_BR)
                gates = (g0 if b < 2 else g1)[:, (2 * b + g // 2) % 4, 2 * (g % 2):2 * (g % 2) + 2]
                if b == 0:
                    dst = mg[:, 2 * g:2 * g + 2]
                    if g == 0:
                        dve.wait_ge(S["y_turned"], 3)
                else:
                    if 4 * (b - 1) + g >= 2:
                        dve.wait_ge(S["br_read"], 4 * (b - 1) + g - 1)
                    dst = mgt[:, g % 2]
                V.tensor_tensor(dst.rearrange("p a t -> p (a t)"), ps[:, 4 * (b % 2) + g, :],
                                gates.rearrange("p a t -> p (a t)"), ALU.mult).then_inc(S["mul_ready"], 1)
                if b == 3 and g > 0:
                    merged_low(g - 1)
                if b == 3 and g < 2:
                    low_m(N_PROJ + N_BR + g)
            if b == 3:
                merged_low(3)

        for n in range(N_PROJ + 2, NM):
            if n not in (N_PROJ + N_BR, N_PROJ + N_BR + 1):
                low_m(n)
            if n < N_PROJ + N_BR:
                merge(n - N_PROJ - 2)
            if n == N_PROJ + N_BR:
                merge(3)
        dve.wait_ge(S["wr_hi"], 1)
        V.tensor_tensor(wrs[:, 1], wr[:], wrs[:, 0].bitcast(F32), ALU.subtract).then_inc(S["wr_lo"], 1)
        dve.wait_ge(S["h0_back"], 16)

        def add_residual(src, t, count):
            for half in range(2):
                last = V.scalar_tensor_tensor(out=src[1][:, t, half * 512:(half + 1) * 512],
                                              in0=src[0][:, t, half * 512:(half + 1) * 512], scalar=ALPHA,
                                              in1=ps[:, 2 * t + half, :], op0=ALU.mult, op1=ALU.add)
            last.then_inc(S["out_read"], 1)
            dve.wait_ge(S["out_read"], count + t + 1)

        def mixed(t):
            if t == 0:
                dve.wait_ge(S["out_first"], 1)
            else:
                dve.wait_ge(S["pe_used"], NM)
            add_residual((h0b, zz), t, 0)

        layer_norm(zz, zz, ln1b, S["ln1_landed"], 32, S["h_ready"], mixed)
        low_turned(NT)
        for n in range(NM, NM + 3):
            low(n, raw_slot(n), n % 3)
        dve.wait_ge(S["h1s_hi"], 1)
        V.tensor_tensor(h1s[:, 1].rearrange("p t c -> p (t c)"), zz[:].rearrange("p t c -> p (t c)"),
                        h1s[:, 0].rearrange("p t c -> p (t c)").bitcast(F32), ALU.subtract).then_inc(S["h1s_lo"], 1)

        dve.wait_ge(S["scores_ready"], 1)
        sc = tk[:, 0:128].rearrange("p (t e) -> p t e", t=NT)
        biased = tk[:, 128:256].rearrange("p (t e) -> p t e", t=NT)
        one(V.tensor_tensor(biased, sc, rbb[:].unsqueeze(1).to_broadcast([P, NT, 64]), ALU.add))
        top = tk[:, 256:384].rearrange("p (t g k) -> p t g k", t=NT, g=N_GROUPS)
        for t in range(NT):
            for g in range(N_GROUPS):
                last = V.max(top[:, t, g], biased[:, t, 8 * g:8 * g + 8])
        one(last)

        def vec(i):
            return tk[:, 896 + 16 * i:912 + 16 * i].rearrange("p (t g) -> p t g", t=NT)

        gs, rank, keep, drop, best = (vec(i) for i in range(5))
        one(V.tensor_tensor(gs, top[:, :, :, 0], top[:, :, :, 1], ALU.add))
        other = gs.unsqueeze(2).to_broadcast([P, NT, 8, 8])
        own = gs.unsqueeze(3).to_broadcast([P, NT, 8, 8])
        gt = tk[:, 384:512].rearrange("p (t a b) -> p t a b", t=NT, a=8)
        eq = tk[:, 512:640].rearrange("p (t a b) -> p t a b", t=NT, a=8)
        V.tensor_tensor(gt, other, own, ALU.is_gt)
        one(V.tensor_tensor(eq, other, own, ALU.is_equal))
        one(V.tensor_tensor(eq, eq, tri[:].rearrange("p (a b) -> p a b", a=8).unsqueeze(1).to_broadcast([P, NT, 8, 8]), ALU.mult))
        one(V.tensor_tensor(gt, gt, eq, ALU.add))
        one(V.tensor_reduce(rank, gt, AX.X, ALU.add))
        one(V.tensor_scalar(keep, rank, TOPK_GROUPS - 0.5, None, ALU.is_lt))
        one(V.tensor_scalar(drop, keep, -MASK, MASK, ALU.mult, ALU.add))
        cand = tk[:, 512:640].rearrange("p (t g k) -> p t g k", t=NT, g=8)
        one(V.tensor_tensor(cand, biased.rearrange("p t (g k) -> p t g k", g=8), keep.unsqueeze(3).to_broadcast([P, NT, 8, 8]), ALU.mult))
        one(V.tensor_tensor(cand, cand, drop.unsqueeze(3).to_broadcast([P, NT, 8, 8]), ALU.add))
        cv = tk[:, 512:640].rearrange("p (t e) -> p t e", t=NT)
        left = tk[:, 384:512].rearrange("p (t e) -> p t e", t=NT)
        for t in range(NT):
            last = V.max(best[:, t], cv[:, t])
        one(last)
        for t in range(NT):
            last = V.match_replace(left[:, t], best[:, t], cv[:, t], 3.0 * MASK)
        one(last)
        chosen = tk[:, 640:768].rearrange("p (t e) -> p t e", t=NT)
        V.tensor_tensor(chosen, cv, left, ALU.not_equal).then_inc(S["mask_ready"], 1)
        dve.wait_ge(S["mask_ready"], 1)
        wts = tk[:, 768:896].rearrange("p (t e) -> p t e", t=NT)
        one(V.tensor_tensor(wts, chosen, sc, ALU.mult))
        one(V.tensor_reduce(tk[:, 976:978], wts, AX.X, ALU.add))
        one(V.tensor_scalar(tk[:, 978:980], tk[:, 976:978], 1e-20, None, ALU.add))
        one(V.reciprocal(tk[:, 980:982], tk[:, 978:980]))
        for t in range(NT):
            last = V.tensor_scalar(comb[:, t], wts[:, t], tk[:, 980 + t:981 + t], ROUTED_SCALE, ALU.mult, ALU.mult)
        last.then_inc(S["comb_ready"], 1)
        dve.wait_ge(S["comb_ready"], 1)

        def dense_hidden(silu_done, done, count, weight):
            for t in range(NT):
                dve.wait_ge(silu_done, count * 2 + t - 1)
                up = ps[:, 4 + t, HID:2 * HID]
                if weight is None:
                    V.tensor_tensor(hid[:, t], up, sil[:, t], ALU.mult).then_inc(done, 1)
                else:
                    V.scalar_tensor_tensor(out=hid[:, t], in0=up, scalar=weight(t), in1=sil[:, t], op0=ALU.mult,
                                           op1=ALU.mult).then_inc(done, 1)

        def dense_low(hi_done, done, count):
            for t in range(NT):
                dve.wait_ge(hi_done, count * 2 + t - 1)
                V.tensor_tensor(hTs[:, 1, t], ps[:, 6 + t, 0:256].rearrange("p (j c) -> p j c", j=2),
                                hTs[:, 0, t].bitcast(F32), ALU.subtract).then_inc(done, 1)

        dense_hidden(S["sh_silu"], S["sh_hid"], 1, None)
        dve.wait_ge(S["ranks"], 1)
        rk = tk[:, 0:192].rearrange("p (t e) -> p t e", t=3)
        V.tensor_copy(tk[:, 0:192], ps[:, 0, 0:192]).then_inc(S["ranks_read"], 1)
        dense_low(S["sh_hi"], S["sh_lo"], 1)
        dve.wait_ge(S["ranks_read"], 1)
        total = tk[:, 128:192].rearrange("p (q e) -> p q e", e=2)
        ranks = tk[:, 0:128].rearrange("p (t q e) -> p t q e", t=NT, e=2)
        for t in range(NT):
            one(V.tensor_tensor(ranks[:, t, :, 1], ranks[:, t, :, 1], total[:, :, 0], ALU.add))
        one(V.scalar_tensor_tensor(out=place[:], in0=rk[:, 0:2], scalar=1.0, in1=chosen, op0=ALU.add, op1=ALU.mult))
        one(V.tensor_scalar(place[:], place[:], -1.0, None, ALU.add))
        def compare_places(q, first=False):
            if not first:
                dve.wait_ge(S["sel_ready"], q)
            for e in range(2):
                c = q * 2 + e
                pl = place[:, :, c:c + 1] if isinstance(c, int) else place[:, :, bass.ds(c, 1)]
                last = V.tensor_tensor(sel_one[:, e], slot_no[:, 0:P].unsqueeze(1).to_broadcast([P, NT, P]),
                                       pl.to_broadcast([P, NT, P]), ALU.is_equal)
            last.then_inc(S["places_compared"], 1)

        compare_places(0, first=True)
        one(V.tensor_scalar(comb_over[:], place[:], P - 0.5, None, ALU.is_gt))
        one(V.tensor_tensor(comb_over[:], comb_over[:], comb[:], ALU.mult))
        one(V.tensor_tensor(tk[:, 192:224], total[:, :, 0], total[:, :, 1], ALU.add))
        one(V.tensor_reduce(tk[:, 224:225], tk[:, 192:224], AX.X, ALU.max))
        V.tensor_scalar(over[:, 0:1], tk[:, 224:225], P + 0.5, None, ALU.is_gt).then_inc(S["over_ready"], 1)
        V.tensor_copy(wc[:, :, :, 4:6], place[:].rearrange("p t (q e) -> p t q e", e=2))
        dve.wait_ge(S["wc_hi"], 1)
        V.tensor_tensor(wc[:, :, :, 2:4], comb[:].rearrange("p t (q e) -> p t q e", e=2), wc[:, :, :, 0:2].bitcast(F32),
                        ALU.subtract).then_inc(S["wc_lo"], 1)

        def gather_low(count, group, kk, bank):
            dve.wait_ge(S["gathered"], count)
            V.tensor_copy(xg[group][:, 1, 2 * kk:2 * kk + 2, :].rearrange("p k s -> p (k s)"), ps[:, bank, :]).then_inc(S["gather_lo"], 1)

        def step_low(q, v):
            low(step_chunk(q, v), step_slot(v), split_slot(v))

        def hidden(q, e):
            dve.wait_ge(S["cw_ready"], q + 1)
            dve.wait_ge(S["pair_silu"], q * 2 + (1 + e))
            V.scalar_tensor_tensor(out=hid[:, e], in0=ps[:, 4 + e, HID:2 * HID], scalar=cw[:, e:e + 1], in1=sil[:, e],
                                   op0=ALU.mult, op1=ALU.mult).then_inc(S["pair_hid"], 1)

        def hidden_low(q, e):
            dve.wait_ge(S["hid_hi"], q * 2 + (1 + e))
            V.tensor_tensor(hTs[:, 1, e].rearrange("p j c -> p (j c)"), ps[:, 4 + e, 0:256],
                            hTs[:, 0, e].rearrange("p j c -> p (j c)").bitcast(F32), ALU.subtract).then_inc(S["hid_lo"], 1)

        def outputs_low(q):
            for half in range(2):
                dve.wait_ge(S["y_hi"], q * 2 + (1 + half))
                V.tensor_tensor(ys[:, 1, half * 512:(half + 1) * 512], ps[:, 6 + half, :],
                                ys[:, 0, half * 512:(half + 1) * 512].bitcast(F32), ALU.subtract).then_inc(S["y_lo"], 1)

        def pair_step(q, r, first=False, compares=True, last=False):
            if not first:
                hidden(q + (-1), 1)
                if not last:
                    gather_low(q * 4 + 8, 1 - (r - 1) % 4 // 2, 2 * ((r + 1) % 2) + 1, 6)
                step_low(q, 2)
                if compares:
                    compare_places(q + 3)
                hidden_low(q + (-1), 1)
                step_low(q, 3)
            else:
                compare_places(q + 3)
                step_low(q, 4)
            hidden(q, 0)
            if not first:
                step_low(q, 4)
            if first:
                hidden_low(q, 0)
            step_low(q, 5)
            if not first:
                hidden_low(q, 0)
            if not first:
                outputs_low(q + (-1))
            step_low(q + 1, 0)

        def next_slots(q, r):
            gather_low(q * 4 + 10, 1 - r // 2, 2 * (r % 2), 6)
            step_low(q + 1, 1)

        compare_places(1)
        for n in range(NM + 3, NM + 5):
            low(n, raw_slot(n), n % 3)
        for kk in range(4):
            gather_low(2 * kk + 2, 0, kk, FIRST_BANKS[1][kk % 2])
        compare_places(2)
        pair_step(0, 0, first=True)
        next_slots(0, 0)
        with dve.Fori(0, (PAIRS - 4) // 4) as i:
            for u in range(4):
                pair_step(i * 4 + (1 + u), (1 + u) % 4)
                next_slots(i * 4 + (1 + u), (1 + u) % 4)
        for q in range(PAIRS - 3, PAIRS):
            pair_step(q, q % 4, compares=False, last=q == PAIRS - 1)
            if q < PAIRS - 2:
                next_slots(q, q % 4)
            else:
                step_low(q + 1, 1)
        hidden(PAIRS - 1, 1)
        hidden_low(PAIRS - 1, 1)
        outputs_low(PAIRS - 1)

        with if_over(dve):
            V.memset(tk[:, 1:2], 0.0).then_inc(S["fb_down"], 1)
            with dve.Fori(0, N_EXPERTS) as e:
                dve.wait_ge(S["fb_split_hi"], e + 1)
                for c in range(3):
                    last = V.tensor_tensor(wlo[:, c], rawL[:, c], whi[:, c].bitcast(F32), ALU.subtract)
                last.then_inc(S["fb_split_lo"], 1)
                dense_hidden(S["fb_silu"], S["fb_hid"], e + 1, lambda t: comb_over[:, t, bass.ds(e, 1)])
                dense_low(S["fb_hi"], S["fb_lo"], e + 1)
            dve.wait_ge(S["fb_down"], N_EXPERTS + 1)
        dve.wait_ge(S["scattered"], PAIRS)
        layer_norm(outb, outb, ln2b, S["ln2_landed"], 32, S["z_ready"], lambda t: add_residual((zz, outb), t, NT))

    ctx.close()


_INPUTS = ["x", "ln_in_g", "ln_in_b", "w_in", "w_gate", "b_gate", "w_br_ret", "w_br_nat", "w_br_hgrn", "w_br_diff",
           "w_out", "ret_gn", "rpb", "hgrn_lb", "hgrn_gn", "diff_lambda", "diff_subln", "ln1_g", "ln1_b", "w_router",
           "router_bias", "w_e_gate", "w_e_up", "w_e_down", "w_s_gate", "w_s_up", "w_s_down", "ln2_g", "ln2_b"]


def kernel(**inputs):
    import concourse.bacc as bacc
    from concourse.bass_utils import run_bass_kernel_spmd

    a = {k: np.asarray(v) for k, v in inputs.items()}
    a["b_gate"] = np.ascontiguousarray(a["b_gate"].reshape(32, P).T)
    rpb = a.pop("nat_rpb")[0]
    pad = np.zeros((HEADS, 7, 127), rpb.dtype)
    pad[:, :, 48:79] = rpb[:, 4:11]
    a["rpb"] = pad
    arrays = {k: np.ascontiguousarray(a[k]) for k in _INPUTS}
    arrays.update(constants())
    nc = bacc.Bacc("TRN2", target_bir_lowering=False, num_devices=1)
    args = {k: nc.dram_tensor("in_" + k, v.shape, mybir.dt.from_np(v.dtype), kind="ExternalInput").ap() for k, v in arrays.items()}
    out = nc.dram_tensor("out_0", (1, TOKENS, D), F32, kind="ExternalOutput").ap()
    build(nc, args, out)
    r = run_bass_kernel_spmd(nc, [{"in_" + k: v for k, v in arrays.items()}], core_ids=[0])
    return r.results[0]["out_0"]
```
